# Optimizing a Trainium2 kernel written in Bass

```python
import math
import jax, jax.numpy as jnp
from jax import lax
import numpy as np

D_MODEL = 1024
BATCH = 1
SEQ = 128
DEPTH = 2
DEC_BATCH = 1
DEC_SEQ = 512
PAST_LEN = 128

GRID_W = 64
D_HYENA = 512
HYENA_ORDER = 2
HYENA_POS_BANDS = 16
HYENA_POS_DIM = 1 + 2 * HYENA_POS_BANDS
HYENA_FILTER_HIDDEN = 64
HYENA_WINDOW_SHIFT = 0.05
N_HEADS = 8
N_KV_HEADS = 2
HEAD_DIM = 64
ATT_Q = N_HEADS * HEAD_DIM
ATT_KV = N_KV_HEADS * HEAD_DIM
Q_BLOCK = 128
ROPE_THETA = 10000.0
D_SCONV = 512
N_BRANCH = 3
N_EXPERTS = 16
EXPERT_FF = 512
CAPACITY_FACTOR = 2
NORM_EPS = 1e-6
HY_COLS = (HYENA_ORDER + 1) * D_HYENA
ATT_COLS = ATT_Q + 2 * ATT_KV
SC_COLS = 3 * D_SCONV
GATE_COLS = N_BRANCH * D_MODEL
D_IN = HY_COLS + ATT_COLS + SC_COLS + GATE_COLS
F32 = jnp.float32

kernel_name = 'hybrid_diffusion_hyena_gqa_shortconv_ecmoe_step'

def rms_norm(x, w):
    x32 = x.astype(F32)
    y = x32 * lax.rsqrt(jnp.mean(x32 * x32, axis=-1, keepdims=True) + NORM_EPS)
    return (y * w.astype(F32)).astype(x.dtype)

def conv3_centred(u, w, b):
    up = jnp.pad(u, ((0, 0), (1, 1), (0, 0)))
    return up[:, :-2] * w[0] + up[:, 1:-1] * w[1] + up[:, 2:] * w[2] + b

def hyena_filters(L, w1, b1, w2, b2, w3, b3, decay):
    n = jnp.arange(L, dtype=F32)
    t = n / max(L - 1, 1)
    bands = jnp.linspace(1e-4, HYENA_POS_BANDS - 1, HYENA_POS_BANDS, dtype=F32)
    ang = 2.0 * math.pi * n[:, None] * bands[None, :] / L
    z = jnp.concatenate([t[:, None], jnp.cos(ang), jnp.sin(ang)], axis=-1).astype(w1.dtype)
    h = jnp.sin(z @ w1 + b1)
    h = jnp.sin(h @ w2 + b2)
    h = (h @ w3 + b3).astype(F32)
    window = jnp.exp(-t[:, None] * jnp.abs(decay.astype(F32))[None, :]) + HYENA_WINDOW_SHIFT
    return (h * window).reshape(L, 2, HYENA_ORDER, D_HYENA)

def bidir_fftconv(u, h_fwd, h_bwd, bias):
    L = u.shape[1]
    C = h_fwd.shape[1]
    k = jnp.concatenate([h_fwd, jnp.zeros((1, C), F32), h_bwd[:0:-1]], axis=0)
    u32 = u.astype(F32)
    U = jnp.fft.rfft(u32, n=2 * L, axis=1)
    K = jnp.fft.rfft(k, n=2 * L, axis=0)
    y = jnp.fft.irfft(U * K[None], n=2 * L, axis=1)[:, :L]
    return (y + u32 * bias.astype(F32)).astype(u.dtype)

def hyena_mixer(hy, short_w, short_b, filt, bias):
    hy = conv3_centred(hy, short_w, short_b)
    parts = jnp.split(hy, HYENA_ORDER + 1, axis=-1)
    z = parts[0]
    for o in range(HYENA_ORDER):
        z = parts[o + 1] * bidir_fftconv(z, filt[:, 0, o], filt[:, 1, o], bias[o])
    return z

def axial_rope_tables(rows):
    row = jnp.repeat(jnp.arange(rows, dtype=F32), GRID_W)
    col = jnp.tile(jnp.arange(GRID_W, dtype=F32), rows)
    axis_dim = HEAD_DIM // 2
    inv_freq = ROPE_THETA ** (-jnp.arange(0, axis_dim, 2, dtype=F32) / axis_dim)
    ar = row[:, None] * inv_freq[None, :]
    ac = col[:, None] * inv_freq[None, :]
    return (jnp.cos(ar), jnp.sin(ar), jnp.cos(ac), jnp.sin(ac))

def rotate_half_pairs(x, cos, sin):
    x1, x2 = jnp.split(x, 2, axis=-1)
    return jnp.concatenate([x1 * cos - x2 * sin, x2 * cos + x1 * sin], axis=-1)

def apply_axial_rope(x, rope):
    cos_r, sin_r, cos_c, sin_c = rope
    xr, xc = jnp.split(x.astype(F32), 2, axis=-1)
    out = jnp.concatenate([
        rotate_half_pairs(xr, cos_r[None, :, None, :], sin_r[None, :, None, :]),
        rotate_half_pairs(xc, cos_c[None, :, None, :], sin_c[None, :, None, :])], axis=-1)
    return out.astype(x.dtype)

def blocked_gqa(q, k, v):
    B, Lq = q.shape[0], q.shape[1]
    nb = Lq // Q_BLOCK
    G = N_HEADS // N_KV_HEADS
    qb = q.reshape(B, nb, Q_BLOCK, N_KV_HEADS, G, HEAD_DIM).transpose(1, 0, 2, 3, 4, 5)
    scale = HEAD_DIM ** -0.5

    def one_block(qblk):
        s = jnp.einsum('bqkgd,bskd->bkgqs', qblk, k).astype(F32) * scale
        p = jax.nn.softmax(s, axis=-1).astype(v.dtype)
        return jnp.einsum('bkgqs,bskd->bqkgd', p, v)

    o = lax.map(one_block, qb)
    return o.transpose(1, 0, 2, 3, 4, 5).reshape(B, Lq, ATT_Q)

def expert_choice_moe(h, router_w, w_gate, w_up, w_down):
    B, N, D = h.shape
    cap = CAPACITY_FACTOR * N // N_EXPERTS
    aff = jax.nn.softmax((h @ router_w).astype(F32), axis=-1)
    gate, idx = lax.top_k(jnp.swapaxes(aff, 1, 2), cap)
    xs = jax.vmap(lambda hb, ib: hb[ib])(h, idx)
    a = jnp.einsum('becd,edf->becf', xs, w_gate)
    u = jnp.einsum('becd,edf->becf', xs, w_up)
    y = jnp.einsum('becf,efd->becd', jax.nn.silu(a) * u, w_down)
    y = y * gate[..., None].astype(y.dtype)
    return jax.vmap(lambda yb, ib: jnp.zeros((N, D), yb.dtype).at[ib.reshape(-1)].add(yb.reshape(-1, D)))(y, idx)

def trunk_layer(x, cond, p, rope, ctx_k, ctx_v):
    B, L, D = x.shape
    mod = (jax.nn.silu(cond) @ p['mod_w'] + p['mod_b']).reshape(-1, 1, 6 * D)
    sh1, sc1, g1, sh2, sc2, g2 = jnp.split(mod, 6, axis=-1)
    h = rms_norm(x, p['norm1_w']) * (1 + sc1) + sh1
    proj = h @ p['w_in']
    hy, qkv, scv, gates = jnp.split(proj, [HY_COLS, HY_COLS + ATT_COLS, HY_COLS + ATT_COLS + SC_COLS], axis=-1)
    filt = hyena_filters(L, p['hy_w1'], p['hy_b1'], p['hy_w2'], p['hy_b2'], p['hy_w3'], p['hy_b3'], p['hy_decay'])
    ya = hyena_mixer(hy, p['hy_short_w'], p['hy_short_b'], filt, p['hy_bias'])
    q, k, v = jnp.split(qkv, [ATT_Q, ATT_Q + ATT_KV], axis=-1)
    q = rms_norm(q.reshape(B, L, N_HEADS, HEAD_DIM), p['q_norm_w'])
    k = rms_norm(k.reshape(B, L, N_KV_HEADS, HEAD_DIM), p['k_norm_w'])
    v = v.reshape(B, L, N_KV_HEADS, HEAD_DIM)
    if rope is None:
        keys, vals = k, v
    else:
        q = apply_axial_rope(q, rope)
        keys = jnp.concatenate([ctx_k, apply_axial_rope(k, rope)], axis=1)
        vals = jnp.concatenate([ctx_v, v], axis=1)
    yb = blocked_gqa(q, keys, vals)
    u, bgate, cgate = jnp.split(scv, 3, axis=-1)
    yc = bgate * conv3_centred(cgate * u, p['sc_w'], p['sc_b'])
    ga, gb, gc = jnp.split(gates, 3, axis=-1)
    merged = (jax.nn.sigmoid(ga) * (ya @ p['w_br_a'])
              + jax.nn.sigmoid(gb) * (yb @ p['w_br_b'])
              + jax.nn.sigmoid(gc) * (yc @ p['w_br_c']))
    x = x + g1 * (merged @ p['w_o'])
    h2 = rms_norm(x, p['norm2_w']) * (1 + sc2) + sh2
    x = x + g2 * expert_choice_moe(h2, p['router_w'], p['exp_w_gate'], p['exp_w_up'], p['exp_w_down'])
    return x, k, v

def setup_inputs(seed: int = 0) -> dict:
    key = jax.random.key(seed)
    ks = iter(jax.random.split(key, 64))

    def nrm(shape, scale):
        return jax.random.normal(next(ks), shape, F32) * scale

    return {
        'x_prompt': nrm((BATCH, SEQ, D_MODEL), 1.0),
        'x_sample': nrm((DEC_BATCH, DEC_SEQ, D_MODEL), 1.0),
        'cache_k': nrm((DEC_BATCH, DEPTH, PAST_LEN, N_KV_HEADS, HEAD_DIM), 1.0),
        'cache_v': nrm((DEC_BATCH, DEPTH, PAST_LEN, N_KV_HEADS, HEAD_DIM), 1.0),
        'c': nrm((DEC_BATCH, D_MODEL), 1.0),
        'c_ctx': nrm((D_MODEL,), 1.0),
        'mod_w': nrm((DEPTH, D_MODEL, 6 * D_MODEL), 0.5 * D_MODEL ** -0.5),
        'mod_b': nrm((DEPTH, 6 * D_MODEL), 0.02),
        'norm1_w': 1.0 + nrm((DEPTH, D_MODEL), 0.05),
        'norm2_w': 1.0 + nrm((DEPTH, D_MODEL), 0.05),
        'w_in': nrm((DEPTH, D_MODEL, D_IN), D_MODEL ** -0.5),
        'hy_short_w': nrm((DEPTH, 3, HY_COLS), 0.5),
        'hy_short_b': nrm((DEPTH, HY_COLS), 0.01),
        'hy_w1': nrm((DEPTH, HYENA_POS_DIM, HYENA_FILTER_HIDDEN), HYENA_POS_DIM ** -0.5),
        'hy_b1': nrm((DEPTH, HYENA_FILTER_HIDDEN), 0.1),
        'hy_w2': nrm((DEPTH, HYENA_FILTER_HIDDEN, HYENA_FILTER_HIDDEN), HYENA_FILTER_HIDDEN ** -0.5),
        'hy_b2': nrm((DEPTH, HYENA_FILTER_HIDDEN), 0.1),
        'hy_w3': nrm((DEPTH, HYENA_FILTER_HIDDEN, 2 * HYENA_ORDER * D_HYENA), 0.02 * HYENA_FILTER_HIDDEN ** -0.5),
        'hy_b3': nrm((DEPTH, 2 * HYENA_ORDER * D_HYENA), 0.01),
        'hy_decay': jax.random.uniform(next(ks), (DEPTH, 2 * HYENA_ORDER * D_HYENA), F32, 3.0, 15.0),
        'hy_bias': nrm((DEPTH, HYENA_ORDER, D_HYENA), 0.1),
        'q_norm_w': 1.0 + nrm((DEPTH, HEAD_DIM), 0.05),
        'k_norm_w': 1.0 + nrm((DEPTH, HEAD_DIM), 0.05),
        'sc_w': nrm((DEPTH, 3, D_SCONV), 0.5),
        'sc_b': nrm((DEPTH, D_SCONV), 0.01),
        'w_br_a': nrm((DEPTH, D_HYENA, D_MODEL), D_HYENA ** -0.5),
        'w_br_b': nrm((DEPTH, ATT_Q, D_MODEL), ATT_Q ** -0.5),
        'w_br_c': nrm((DEPTH, D_SCONV, D_MODEL), D_SCONV ** -0.5),
        'w_o': nrm((DEPTH, D_MODEL, D_MODEL), D_MODEL ** -0.5),
        'router_w': nrm((DEPTH, D_MODEL, N_EXPERTS), D_MODEL ** -0.5),
        'exp_w_gate': nrm((DEPTH, N_EXPERTS, D_MODEL, EXPERT_FF), D_MODEL ** -0.5),
        'exp_w_up': nrm((DEPTH, N_EXPERTS, D_MODEL, EXPERT_FF), D_MODEL ** -0.5),
        'exp_w_down': nrm((DEPTH, N_EXPERTS, EXPERT_FF, D_MODEL), EXPERT_FF ** -0.5),
    }

def reference(x_prompt, x_sample, cache_k, cache_v, c, c_ctx, mod_w, mod_b, norm1_w, norm2_w, w_in,
              hy_short_w, hy_short_b, hy_w1, hy_b1, hy_w2, hy_b2, hy_w3, hy_b3, hy_decay, hy_bias,
              q_norm_w, k_norm_w, sc_w, sc_b, w_br_a, w_br_b, w_br_c, w_o, router_w,
              exp_w_gate, exp_w_up, exp_w_down):
    def layer_params(l):
        return {
            'mod_w': mod_w[l], 'mod_b': mod_b[l], 'norm1_w': norm1_w[l], 'norm2_w': norm2_w[l],
            'w_in': w_in[l], 'hy_short_w': hy_short_w[l], 'hy_short_b': hy_short_b[l],
            'hy_w1': hy_w1[l], 'hy_b1': hy_b1[l], 'hy_w2': hy_w2[l], 'hy_b2': hy_b2[l],
            'hy_w3': hy_w3[l], 'hy_b3': hy_b3[l], 'hy_decay': hy_decay[l], 'hy_bias': hy_bias[l],
            'q_norm_w': q_norm_w[l], 'k_norm_w': k_norm_w[l], 'sc_w': sc_w[l], 'sc_b': sc_b[l],
            'w_br_a': w_br_a[l], 'w_br_b': w_br_b[l], 'w_br_c': w_br_c[l], 'w_o': w_o[l],
            'router_w': router_w[l], 'exp_w_gate': exp_w_gate[l], 'exp_w_up': exp_w_up[l],
            'exp_w_down': exp_w_down[l],
        }

    xp = x_prompt
    ks_new, vs_new = [], []
    for l in range(DEPTH):
        xp, k_l, v_l = trunk_layer(xp, c_ctx, layer_params(l), None, None, None)
        ks_new.append(k_l)
        vs_new.append(v_l)
    new_cache_k = jnp.stack(ks_new, axis=1)
    new_cache_v = jnp.stack(vs_new, axis=1)

    rows = x_sample.shape[1] // GRID_W
    rope = axial_rope_tables(rows)
    xs = x_sample
    for l in range(DEPTH):
        xs, _, _ = trunk_layer(xs, c, layer_params(l), rope, cache_k[:, l], cache_v[:, l])

    return (xp, xs, new_cache_k, new_cache_v)


_drawn_inputs = setup_inputs


def setup_inputs(seed=0):
    import zlib

    import numpy as np

    out = dict(_drawn_inputs(seed))
    spreads = {}
    factors = {'cache_k': 8.0,
     'cache_v': 6.733,
     'norm2_w': 3.578,
     'hy_short_w': 2.958,
     'hy_short_b': 8.0,
     'hy_w1': 6.585,
     'hy_b1': 8.0,
     'hy_w2': 6.833,
     'hy_b2': 8.0,
     'hy_w3': 5.301,
     'hy_b3': 3.16,
     'hy_decay': 7.715,
     'hy_bias': 8.0,
     'q_norm_w': 8.0,
     'sc_b': 38.253,
     'w_br_a': 3.151}
    for name, (base, spread) in spreads.items():
        noise = np.random.default_rng([zlib.crc32(name.encode()), seed]).standard_normal(out[name].shape)
        drawn = base * np.exp(spread * noise) if base else spread * noise
        out[name] = __import__('jax').numpy.asarray(drawn.astype(out[name].dtype))
    for name, factor in factors.items():
        out[name] = (out[name] * factor).astype(out[name].dtype)
    return out
```

```python
from contextlib import ExitStack

import concourse.bass as bass
import numpy as np
from concourse import mybir

ACT = mybir.ActivationFunctionType
ALU = mybir.AluOpType
AX = mybir.AxisListType
F32 = mybir.dt.float32

P = 128
D = 1024
KC = D // P
DEPTH = 2
LI, LS = 128, 512
T = LI + LS
NT = T // P
GROUPS = ((0, 0, LI), (1, LI, T))
DH = 512
NE = 16
EPS = 1e-6
SHIFT = 0.05
HD = 64
NQ, NKV = 8, 2
QK = (NQ + NKV) * HD
QKV = QK + NKV * HD
PAST = 128
POS = 33
FH = 64
CAP = (2 * LI // NE, 2 * LS // NE)
SLOTS = CAP[0] + CAP[1]

ITEM = 2048
SLOT = 4
N_MOD, N_FILT, N_HY, N_SC, N_QKV, N_GATE, N_BR, N_WO, N_EXP = 24, 3, 6, 6, 3, 12, 6, 4, 96
P_FILT = N_MOD
P_HY = P_FILT + N_FILT
P_SC = P_HY + N_HY
P_QKV = P_SC + N_SC
P_GATE = P_QKV + N_QKV
P_BR = P_GATE + N_GATE
P_WO = P_BR + N_BR
P_EXP = P_WO + N_WO
ITEMS = P_EXP + N_EXP
LAPS = ITEMS // SLOT
assert ITEMS % SLOT == 0

V_MODB, V_N1, V_N2, V_HYW, V_HYB, V_SCW, V_SCB, NV = 0, 48, 56, 64, 100, 112, 124, 128

PHASES = 9
TWO_PI = (6.28125, 0.0019340515136718750, 2 * np.pi - 6.28125 - 0.0019340515136718750)
ROUND = 1.5 * 2.0 ** 23
PI_IN = 3.1415925
SEQ_C = LI
N_CONSTS = 16 * 13
QSCALE = HD ** -0.5


def build(nc, a):
    with ExitStack() as ctx:
        def sb(name, shape):
            return ctx.enter_context(nc.sbuf_tensor(name, shape, F32))

        def sem(name):
            return ctx.enter_context(nc.semaphore(name))

        ring = sb("ring", [P, SLOT, ITEM])
        X = sb("X", [P, KC, T])
        ident = sb("ident", [P, P])
        onesm = sb("onesm", [P, P])
        ones1 = sb("ones1", [P, P])
        utri = sb("utri", [P, P])
        sel = sb("sel", [P, 2])
        zfeat = sb("zfeat", [POS, T])
        tneg = sb("tneg", [P, NT])
        rope = sb("rope", [P, 2, NT - 1, HD])
        iota = sb("iota", [P, HD])
        csi = sb("csi", [P, 2, P])
        cfi = sb("cfi", [P, 2, P])
        vec = sb("vec", [P, NV])
        fw = sb("fw", [FH, 2 * FH + 2])
        rw = sb("rw", [P, KC, NE])
        qkw = sb("qkw", [P, QK])
        cs = sb("cs", [P, KC, 32])
        cond = sb("cond", [P, KC, 2])
        mod = sb("mod", [P, 48, 2])
        ws = sb("ws", [P, 2, KC, 2])
        st5 = sb("st5", [P, NT, 10])
        rst5 = sb("rst5", [P, NT, 10])
        mx = sb("mx", [P, 2])
        nb = sb("nb", [P, 2])
        rsum = sb("rsum", [P, 2])
        rinv = sb("rinv", [P, 2])
        gt = sb("gt", [P, NE])
        m8 = sb("m8", [NE, 8])
        eps = sb("eps", [P, 1])
        arena = sb("arena", [P, 139 * 256])
        ps = ctx.enter_context(nc.psum_tensor("ps", [P, 8, 512], F32))

        def region(kb, shape, parts=P):
            n = int(np.prod(shape))
            o = int(kb * 256)
            assert o + n <= 139 * 256, (kb, shape)
            v = arena[0:parts, o:o + n]
            names = "abcd"[:len(shape)]
            if len(shape) == 1:
                return v
            return v.rearrange(f"p ({' '.join(names)}) -> p {' '.join(names)}",
                               **{names[i]: shape[i] for i in range(len(shape) - 1)})

        fa, fb = region(0, [NT, 2, DH]), region(20, [NT, 2, DH])
        win, dec = region(40, [2048]), region(48, [2048])
        fdir = region(56, [2, DH])
        kout = region(60, [4, DH])
        farg, frnd = region(68, [T], FH), region(70.5, [T], FH)
        fh1, fh2 = region(73, [T], FH), region(75.5, [T], FH + 1)
        fbias = region(78, [2, DH], 1)
        mrow = region(82, [4, 256])
        h = region(0, [KC, T])
        Y3 = region(20, [3, 4, T])
        u_tm, x1_tm = region(50, [NT, DH]), region(60, [NT, DH])
        qkv = region(70, [NT, QKV])
        sq = region(85, [KC, T])
        prep = region(85, [NT, QK])
        rstd = region(105, [T])
        raw = region(108, [2, T + 3])
        cv = region(113.25, [2, T + 1])
        cvs = region(118.5, [2, T + 1])
        ubuf = region(123.75, [2, T])
        sgb = region(129, [4, T])
        qT, kT, qj = region(0, [4, T]), region(10, [P + PAST + LS]), region(13, [T])
        ctxv = region(15.5, [P])
        PT = region(85, [2, NT, LS])
        PTi = region(110, [2, P])
        Pb = region(105, [2, T])
        Kb = region(0, [NT, 2, DH])
        Yb = region(85, [NT, 2, DH])
        ytmp = region(105, [4, DH])
        CS = region(113, [2, 4, DH])
        merged = region(70, [KC, T])
        sgin, mtmp = region(0, [4, T]), region(10, [2, T])
        h2_tm = region(20, [NT, D])
        Ps, Pi = region(40, [4, NE * HD]), region(56, [NE, 32])
        PTs, PTc = region(58, [8, LS]), region(74, [4, P])
        xs = region(76, [KC, NE, SLOTS])
        sq2, rstd2 = region(116, [KC, T]), region(136, [T])
        aft, work, mask = (region(116 + 2.5 * i, [T], NE) for i in range(3))
        maskT, q1, aff = (region(123.5 + 0.5 * i, [NT, NE]) for i in range(3))
        lg, r1 = region(125, [NT, NE]), region(125.5, [NT, 2])
        ys, yc = region(0, [8, D]), region(32, [4, D])
        xe = region(116, [2, KC, SLOTS])
        sg, hid = region(121, [2, DH], SLOTS), region(125, [2, DH], SLOTS)
        hidT = region(129, [2, 4, SLOTS])

        landed = [sem(f"item_landed{s}") for s in range(SLOT)]
        item_used = sem("item_used")
        phase = sem("phase")
        consts = sem("consts")
        waited = sem("waited")
        lay = sem("layer_vectors")
        s_cs, s_csz = sem("silu_cond"), sem("cs_zeroed")
        modrow_sb, modcol_ready, modcol_read = sem("modrow_sb"), sem("modcol_ready"), sem("modcol_read")
        f_mm, f_arg, f_sin, f_win, f_winread = sem("f_mm"), sem("f_arg"), sem("f_sin"), sem("f_win"), sem("f_winread")
        f_ones, f_dec = sem("f_ones"), sem("f_dec")
        f_taps, f_tapsread = sem("f_taps"), sem("f_taps_read")
        k_ready, k_evac = sem("k_ready"), sem("k_evac")
        k_stored = [sem(f"k_stored{i}") for i in range(4)]
        s_sq, s_ms, s_rt, s_rstd, s_xn, s_h = (sem(n) for n in (
            "squares", "mean_square", "root", "rstd_ready", "x_normed", "h_ready"))
        chunk_ready = sem("chunk_ready")
        act_freed, dve_freed = sem("act_freed"), sem("dve_freed")
        conv_done, tr_ready, tr_evac, pads = sem("conv_done"), sem("tr_ready"), sem("tr_evac"), sem("pads_zeroed")
        prep_done = sem("prep_done")
        qs_ready, qrt = sem("q_squares"), sem("q_root")
        sg_ready, sg_free = sem("sg_ready"), sem("sg_free")
        sg_stored = [sem(f"sg_stored{i}") for i in range(4)]
        cache_st = sem("cache_stored")
        a_tr, a_trev, a_ctx = sem("a_tr"), sem("a_tr_evac"), sem("ctx_loaded")
        a_qj, a_s, a_max, a_exp, a_norm, a_pt, a_ptev, a_pv, a_pvev = (sem(n) for n in (
            "a_qj", "a_scores", "a_max", "a_exp", "a_norm", "a_pt", "a_ptev", "a_pv", "a_pvev"))
        cs_loaded, k_loaded, k_free = sem("cs_loaded"), sem("k_loaded"), sem("k_free")
        y_fwd, y_mul, y_inv, y_out = sem("y_fwd"), sem("y_mul"), sem("y_inv"), sem("y_out")
        sg_in = [sem(f"sg_in{i}") for i in range(4)]
        br_ready, br_read = sem("br_ready"), sem("br_read")
        wo_ready, wo_read = sem("wo_ready"), sem("wo_read")
        r_lg, r_sub, r_exp, r_aff, r_affT, r_aft, r_mask, r_maskT, r_mt, r_pos, r_P = (sem(n) for n in (
            "r_lg", "r_sub", "r_exp", "r_aff", "r_affT", "r_aft", "r_mask", "r_maskT", "r_mt", "r_pos", "r_P"))
        t_ready, t_evac, g_ready, g_evac, g_zero = (sem(n) for n in (
            "t_ready", "t_evac", "g_ready", "g_evac", "yc_zeroed"))
        e_x, e_up, e_silu, e_hid, e_t, e_hidT, e_yev, e_ycev = (sem(n) for n in (
            "e_x", "e_up", "e_silu", "e_hid", "e_t", "e_hidT", "e_yev", "e_ycev"))
        c_ready, c_read = sem("c_ready"), sem("c_read")
        out_st = sem("out_stored")

        block = ctx.enter_context(nc.Block())

        def apart(eng):
            eng.sem_inc(waited, 1)

        def end_phase(eng, l, n):
            eng.drain().then_inc(phase, 1)
            eng.wait_ge(phase, l * (4 * PHASES) + 4 * (n + 1))
            apart(eng)

        def tok(b):
            return ps[:, 2 * b:2 * b + 2, :].rearrange("p a n -> p (a n)")[:, 384:1024]

        def freed_by(c):
            def kind(x):
                return "act" if x < 12 or (x - 12) % 6 < 2 or x >= 24 else "dve"
            me = kind(c)
            return me, sum(kind(x) == me for x in range(c + 1))

        A_FREED = 12 + 4 + 9

        def wait_chunk_freed(eng, l, c):
            who, n = freed_by(c)
            if who == "act":
                eng.wait_ge(act_freed, l * A_FREED + n)
            else:
                eng.wait_ge(dve_freed, l * 8 + n)

        def wait_chunk(eng, l, c):
            if c < 24:
                p, odd, before = P_HY + c // 2, c % 2, c // 2 + 1
            else:
                p, odd, before = P_QKV + (c - 24) // 3, (c - 24) % 3 == 2, 12 + 2 * ((c - 24) // 3) + (c - 24) % 3 + 1
            if odd:
                eng.wait_ge(item_used, l * ITEMS + p + 1)
            else:
                eng.wait_ge(chunk_ready, l * (12 + 6 + 12) + before)

        @block.sync
        def _(sp):
            for s in range(SLOT):
                sp.dma_start(ring[:, s, :], a["stream"][s]).then_inc(landed[s], 16)
            with sp.Fori(1, LAPS * DEPTH) as lap:
                for s in range(SLOT):
                    sp.wait_ge(item_used, lap * SLOT + (s + 1 - SLOT))
                    sp.dma_start(ring[:, s, :], a["stream"][lap * SLOT + s]).then_inc(landed[s], 16)

        @block.gpsimd
        def _(pool):
            pairs = [(X, "x"), (ident, "ident"), (onesm, "onesm"), (ones1, "ones1"), (utri, "utri"), (sel, "sel"),
                     (zfeat, "zfeat"), (tneg, "tneg"), (rope, "rope"), (iota, "iota"), (csi, "csi"), (cfi, "cfi"),
                     (cond, "cond")]
            for dst, name in pairs:
                pool.dma_start(dst[:], a[name]).then_inc(consts, 16)
            for i in range(4):
                pool.drain().then_inc(sg_free, 1)
            with pool.Fori(0, DEPTH) as l:
                for dst, src in ((vec[:], a["vec"][l]), (fw[:], a["fw"][l]), (dec, a["decay"][l]),
                                 (rw[:], a["router"][l]), (qkw[:], a["qkw"][l]), (fbias, a["fbias"][l])):
                    pool.dma_start(dst, src).then_inc(lay, 16)
                for n in range(20):
                    pool.wait_ge(k_evac, l * 20 + n + 1)
                    apart(pool)
                    pool.dma_start(a["kspec"][n // 10, (n % 10) // 2, n % 2],
                                   kout[:, n % 4, :]).then_inc(k_stored[n % 4], 16)
                for i in range(4):
                    pool.wait_ge(k_stored[i], l * 80 + 80)
                    apart(pool)
                end_phase(pool, l, 0)
                with pool.Fori(0, 6) as g:
                    for i in range(4):
                        pool.wait_ge(sg_ready, l * 24 + g * 4 + (i + 5))
                        apart(pool)
                        pool.dma_start(a["gates"][g * 4 + i], sgb[:, i, :]).then_inc(sg_stored[i], 16)
                    for i in range(4):
                        pool.wait_ge(sg_stored[i], l * 96 + g * 16 + 16)
                        apart(pool)
                        pool.drain().then_inc(sg_free, 1)
                pool.wait_ge(prep_done, l + 1)
                apart(pool)
                pool.dma_start(a["new_k"][l], qkv[:, 0, NQ * HD:QK]).then_inc(cache_st, 16)
                pool.dma_start(a["new_v"][l], qkv[:, 0, QK:QKV]).then_inc(cache_st, 16)
                pool.wait_ge(cache_st, l * 32 + 32)
                apart(pool)
                end_phase(pool, l, 1)
                pool.dma_start(kT[:, P:P + PAST], a["ctx_k"][l]).then_inc(a_ctx, 16)
                pool.dma_start(ctxv, a["ctx_v"][l]).then_inc(a_ctx, 16)
                end_phase(pool, l, 2)
                pool.dma_start(CS, a["cs"]).then_inc(cs_loaded, 16)
                for o in range(2):
                    if o:
                        pool.wait_ge(y_mul, l * 10 + 5)
                        apart(pool)
                    pool.dma_start(Kb, a["kspec"][o].rearrange("c r p n -> p c r n")).then_inc(k_loaded, 16)
                end_phase(pool, l, 3)
                for n in range(24):
                    half, br, m = n // 12, n % 12 // 4, n % 4
                    if n >= 4:
                        pool.wait_ge(br_read, l * 24 + n - 3)
                        apart(pool)
                    pool.dma_start(sgin[:, n % 4, :], a["gates"][8 * br + 4 * half + m]).then_inc(sg_in[n % 4], 16)
                for i in range(4, PHASES):
                    if i == 7:
                        pool.memset(yc, 0.0).then_inc(g_zero, 1)
                    end_phase(pool, l, i)
            pool.dma_start(a["y"], X[:]).then_inc(out_st, 16)
            pool.wait_ge(out_st, 16)
            apart(pool)

        @block.tensor
        def _(pe):
            def item(l, p, j=0):
                pe.wait_ge(landed[p % SLOT], l * (16 * LAPS) + j * 16 + 16 * (p // SLOT + 1))
                return ring[:, p % SLOT, :]

            def chunk(b, lhs, rhs, n=KC):
                for k in range(n):
                    for g, c0, c1 in GROUPS:
                        mm = pe.matmul(tok(b)[:, c0:c1], lhs(k), rhs(k, c0, c1), start=k == 0, stop=k == n - 1)
                return mm

            def mean_square(l, src, n):
                for k in range(KC):
                    pe.wait_ge(s_sq, l * 16 + 8 * n + k + 1)
                    for g, c0, c1 in GROUPS:
                        mm = pe.matmul(tok(0)[:, c0:c1], onesm[:], src[:, k, c0:c1], start=k == 0, stop=k == KC - 1)
                mm.then_inc(s_ms, 1)

            pe.wait_ge(consts, N_CONSTS)
            pe.wait_ge(s_cs, 1)
            for _ in range(2):
                pe.drain().then_inc(a_pv, 1)
            with pe.Fori(0, DEPTH) as l:
                with pe.Fori(0, N_MOD // SLOT) as it:
                    def turn(s):
                        pe.wait_ge(modrow_sb, l * N_MOD + it * SLOT + (s + 1 + SLOT))
                        pe.wait_ge(modcol_read, l * N_MOD + it * SLOT + (s + 1))
                        for c in range(2):
                            mm = pe.matmul(ps[:, 4 + s, 2 * c:2 * c + 2], mrow[:, s, P * c:P * c + P], sel[:],
                                           start=True, stop=True)
                        mm.then_inc(modcol_ready, 1)

                    for s in range(SLOT):
                        w = item(l, s, it).rearrange("p (k n) -> p k n", k=KC)
                        pe.wait_ge(modrow_sb, l * N_MOD + it * SLOT + (s + 1))
                        for k in range(KC):
                            j = k % 4
                            mm = pe.matmul(ps[32 * j:32 * j + 32, s, 0:256], cs[:, k, :], w[:, k, :],
                                           start=k < 4, stop=k >= 4)
                        mm.then_inc(item_used, 1)
                        if s:
                            turn(s - 1)
                    turn(SLOT - 1)
                pe.wait_ge(lay, l * 96 + 96)
                for n, (w, src) in enumerate(((fw[0:POS, 0:FH], zfeat), (fw[:, FH:2 * FH], fh1))):
                    if n:
                        pe.wait_ge(f_sin, l * 2 + 1)
                    else:
                        pe.wait_ge(modrow_sb, l * N_MOD + N_MOD + SLOT)
                        pe.wait_ge(modcol_read, l * N_MOD + N_MOD + SLOT)
                    apart(pe)
                    for g, c0, c1 in GROUPS:
                        mm = pe.matmul(tok(0)[0:FH, c0:c1], w, src[:, c0:c1], start=True, stop=True)
                    mm.then_inc(f_mm, 1)
                pe.wait_ge(f_sin, l * 2 + 2)
                pe.wait_ge(f_ones, l + 1)
                w3 = item(l, P_FILT)
                for n in range(2 * NT):
                    t, o = n // 2, n % 2
                    if n >= 2:
                        pe.wait_ge(f_tapsread, l * 10 + n - 1)
                    for d in range(2):
                        mm = pe.matmul(ps[:, 2 + 2 * (n % 2) + d, :], fh2[:, P * t:P * t + P],
                                       w3[0:FH + 1, DH * (2 * d + o):DH * (2 * d + o + 1)], start=True, stop=True)
                    mm.then_inc(item_used if n == 2 * NT - 1 else f_taps, 1)
                cf = [item(l, P_FILT + 1 + r).rearrange("p (t k) -> p t k", t=4) for r in range(2)]
                pe.wait_ge(f_tapsread, l * 10 + 10)
                for n in range(20):
                    o, kc, r = n // 10, n % 10 // 2, n % 2
                    src = (fa, fb)[r]
                    if n >= 2:
                        pe.wait_ge(k_evac, l * 20 + n - 1)
                    if kc == 0:
                        mm = pe.matmul(ps[:, n % 2, :], cfi[:, r, :], src[:, 0, o, :], start=True, stop=True)
                    for t in range(4 if kc else 0):
                        mm = pe.matmul(ps[:, n % 2, :], cf[r][:, t, P * (kc - 1):P * kc], src[:, 1 + t, o, :],
                                       start=t == 0, stop=t == 3)
                    mm.then_inc(item_used if n >= 18 else k_ready, 1)
                end_phase(pe, l, 0)

                mean_square(l, sq, 0)
                pe.wait_ge(s_h, l * 32 + 16)

                def transposes(c):
                    pe.wait_ge(conv_done, l * 12 + c + 1)
                    if c:
                        pe.wait_ge(tr_evac, l * 8 + c)
                    for t in range(NT):
                        x0 = P * t + (t > 0)
                        mm = pe.transpose(ps[:, 6 + t // 4, P * (t % 4):P * (t % 4) + P], cv[:, c % 2, x0:x0 + P],
                                          ident[:])
                    mm.then_inc(tr_ready, 1)

                for c in range(24):
                    p = P_HY + c // 2
                    w = item(l, p).rearrange("p (k n) -> p k n", k=KC)
                    if c >= 3:
                        wait_chunk_freed(pe, l, c - 3)
                    mm = chunk(c % 3, lambda k: w[:, k, P * (c % 2):P * (c % 2) + P], lambda k, c0, c1: h[:, k, c0:c1])
                    mm.then_inc(item_used if c % 2 else chunk_ready, 1)
                    if 1 <= c <= 8:
                        transposes(c - 1)
                for i in range(3):
                    w = item(l, P_QKV + i).rearrange("p (k n) -> p k n", k=KC)
                    for u in range(3):
                        n = 24 + 3 * i + u
                        wait_chunk_freed(pe, l, n - 3)
                        for t in range(2 * u, min(2 * u + 2, NT)):
                            for k in range(KC):
                                mm = pe.matmul(ps[:, 2 * (n % 3) + t % 2, 0:256], h[:, k, P * t:P * t + P], w[:, k, :],
                                               start=k == 0, stop=k == KC - 1)
                        mm.then_inc(item_used if u == 2 else chunk_ready, 1)
                wait_chunk_freed(pe, l, 32)
                pe.wait_ge(tr_evac, l * 8 + 8)
                apart(pe)
                with pe.Fori(0, 3) as it:
                    for s in range(4):
                        p = P_GATE + s
                        w = item(l, p, it).rearrange("p (k n) -> p k n", k=KC)
                        for c in range(2):
                            n = 2 * s + c
                            pe.wait_ge(sg_ready, l * 24 + it * 8 + (n + 1))
                            mm = chunk(n % 4, lambda k: w[:, k, P * c:P * c + P], lambda k, c0, c1: h[:, k, c0:c1])
                            mm.then_inc(item_used if c else chunk_ready, 1)
                end_phase(pe, l, 1)

                for t in range(NT):
                    if t >= 2:
                        pe.wait_ge(a_trev, l * 6 + t - 1)
                    for j in range(4):
                        mm = pe.transpose(ps[:, t % 2, P * j:P * j + P], qkv[:, t, P * j:P * j + P], ident[:])
                    mm.then_inc(a_tr, 1)
                for t in range(NT):
                    mm = pe.transpose(ps[:, 2 + (t + 3) // 4, P * ((t + 3) % 4):P * ((t + 3) % 4) + P],
                                      qkv[:, t, NQ * HD:QK], ident[:])
                mm.then_inc(a_tr, 1)
                pe.wait_ge(a_trev, l * 6 + 6)
                pe.wait_ge(a_ctx, l * 32 + 32)
                apart(pe)
                def scores(j, u):
                    g, t = u // 5, u % 5
                    if t == 0:
                        pe.wait_ge(a_qj, l * 8 + j * 2 + (g + 1))
                    pe.wait_ge(a_exp, l * 40 + j * 10 + (u + 1))
                    apart(pe)
                    q = qj[HD * g:HD * g + HD, P * t:P * t + P]
                    kk = kT[HD * g:HD * g + HD, :]
                    b = 2 * (u % 2)
                    if t == 0:
                        mm = pe.matmul(ps[:, b, 0:P], q, kk[:, 0:P], start=True, stop=True)
                    else:
                        pe.matmul(ps[:, b, 0:512], q, kk[:, P:P + 512], start=True, stop=True)
                        mm = pe.matmul(ps[:, b + 1, 0:P], q, kk[:, P + 512:P + 640], start=True, stop=True)
                    mm.then_inc(a_s, 1)

                def turn_p(j, u):
                    t = u % 5
                    pe.wait_ge(a_norm, l * 40 + j * 10 + (u + 1))
                    pe.wait_ge(a_ptev, l * 40 + j * 10 + (u + 1))
                    for kt in range(1 if t == 0 else NT):
                        mm = pe.transpose(ps[:, 4 + kt // 4, P * (kt % 4):P * (kt % 4) + P],
                                          Pb[:, u % 2, P * kt:P * kt + P], ident[:])
                    mm.then_inc(a_pt, 1)

                def values(j, g, kt):
                    vc = slice(QK + HD * g, QK + HD * g + HD)
                    o = slice(HD * g, HD * g + HD)
                    if kt == 0:
                        pe.wait_ge(a_ptev, l * 40 + j * 10 + (5 * g + 6))
                        if g == 0:
                            pe.wait_ge(a_pvev, l * 4 + j + 1)
                            apart(pe)
                        pe.matmul(ps[o, 6, 0:P], qkv[:, 0, vc], PTi[:, g, :], start=True, stop=True)
                    v = ctxv[:, HD * g:HD * g + HD] if kt == 0 else qkv[:, kt, vc]
                    mm = pe.matmul(ps[o, 7, :], v, PT[:, g, kt, :], start=kt == 0, stop=kt == NT - 1)
                    if kt == NT - 1:
                        mm.then_inc(a_pv, 1)

                def heads(j, first, last):
                    for u in range(10):
                        turn_p(j, u)
                        if u + 2 < 10:
                            scores(j, u + 2)
                        elif not last:
                            scores(j + 1, u - 8)
                        if u >= 5:
                            values(j, 0, u - 5)
                        elif not first:
                            values(j - 1, 1, u)

                scores(0, 0)
                scores(0, 1)
                heads(0, True, False)
                with pe.Fori(1, 3) as j:
                    heads(j, False, False)
                heads(3, False, True)
                for kt in range(NT):
                    values(3, 1, kt)
                end_phase(pe, l, 2)

                pe.wait_ge(cs_loaded, l * 16 + 16)
                for o in range(2):
                    if o:
                        pe.wait_ge(y_out, l * 9 + 5)
                    for kc in range(NT):
                        n = 5 * o + kc
                        if kc >= 4:
                            pe.wait_ge(y_mul, l * 10 + n - 3)
                        for r in range(2):
                            bank = 2 * (kc % 4) + r
                            if kc == 0:
                                mm = pe.matmul(ps[:, bank, :], csi[:, r, :], u_tm[:, 0, :], start=True, stop=True)
                            for t in range(4 if kc else 0):
                                mm = pe.matmul(ps[:, bank, :], CS[:, r, t, P * (kc - 1):P * kc], u_tm[:, 1 + t, :],
                                               start=t == 0, stop=t == 3)
                        mm.then_inc(y_fwd, 1)
                    pe.wait_ge(y_mul, l * 10 + 5 * o + 5)
                    for m in range(NT - o):
                        n = 5 * o + m
                        if m >= 2:
                            pe.wait_ge(y_out, l * 9 + n - 1)
                        b = 2 * (m % 2)
                        if o == 0 and m == 0:
                            for r in range(2):
                                mm = pe.matmul(ps[:, b, :], csi[:, r, :], Yb[:, 0, r, :], start=r == 0, stop=r == 1)
                        elif o == 0:
                            for kc in range(4):
                                for r in range(2):
                                    mm = pe.matmul(ps[:, b, :], CS[:, r, kc, P * (m - 1):P * m], Yb[:, 1 + kc, r, :],
                                                   start=kc + r == 0, stop=kc + r == 4)
                        else:
                            tb = tok(m % 2)
                            for r in range(2):
                                pe.matmul(tb[:, 0:LI], Yb[:, 0, r, P * m:P * m + P], csi[:, r, :], start=r == 0,
                                          stop=r == 1)
                            for kc in range(4):
                                for r in range(2):
                                    mm = pe.matmul(tb[:, LI:T], Yb[:, 1 + kc, r, P * m:P * m + P], CS[:, r, kc, :],
                                                   start=kc + r == 0, stop=kc + r == 4)
                        mm.then_inc(y_inv, 1)
                end_phase(pe, l, 3)

                for n in range(24):
                    half, br, m = n // 12, n % 12 // 4, n % 4
                    w = item(l, P_BR + n // 4).rearrange("p (k n) -> p k n", k=4)
                    if n >= 4:
                        pe.wait_ge(br_read, l * 24 + n - 3)
                    mm = chunk(n % 4, lambda k: w[:, k, P * m:P * m + P], lambda k, c0, c1: Y3[:, br, k, c0:c1], 4)
                    mm.then_inc(item_used if m == 3 else br_ready, 1)
                pe.wait_ge(br_read, l * 24 + 24)
                for c in range(KC):
                    w = item(l, P_WO + c // 2).rearrange("p (k n) -> p k n", k=KC)
                    if c >= 4:
                        pe.wait_ge(wo_read, l * 8 + c - 3)
                    mm = chunk(c % 4, lambda k: w[:, k, P * (c % 2):P * (c % 2) + P],
                               lambda k, c0, c1: merged[:, k, c0:c1])
                    mm.then_inc(item_used if c % 2 else wo_ready, 1)
                end_phase(pe, l, 4)

                mean_square(l, sq2, 1)
                end_phase(pe, l, 5)

                for t in range(NT):
                    for k in range(KC):
                        mm = pe.matmul(ps[:, 0, NE * t:NE * t + NE], h[:, k, P * t:P * t + P], rw[:, k, :],
                                       start=k == 0, stop=k == KC - 1)
                mm.then_inc(r_lg, 1)
                for n in range(2 * NT):
                    t, hf = n // 2, n % 2
                    if n >= 2:
                        pe.wait_ge(t_evac, l * 19 + n - 1)
                    for i in range(4):
                        mm = pe.transpose(ps[:, 4 + n % 2, P * i:P * i + P], h[:, 4 * hf + i, P * t:P * t + P],
                                          ident[:])
                    mm.then_inc(t_ready, 1)
                pe.wait_ge(r_aff, l + 1)
                for t in range(NT):
                    mm = pe.transpose(tok(1)[0:NE, P * t:P * t + P], aff[:, t, :], ident[:])
                mm.then_inc(r_affT, 1)
                pe.wait_ge(r_mask, l + 1)
                apart(pe)
                for t in range(NT):
                    mm = pe.transpose(ps[:, 0, NE * t:NE * t + NE], mask[:, P * t:P * t + P], ident[0:NE, 0:NE])
                mm.then_inc(r_maskT, 1)
                pe.wait_ge(r_mt, l + 1)
                for t in range(NT):
                    pe.matmul(ps[:, 1, NE * t:NE * t + NE], utri[:], maskT[:, t, :], start=True, stop=t <= 1)
                    for s in range(1, t):
                        mm = pe.matmul(ps[:, 1, NE * t:NE * t + NE], ones1[:], maskT[:, s, :], start=False,
                                       stop=s == t - 1)
                mm.then_inc(r_pos, 1)
                pe.wait_ge(r_P, l + 1)
                pe.wait_ge(t_evac, l * 19 + 10)
                for n in range(3 * KC):
                    k, part = n // 3, n % 3
                    if n >= 4:
                        pe.wait_ge(g_evac, l * 25 + n - 3)
                    bank = ps[:, n % 4, :]
                    if part < 2:
                        for t in range(4):
                            mm = pe.matmul(bank, h2_tm[:, 1 + t, P * k:P * k + P], Ps[:, t, 512 * part:512 * part + 512],
                                           start=t == 0, stop=t == 3)
                    else:
                        mm = pe.matmul(bank[:, 0:256], h2_tm[:, 0, P * k:P * k + P], Pi[:, :, 0:CAP[0]],
                                       start=True, stop=True)
                    mm.then_inc(g_ready, 1)
                pe.wait_ge(g_evac, l * 25 + 21)
                for e in range(NE):
                    for t in range(4):
                        pe.matmul(ps[0:CAP[1], 0, e:e + 1], Ps[:, t, HD * e:HD * e + HD], aff[:, 1 + t, e:e + 1],
                                  start=t == 0, stop=t == 3)
                    mm = pe.matmul(ps[CAP[1]:SLOTS, 0, e:e + 1], Pi[:, e, 0:CAP[0]], aff[:, 0, e:e + 1],
                                   start=True, stop=True)
                mm.then_inc(g_ready, 1)
                for n in range(8):
                    pe.wait_ge(t_evac, l * 19 + 10 + max(n - 1, 0))
                    for t in range(4):
                        mm = pe.transpose(ps[:, 4 + n % 2, P * t:P * t + P], Ps[:, t, P * n:P * n + P], ident[:])
                    mm.then_inc(t_ready, 1)
                for g in range(4):
                    mm = pe.transpose(ps[:, 6, P * g:P * g + P],
                                      Pi[:, 4 * g:4 * g + 4, :].rearrange("p e s -> p (e s)"), ident[:])
                mm.then_inc(t_ready, 1)
                end_phase(pe, l, 6)

                with pe.Fori(0, NE // 4) as b:
                    for ee in range(4):
                        p0 = P_EXP + 6 * ee

                        def w_in_item(i):
                            return item(l, p0 + i, b * 6).rearrange("p (k n) -> p k n", k=KC)

                        x = xe[:, ee % 2]
                        pe.wait_ge(e_x, l * NE + b * 4 + ee + 1)
                        def up(hf, which):
                            w = w_in_item(2 * hf + which)
                            for k in range(KC):
                                mm = pe.matmul(ps[0:SLOTS, 2 * hf + which, 0:256], x[:, k, :], w[:, k, :],
                                               start=k == 0, stop=k == KC - 1)
                            mm.then_inc(item_used, 1)

                        def turn_hidden(hf):
                            pe.wait_ge(e_hid, l * 2 * NE + b * 8 + 2 * ee + hf + 1)
                            for i in range(2):
                                mm = pe.transpose(ps[:, 4 + hf, SLOTS * i:SLOTS * i + SLOTS],
                                                  hid[:, ee % 2, P * (2 * hf + i):P * (2 * hf + i) + P],
                                                  ident[0:SLOTS, 0:SLOTS])
                            mm.then_inc(e_t, 1)

                        def down(c, hf):
                            for k in range(2 * hf, 2 * hf + 2):
                                mm = pe.matmul(ps[0:SLOTS, 6 + c, :], hidT[:, ee % 2, k, :], wd[c][:, k, :],
                                               start=k == 0, stop=k == 3)
                            return mm

                        up(0, 0)
                        up(0, 1)
                        up(1, 0)
                        turn_hidden(0)
                        up(1, 1)
                        wd = [item(l, p0 + 4 + i, b * 6).rearrange("p (k n) -> p k n", k=4) for i in range(2)]
                        pe.wait_ge(e_hidT, l * 2 * NE + b * 8 + 2 * ee + 1)
                        pe.wait_ge(e_yev, l * NE + b * 4 + ee + 1)
                        pe.wait_ge(e_ycev, l * NE + b * 4 + ee + 1)
                        down(0, 0)
                        turn_hidden(1)
                        down(1, 0)
                        pe.wait_ge(e_hidT, l * 2 * NE + b * 8 + 2 * ee + 2)
                        down(0, 1).then_inc(item_used, 1)
                        down(1, 1).then_inc(item_used, 1)
                end_phase(pe, l, 7)

                for m in range(KC):
                    if m >= 4:
                        pe.wait_ge(c_read, l * 8 + m - 3)
                    tb = tok(m % 4)
                    for g in range(4):
                        pe.matmul(tb[:, 0:LI], yc[:, g, P * m:P * m + P], PTc[:, g, :], start=g == 0, stop=g == 3)
                    for n in range(8):
                        mm = pe.matmul(tb[:, LI:T], ys[:, n, P * m:P * m + P], PTs[:, n, :], start=n == 0, stop=n == 7)
                    mm.then_inc(c_ready, 1)
                end_phase(pe, l, 8)

        @block.scalar
        def _(act):
            def copy(o, i):
                return act.activation(o, i, ACT.Copy)

            def norm(l, n, squares, root, dst):
                for k in range(KC):
                    act.activation(squares[:, k, :], X[:, k, :], ACT.Square).then_inc(s_sq, 1)
                act.wait_ge(s_ms, l * 2 + n + 1)
                act.activation(root, tok(0), ACT.Sqrt, bias=eps[:, 0:1]).then_inc(s_rt, 1)
                for k in range(KC):
                    act.wait_ge(s_xn, l * 16 + 8 * n + k + 1)
                    for g, c0, c1 in GROUPS:
                        act.activation(dst[:, k, c0:c1], dst[:, k, c0:c1], ACT.Identity,
                                       bias=mod[:, 24 * n + k, g:g + 1]).then_inc(s_h, 1)

            act.wait_ge(consts, N_CONSTS)
            act.wait_ge(s_csz, 1)
            act.activation(cs[:, :, 0:2], cond[:], ACT.Silu).then_inc(s_cs, 1)
            for _ in range(SLOT):
                act.drain().then_inc(modrow_sb, 1)
                act.drain().then_inc(sg_ready, 1)
            act.drain().then_inc(e_ycev, 1)
            for _ in range(2):
                act.drain().then_inc(a_exp, 1)
            act.drain().then_inc(a_ptev, 1)
            act.drain().then_inc(a_pvev, 1)
            with act.Fori(0, DEPTH) as l:
                with act.Fori(0, N_MOD // SLOT) as it:
                    for s in range(SLOT):
                        act.wait_ge(item_used, l * ITEMS + it * SLOT + (s + 1))
                        act.wait_ge(modcol_read, l * N_MOD + it * SLOT + (s + 1))
                        copy(mrow[:, s, :], ps[:, s, 0:256]).then_inc(modrow_sb, 1)
                for n, dst in enumerate((fh1, fh2)):
                    act.wait_ge(f_arg, l * 2 + n + 1)
                    act.activation(dst[0:FH, :], farg, ACT.Sin).then_inc(f_sin, 1)
                act.wait_ge(f_dec, l + 1)
                for t in range(NT):
                    if t:
                        act.wait_ge(f_tapsread, l * 10 + 2 * t)
                    act.activation(win, dec, ACT.Exp, scale=tneg[:, t:t + 1]).then_inc(f_win, 1)
                for n in range(20):
                    if n >= 18:
                        act.wait_ge(item_used, l * ITEMS + P_FILT + 1 + n - 17)
                    else:
                        act.wait_ge(k_ready, l * 18 + n + 1)
                    if n >= 4:
                        act.wait_ge(k_stored[n % 4], l * 80 + 16 * (n // 4))
                    copy(kout[:, n % 4, :], ps[:, n % 2, :]).then_inc(k_evac, 1)
                end_phase(act, l, 0)
                norm(l, 0, sq, rstd, h)
                act.wait_ge(pads, l + 1)

                def evac_tr(c):
                    act.wait_ge(tr_ready, l * 8 + c + 1)
                    dst = (u_tm, x1_tm)[c // 4][:, :, P * (c % 4):P * (c % 4) + P]
                    src = ps[:, 6:8, :].rearrange("p a n -> p (a n)")[:, 0:T].rearrange("p (t n) -> p t n", t=NT)
                    copy(dst, src).then_inc(tr_evac, 1)

                for c in range(24):
                    if freed_by(c)[0] == "act":
                        wait_chunk(act, l, c)
                        if c < 12:
                            if c >= 2:
                                act.wait_ge(conv_done, l * 12 + c - 1)
                            copy(raw[:, c % 2, 1:1 + LI], tok(c % 3)[:, 0:LI])
                            copy(raw[:, c % 2, 2 + LI:2 + T], tok(c % 3)[:, LI:T]).then_inc(act_freed, 1)
                        else:
                            if c >= 18:
                                act.wait_ge(dve_freed, l * 8 + c % 2 + 1)
                            copy(ubuf[:, c % 2, :], tok(c % 3)).then_inc(act_freed, 1)
                    if 2 <= c <= 9:
                        evac_tr(c - 2)
                for n in range(9):
                    i, u = n // 3, n % 3
                    wait_chunk(act, l, 24 + n)
                    t1 = min(2 * u + 2, NT)
                    b = 2 * ((24 + n) % 3)
                    copy(qkv[:, 2 * u:t1, 256 * i:256 * i + 256], ps[:, b:b + t1 - 2 * u, 0:256]).then_inc(act_freed, 1)
                act.wait_ge(qs_ready, l + 1)
                act.activation(st5[:], st5[:], ACT.Sqrt, bias=eps[:, 0:1], scale=1.0 / HD).then_inc(qrt, 1)
                with act.Fori(0, 3) as it:
                    for n in range(8):
                        if n % 2:
                            act.wait_ge(item_used, l * ITEMS + it * 4 + (P_GATE + n // 2 + 1))
                        else:
                            act.wait_ge(chunk_ready, l * 30 + it * 4 + (18 + n // 2 + 1))
                        act.wait_ge(sg_free, l * 24 + it * 8 + (n + 1))
                        act.activation(sgb[:, n % 4, :], tok(n % 4), ACT.Sigmoid).then_inc(sg_ready, 1)
                end_phase(act, l, 1)
                for t in range(NT):
                    act.wait_ge(a_tr, l * 6 + t + 1)
                    act.activation(qT[:, :, P * t:P * t + P], ps[:, t % 2, :].rearrange("p (j n) -> p j n", j=4),
                                   ACT.Copy, scale=QSCALE).then_inc(a_trev, 1)
                act.wait_ge(a_tr, l * 6 + 6)
                copy(kT[:, 0:P], tok(1)[:, 0:LI])
                copy(kT[:, P + PAST:], tok(1)[:, LI:T]).then_inc(a_trev, 1)
                def exp(j, u):
                    t = u % 5
                    n = P if t == 0 else T
                    act.wait_ge(a_max, l * 40 + j * 10 + (u + 1))
                    src = ps[:, 2 * (u % 2):2 * (u % 2) + 2, :].rearrange("p a n -> p (a n)")[:, 0:n]
                    act.activation(Pb[:, u % 2, 0:n], src, ACT.Exp, bias=nb[:, u % 2:u % 2 + 1],
                                   accum_out=rsum[:, u % 2:u % 2 + 1]).then_inc(a_exp, 1)

                def evac_pt(j, u):
                    g, t = u // 5, u % 5
                    act.wait_ge(a_pt, l * 40 + j * 10 + (u + 1))
                    act.wait_ge(a_pv, l * 8 + j * 2 + (g + 1))
                    flat = ps[:, 4:6, :].rearrange("p a n -> p (a n)")
                    if t == 0:
                        copy(PTi[:, g, :], flat[:, 0:P]).then_inc(a_ptev, 1)
                    else:
                        copy(PT[:, g, :, P * (t - 1):P * t],
                             flat[:, 0:T].rearrange("p (k n) -> p k n", k=NT)).then_inc(a_ptev, 1)

                def evac_values(j):
                    act.wait_ge(a_pv, l * 8 + j * 2 + 4)
                    copy(Y3[:, 1, j, 0:LI], ps[:, 6, 0:LI])
                    copy(Y3[:, 1, j, LI:T], ps[:, 7, :]).then_inc(a_pvev, 1)

                def heads(j, first, last):
                    for u in range(10):
                        evac_pt(j, u)
                        if u == 5 and not first:
                            evac_values(j - 1)
                        if u + 2 < 10:
                            exp(j, u + 2)
                        elif not last:
                            exp(j + 1, u - 8)

                exp(0, 0)
                exp(0, 1)
                heads(0, True, False)
                with act.Fori(1, 3) as j:
                    heads(j, False, False)
                heads(3, False, True)
                evac_values(3)
                end_phase(act, l, 2)
                end_phase(act, l, 3)
                end_phase(act, l, 4)
                norm(l, 1, sq2, rstd2, h)
                end_phase(act, l, 5)

                def evac_t(n):
                    act.wait_ge(t_ready, l * 19 + n + 1)
                    copy(h2_tm[:, n // 2, 512 * (n % 2):512 * (n % 2) + 512], ps[:, 4 + n % 2, :]).then_inc(t_evac, 1)

                evac_t(0)
                evac_t(1)
                act.wait_ge(r_sub, l + 1)
                act.activation(lg, lg, ACT.Exp).then_inc(r_exp, 1)
                for n in range(2, 10):
                    evac_t(n)
                for n in range(8):
                    act.wait_ge(t_ready, l * 19 + 10 + n + 1)
                    copy(PTs[:, n, :], ps[:, 4 + n % 2, :]).then_inc(t_evac, 1)
                act.wait_ge(t_ready, l * 19 + 19)
                copy(PTc, ps[:, 6, :].rearrange("p (g n) -> p g n", g=4)).then_inc(t_evac, 1)
                end_phase(act, l, 6)

                act.wait_ge(g_zero, l + 1)
                with act.Fori(0, NE // 4) as b:
                    for ee in range(4):
                        p0 = P_EXP + 6 * ee
                        if ee == 0:
                            copy(xe[:, 0], xs[:, :, b * 4, :]).then_inc(e_x, 1)
                        for hf in range(2):
                            act.wait_ge(item_used, l * ITEMS + b * 24 + (p0 + 2 * hf + 1))
                            act.activation(sg[:, ee % 2, 256 * hf:256 * hf + 256], ps[0:SLOTS, 2 * hf, 0:256],
                                           ACT.Silu).then_inc(e_silu, 1)
                        for hf in range(2):
                            act.wait_ge(e_t, l * 2 * NE + b * 8 + (2 * ee + hf + 1))
                            copy(hidT[:, ee % 2, 2 * hf:2 * hf + 2, :],
                                 ps[:, 4 + hf, 0:2 * SLOTS].rearrange("p (k n) -> p k n", k=2)).then_inc(e_hidT, 1)
                            if hf == 0 and ee < 3:
                                copy(xe[:, (ee + 1) % 2], xs[:, :, b * 4 + (ee + 1), :]).then_inc(e_x, 1)
                        act.wait_ge(item_used, l * ITEMS + b * 24 + (p0 + 6))
                        act.activation(yc[32 * ee:32 * ee + CAP[0], b, :],
                                       ps[CAP[1]:SLOTS, 6:8, :].rearrange("p a n -> p (a n)"), ACT.Copy,
                                       scale=gt[CAP[1]:SLOTS, bass.ds(b * 4 + ee, 1)]).then_inc(e_ycev, 1)
                end_phase(act, l, 7)
                end_phase(act, l, 8)

        @block.vector
        def _(dve):
            settle = dve.drain

            def norm(l, n, root, dst):
                dve.wait_ge(s_rt, l * 2 + n + 1)
                dve.reciprocal(root, root)
                settle()
                for k in range(KC):
                    for g, c0, c1 in GROUPS:
                        ins = dve.scalar_tensor_tensor(out=dst[:, k, c0:c1], in0=X[:, k, c0:c1],
                                                       scalar=ws[:, n, k, g:g + 1], in1=root[:, c0:c1],
                                                       op0=ALU.mult, op1=ALU.mult)
                    ins.then_inc(s_xn, 1)

            def residual(src, k, gate):
                for g, c0, c1 in GROUPS:
                    ins = dve.scalar_tensor_tensor(out=X[:, k, c0:c1], in0=src[:, c0:c1],
                                                   scalar=mod[:, gate + k, g:g + 1], in1=X[:, k, c0:c1],
                                                   op0=ALU.mult, op1=ALU.add)
                return ins

            dve.memset(cs[:], 0.0)
            dve.memset(eps[:], EPS)
            settle().then_inc(s_csz, 1)
            for _ in range(SLOT):
                settle().then_inc(modcol_read, 1)
            settle().then_inc(e_yev, 1)
            dve.wait_ge(consts, N_CONSTS)
            with dve.Fori(0, DEPTH) as l:
                dve.wait_ge(lay, l * 96 + 96)
                dve.memset(fh2[FH:FH + 1, :], 1.0).then_inc(f_ones, 1)
                dve.tensor_scalar(win, dec, -1.0, None, ALU.mult)
                settle()
                dve.tensor_tensor(dec, dec, win, ALU.max).then_inc(f_dec, 1)
                with dve.Fori(0, N_MOD // SLOT) as it:
                    for s in range(SLOT):
                        dve.wait_ge(modcol_ready, l * N_MOD + it * SLOT + (s + 1))
                        n = it * (2 * SLOT) + 2 * s
                        dve.tensor_tensor(mod[:, bass.ds(n, 2), :],
                                          ps[:, 4 + s, 0:4].rearrange("p (c g) -> p c g", c=2),
                                          vec[:, bass.ds(n, 2)].unsqueeze(2).to_broadcast([P, 2, 2]),
                                          ALU.add).then_inc(modcol_read, 1)
                settle()
                for n in range(2):
                    dve.scalar_tensor_tensor(out=ws[:, n], in0=mod[:, 24 * n + 8:24 * n + 16, :], scalar=1.0,
                                             in1=vec[:, V_N1 + 8 * n:V_N1 + 8 * n + 8].unsqueeze(2)
                                             .to_broadcast([P, KC, 2]),
                                             op0=ALU.add, op1=ALU.mult)
                for n in range(2):
                    dve.wait_ge(f_mm, l * 2 + n + 1)
                    dve.tensor_scalar(farg, tok(0)[0:FH, :], fw[:, 2 * FH + n:2 * FH + n + 1], None, ALU.add)
                    settle()
                    dve.tensor_scalar(frnd, farg, float(1 / (2 * np.pi)), ROUND, ALU.mult, ALU.add)
                    settle()
                    dve.tensor_scalar(frnd, frnd, -ROUND, None, ALU.add)
                    for part in TWO_PI:
                        settle()
                        dve.scalar_tensor_tensor(out=farg, in0=frnd, scalar=-part, in1=farg, op0=ALU.mult,
                                                 op1=ALU.add)
                    settle()
                    dve.tensor_scalar(farg, farg, -PI_IN, PI_IN, ALU.max, ALU.min).then_inc(f_arg, 1)
                for n in range(2 * NT):
                    t, o = n // 2, n % 2
                    settle()
                    dve.wait_ge(f_win, l * 5 + t + 1)
                    if n == 2 * NT - 1:
                        dve.wait_ge(item_used, l * ITEMS + P_FILT + 1)
                    else:
                        dve.wait_ge(f_taps, l * 9 + n + 1)
                    for d in range(2):
                        w0 = DH * (2 * d + o)
                        dve.scalar_tensor_tensor(out=fdir[:, d, :], in0=win[:, w0:w0 + DH], scalar=SHIFT,
                                                 in1=ps[:, 2 + 2 * (n % 2) + d, :], op0=ALU.add, op1=ALU.mult)
                    settle()
                    if t <= 1:
                        dve.memset(fdir[0:1, 1, :], 0.0)
                        settle()
                    dve.tensor_tensor(fa[:, t, o, :], fdir[:, 0, :], fdir[:, 1, :], ALU.add)
                    ins = dve.tensor_tensor(fb[:, t, o, :], fdir[:, 1, :], fdir[:, 0, :], ALU.subtract)
                    if t <= 1:
                        settle()
                        ins = dve.tensor_tensor(fa[0:1, t, o, :], fa[0:1, t, o, :], fbias[:, o, :], ALU.add)
                    ins.then_inc(f_tapsread, 1)
                end_phase(dve, l, 0)

                for b in range(2):
                    for c0 in (0, LI + 1, T + 2):
                        ins = dve.memset(raw[:, b, c0:c0 + 1], 0.0)
                ins.then_inc(pads, 1)
                norm(l, 0, rstd, h)

                def conv(dst, src, w, bias):
                    dve.tensor_scalar(dst, src(1), vec[:, w + 1:w + 2], vec[:, bias:bias + 1], ALU.mult, ALU.add)
                    for tap in (0, 2):
                        settle()
                        ins = dve.scalar_tensor_tensor(out=dst, in0=src(tap), scalar=vec[:, w + tap:w + tap + 1],
                                                       in1=dst, op0=ALU.mult, op1=ALU.add)
                    return ins

                for c in range(24):
                    b = c % 2
                    if c < 12:
                        before = (c // 2) * 2 + c % 2
                        dve.wait_ge(act_freed, l * A_FREED + before + 1)
                        if 2 <= c < 8 or c in (8, 9):
                            dve.wait_ge(tr_ready, l * 8 + c - 1)
                        ins = conv(cv[:, b, :], lambda i: raw[:, b, i:i + T + 1], V_HYW + 3 * c, V_HYB + c)
                        if c < 8:
                            ins.then_inc(conv_done, 1)
                        else:
                            settle()
                            dve.tensor_copy(Y3[:, 0, c - 8, 0:LI], cv[:, b, 0:LI])
                            dve.tensor_copy(Y3[:, 0, c - 8, LI:T], cv[:, b, LI + 1:T + 1]).then_inc(conv_done, 1)
                        continue
                    if freed_by(c)[0] == "act":
                        continue
                    j = 2 * ((c - 12) // 6) + b
                    settle()
                    wait_chunk(dve, l, c)
                    pieces = ((0, LI, 0), (LI, T, 1))
                    if (c - 12) % 6 < 4:
                        dve.wait_ge(act_freed, l * A_FREED + freed_by(12 + 6 * ((c - 12) // 6) + b)[1])
                        for c0, c1, x in pieces:
                            ins = dve.tensor_tensor(raw[:, b, 1 + c0 + x:1 + c1 + x], tok(c % 3)[:, c0:c1],
                                                    ubuf[:, b, c0:c1], ALU.mult)
                        ins.then_inc(dve_freed, 1)
                        settle()
                        conv(cvs[:, b, :], lambda i: raw[:, b, i:i + T + 1], V_SCW + 3 * j, V_SCB + j)
                    else:
                        for c0, c1, x in pieces:
                            ins = dve.tensor_tensor(Y3[:, 2, j, c0:c1], tok(c % 3)[:, c0:c1],
                                                    cvs[:, b, c0 + x:c1 + x], ALU.mult)
                        ins.then_inc(dve_freed, 1)
                dve.wait_ge(act_freed, l * A_FREED + A_FREED)
                qk = qkv[:, :, 0:QK]
                dve.tensor_tensor(prep, qk, qk, ALU.mult)
                settle()
                dve.tensor_reduce(st5[:], prep.rearrange("p t (h d) -> p t h d", h=10), AX.X, ALU.add)\
                    .then_inc(qs_ready, 1)
                dve.wait_ge(qrt, l + 1)
                dve.reciprocal(rst5[:], st5[:])
                settle()
                for t in range(NT):
                    heads = qkv[:, t, 0:QK].rearrange("p (h d) -> p h d", h=10)
                    dve.tensor_tensor(heads, heads, rst5[:, t, :].unsqueeze(2).to_broadcast([P, 10, HD]), ALU.mult)
                settle()
                for t in range(NT):
                    dve.tensor_tensor(qkv[:, t, 0:QK], qkv[:, t, 0:QK], qkw[:], ALU.mult)
                settle()
                prep2 = region(98, [NT - 1, QK])
                for t in range(1, NT):
                    v4 = "p (h a f i) -> p h a f i"
                    src = qkv[:, t, 0:QK]
                    dve.tensor_tensor(prep[:, t, :].rearrange("p (h d) -> p h d", h=10),
                                      src.rearrange("p (h d) -> p h d", h=10),
                                      rope[:, 0, t - 1, :].unsqueeze(1).to_broadcast([P, 10, HD]), ALU.mult)
                    for f in range(2):
                        sin = rope[:, 1, t - 1, :].rearrange("p (a f i) -> p a f i", a=2, f=2)[:, :, f, :]
                        for axis in range(2):
                            dve.tensor_tensor(prep2[:, t - 1, :].rearrange(v4, h=10, a=2, f=2)[:, :, axis, f, :],
                                              src.rearrange(v4, h=10, a=2, f=2)[:, :, axis, 1 - f, :],
                                              sin[:, axis, :].unsqueeze(1).to_broadcast([P, 10, 16]), ALU.mult)
                settle()
                for t in range(1, NT):
                    dve.tensor_tensor(qkv[:, t, 0:QK], prep[:, t, :], prep2[:, t - 1, :], ALU.add)
                settle().then_inc(prep_done, 1)
                end_phase(dve, l, 1)

                dve.wait_ge(a_trev, l * 6 + 6)
                apart(dve)
                def queries(j, g):
                    dve.tensor_copy(qj[HD * g:HD * g + HD, :], qT[HD * g:HD * g + HD, j, :]).then_inc(a_qj, 1)

                def row_max(j, u):
                    t = u % 5
                    n = P if t == 0 else T
                    dve.wait_ge(a_s, l * 40 + j * 10 + (u + 1))
                    src = ps[:, 2 * (u % 2):2 * (u % 2) + 2, :].rearrange("p a n -> p (a n)")[:, 0:n]
                    dve.tensor_reduce(nb[:, u % 2:u % 2 + 1], src, AX.X, ALU.max, negate=True).then_inc(a_max, 1)

                def scale_rows(j, u):
                    n = P if u % 5 == 0 else T
                    i = slice(u % 2, u % 2 + 1)
                    dve.wait_ge(a_exp, l * 40 + j * 10 + (u + 3))
                    dve.reciprocal(rinv[:, i], rsum[:, i])
                    settle()
                    dve.tensor_scalar(Pb[:, u % 2, 0:n], Pb[:, u % 2, 0:n], rinv[:, i], None,
                                      ALU.mult).then_inc(a_norm, 1)

                def heads(j, last):
                    for u in range(10):
                        if u + 1 < 10:
                            scale_rows(j, u + 1)
                        elif not last:
                            scale_rows(j + 1, 0)
                        if u + 2 < 10:
                            row_max(j, u + 2)
                        elif not last:
                            row_max(j + 1, u - 8)
                        if u % 5 == 3 and not last:
                            queries(j + 1, u // 5)

                queries(0, 0)
                queries(0, 1)
                row_max(0, 0)
                row_max(0, 1)
                scale_rows(0, 0)
                with dve.Fori(0, 3) as j:
                    heads(j, False)
                heads(3, True)
                end_phase(dve, l, 2)

                for o in range(2):
                    dve.wait_ge(k_loaded, l * 32 + 16 * o + 16)
                    apart(dve)
                    for kc in range(NT):
                        settle()
                        dve.wait_ge(y_fwd, l * 10 + 5 * o + kc + 1)
                        uc, us = ps[:, 2 * (kc % 4), :], ps[:, 2 * (kc % 4) + 1, :]
                        kr, ki = Kb[:, kc, 0, :], Kb[:, kc, 1, :]
                        for i, (x, y) in enumerate(((uc, kr), (us, ki), (us, kr), (uc, ki))):
                            dve.tensor_tensor(ytmp[:, i, :], x, y, ALU.mult)
                        settle()
                        dve.tensor_tensor(Yb[:, kc, 0, :], ytmp[:, 0, :], ytmp[:, 1, :], ALU.add)
                        dve.tensor_tensor(Yb[:, kc, 1, :], ytmp[:, 2, :], ytmp[:, 3, :],
                                          ALU.subtract).then_inc(y_mul, 1)
                    for m in range(NT - o):
                        dve.wait_ge(y_inv, l * 9 + 5 * o + m + 1)
                        if o == 0:
                            ins = dve.tensor_tensor(u_tm[:, m, :], ps[:, 2 * (m % 2), :], x1_tm[:, m, :], ALU.mult)
                        else:
                            ins = dve.tensor_tensor(Y3[:, 0, m, :], tok(m % 2), Y3[:, 0, m, :], ALU.mult)
                        ins.then_inc(y_out, 1)
                end_phase(dve, l, 3)

                for n in range(24):
                    half, br, m = n // 12, n % 12 // 4, n % 4
                    c = 4 * half + m
                    dve.wait_ge(sg_in[n % 4], l * 96 + 16 * (n // 4) + 16)
                    if m == 3:
                        dve.wait_ge(item_used, l * ITEMS + P_BR + n // 4 + 1)
                    else:
                        dve.wait_ge(br_ready, l * 18 + 3 * (n // 4) + m + 1)
                    dst = mtmp[:, n % 2, :] if br else merged[:, c, :]
                    ins = dve.tensor_tensor(dst, tok(n % 4), sgin[:, n % 4, :], ALU.mult)
                    if br:
                        settle()
                        ins = dve.tensor_tensor(merged[:, c, :], merged[:, c, :], dst, ALU.add)
                    ins.then_inc(br_read, 1)
                for c in range(KC):
                    if c % 2:
                        dve.wait_ge(item_used, l * ITEMS + P_WO + c // 2 + 1)
                    else:
                        dve.wait_ge(wo_ready, l * 4 + c // 2 + 1)
                    residual(tok(c % 4), c, 16).then_inc(wo_read, 1)
                end_phase(dve, l, 4)
                norm(l, 1, rstd2, h)
                end_phase(dve, l, 5)

                dve.wait_ge(r_lg, l + 1)
                logits = ps[:, 0, 0:NT * NE].rearrange("p (t e) -> p t e", t=NT)
                dve.tensor_reduce(r1[:, :, 0:1], logits, AX.X, ALU.max)
                settle()
                dve.tensor_tensor(lg, logits, r1[:, :, 0:1].to_broadcast([P, NT, NE]), ALU.subtract)\
                    .then_inc(r_sub, 1)
                dve.wait_ge(r_exp, l + 1)
                dve.tensor_reduce(r1[:, :, 0:1], lg, AX.X, ALU.add)
                settle()
                dve.reciprocal(r1[:, :, 1:2], r1[:, :, 0:1])
                settle()
                dve.tensor_tensor(aff, lg, r1[:, :, 1:2].to_broadcast([P, NT, NE]), ALU.mult).then_inc(r_aff, 1)
                dve.wait_ge(r_affT, l + 1)
                dve.tensor_copy(work, tok(1)[0:NE, :])
                for g, c0, c1 in GROUPS:
                    for _ in range(CAP[g] // 8):
                        settle()
                        dve.max(m8[:], work[:, c0:c1])
                        settle()
                        dve.match_replace(work[:, c0:c1], m8[:], work[:, c0:c1], -1.0)
                settle()
                dve.tensor_scalar(mask, work, 0.0, None, ALU.is_lt).then_inc(r_mask, 1)
                dve.wait_ge(r_maskT, l + 1)
                dve.tensor_copy(maskT, ps[:, 0, 0:NT * NE].rearrange("p (t e) -> p t e", t=NT)).then_inc(r_mt, 1)
                settle()
                dve.wait_ge(r_pos, l + 1)
                dve.scalar_tensor_tensor(out=q1, in0=ps[:, 1, 0:NT * NE].rearrange("p (t e) -> p t e", t=NT),
                                         scalar=1.0, in1=maskT, op0=ALU.add, op1=ALU.mult)
                settle()
                for t in range(NT):
                    n = HD if t else 32
                    dst = Ps[:, t - 1, :].rearrange("p (e s) -> p e s", e=NE) if t else Pi
                    ins = dve.tensor_tensor(dst, iota[:, 0:n].unsqueeze(1).to_broadcast([P, NE, n]),
                                            q1[:, t, :].unsqueeze(2).to_broadcast([P, NE, n]), ALU.is_equal)
                ins.then_inc(r_P, 1)
                for n in range(3 * KC):
                    k, part = n // 3, n % 3
                    dve.wait_ge(g_ready, l * 25 + n + 1)
                    if part < 2:
                        ins = dve.tensor_copy(xs[:, k, 8 * part:8 * part + 8, 0:CAP[1]],
                                              ps[:, n % 4, :].rearrange("p (e s) -> p e s", e=8))
                    else:
                        ins = dve.tensor_copy(xs[:, k, :, CAP[1]:SLOTS],
                                              ps[:, n % 4, 0:256].rearrange("p (e s) -> p e s", e=NE))
                    ins.then_inc(g_evac, 1)
                dve.wait_ge(g_ready, l * 25 + 25)
                dve.tensor_copy(gt[0:SLOTS, :], ps[0:SLOTS, 0, 0:NE]).then_inc(g_evac, 1)
                end_phase(dve, l, 6)

                with dve.Fori(0, NE // 4) as b:
                    for ee in range(4):
                        p0 = P_EXP + 6 * ee
                        for hf in range(2):
                            dve.wait_ge(e_silu, l * 2 * NE + b * 8 + (2 * ee + hf + 1))
                            dve.wait_ge(item_used, l * ITEMS + b * 24 + (p0 + 2 * hf + 2))
                            cols = slice(256 * hf, 256 * hf + 256)
                            dve.tensor_tensor(hid[:, ee % 2, cols], ps[0:SLOTS, 2 * hf + 1, 0:256],
                                              sg[:, ee % 2, cols], ALU.mult).then_inc(e_hid, 1)
                        dve.wait_ge(item_used, l * ITEMS + b * 24 + (p0 + 6))
                        r0 = HD * (ee % 2)
                        dve.tensor_scalar(ys[r0:r0 + HD, b * 2 + ee // 2, :],
                                          ps[0:CAP[1], 6:8, :].rearrange("p a n -> p (a n)"),
                                          gt[0:CAP[1], bass.ds(b * 4 + ee, 1)], None, ALU.mult).then_inc(e_yev, 1)
                end_phase(dve, l, 7)

                for m in range(KC):
                    dve.wait_ge(c_ready, l * 8 + m + 1)
                    residual(tok(m % 4), m, 40).then_inc(c_read, 1)
                end_phase(dve, l, 8)


CONSTS = ("ident", "onesm", "ones1", "utri", "sel", "zfeat", "tneg", "rope", "iota", "csi", "cfi", "cs")


def constants():
    f = np.float32
    out = {"ident": np.eye(P), "onesm": np.full((P, P), 1 / D), "ones1": np.ones((P, P)),
           "utri": np.triu(np.ones((P, P)), 1), "iota": np.tile(np.arange(1, HD + 1), (P, 1))}
    sel = np.zeros((P, 2))
    for g in range(2):
        sel[g::32, g] = 1
    out["sel"] = sel
    z, tn = np.zeros((POS, T)), np.zeros((P, NT))
    for (g, c0, c1), L in zip(GROUPS, (LI, LS)):
        n = np.arange(L)
        bands = np.linspace(1e-4, 15, 16)
        ang = 2 * np.pi * n[:, None] * bands[None] / L
        z[:, c0:c1] = np.concatenate([(n / (L - 1))[:, None], np.cos(ang), np.sin(ang)], 1).T
        for t in range(c0 // P, c1 // P):
            tn[:, t] = -(np.arange(P) + P * t - c0) / (L - 1)
    out["zfeat"], out["tneg"] = z, tn
    n = np.arange(LS)
    inv = 10000.0 ** (-np.arange(0, 32, 2) / 32)
    ar, ac = (n // 64)[:, None] * inv, (n % 64)[:, None] * inv
    cosv = np.concatenate([np.cos(ar), np.cos(ar), np.cos(ac), np.cos(ac)], 1)
    sinv = np.concatenate([-np.sin(ar), np.sin(ar), -np.sin(ac), np.sin(ac)], 1)
    out["rope"] = np.stack([x.reshape(4, P, HD).transpose(1, 0, 2) for x in (cosv, sinv)], 1)

    def tables(L):
        k = np.arange(L) + 0.5
        th, ph = np.pi * np.outer(k, k) / L, np.pi * np.outer(np.arange(L), k) / L
        return np.stack([np.cos(th), np.sin(th)]), np.stack([np.cos(ph), np.sin(ph)]) / L

    (ci, fi), (cl, fl) = tables(LI), tables(LS)
    out["csi"], out["cfi"] = ci.transpose(1, 0, 2), fi.transpose(1, 0, 2)
    out["cs"] = cl.reshape(2, 4, P, LS).transpose(2, 0, 1, 3)
    out["cf"] = fl.reshape(2, 4, P, LS).transpose(0, 2, 1, 3).reshape(2, P, ITEM)
    return {k: np.ascontiguousarray(v, dtype=f) for k, v in out.items()}


def weight_stream(w, cf):
    out = np.zeros((DEPTH, ITEMS, P, ITEM), np.float32)

    def columns(dst, m, width, kc):
        for i in range(m.shape[1] // width):
            dst[i] = m[:, i * width:(i + 1) * width].reshape(kc, P, width).transpose(1, 0, 2).reshape(P, -1)

    heads = np.concatenate([np.concatenate([np.arange(HD) + HD * j, np.arange(HD) + HD * (4 + j)])
                            for j in range(4)])
    for l in range(DEPTH):
        o = out[l]
        columns(o[0:], w["mod_w"][l], 256, KC)
        o[P_FILT, 0:FH] = w["hy_w3"][l]
        o[P_FILT, FH] = w["hy_b3"][l]
        o[P_FILT + 1:P_FILT + 3] = cf
        win = w["w_in"][l]
        columns(o[P_HY:], win[:, 0:1536], 256, KC)
        base = 1536 + QKV
        for jp in range(2):
            for n, part in enumerate((0, 2, 1)):
                c = base + 512 * part + 256 * jp
                columns(o[P_SC + 3 * jp + n:], win[:, c:c + 256], 256, KC)
        columns(o[P_QKV:], win[:, 1536:base][:, np.concatenate([heads, np.arange(NQ * HD, QKV)])], 256, KC)
        columns(o[P_GATE:], win[:, base + 1536:], 256, KC)
        for n, (name, rows) in enumerate((("w_br_a", slice(None)), ("w_br_b", heads), ("w_br_c", slice(None)))):
            for half in range(2):
                columns(o[P_BR + 3 * half + n:], w[name][l][rows][:, 512 * half:512 * half + 512], 512, 4)
        columns(o[P_WO:], w["w_o"][l], 256, KC)
        for e in range(NE):
            p = P_EXP + 6 * e
            for hf in range(2):
                columns(o[p + 2 * hf:], w["exp_w_gate"][l, e][:, 256 * hf:256 * hf + 256], 256, KC)
                columns(o[p + 2 * hf + 1:], w["exp_w_up"][l, e][:, 256 * hf:256 * hf + 256], 256, KC)
            columns(o[p + 4:], w["exp_w_down"][l, e], 512, 4)
    return out.reshape(DEPTH * ITEMS, P, ITEM)


def kernel(**inputs):
    import concourse.bacc as bacc
    from concourse.bass_utils import run_bass_kernel_spmd

    w = {k: np.asarray(v) for k, v in inputs.items()}
    f = constants()
    arrays = {"stream": weight_stream(w, f.pop("cf")), **f}

    def feature_major(x):
        return np.swapaxes(x.reshape(*x.shape[:-1], -1, P), -1, -2)

    tokens = np.concatenate([w["x_prompt"][0], w["x_sample"][0]], 0)
    arrays["x"] = tokens.T.reshape(KC, P, T).transpose(1, 0, 2)
    arrays["cond"] = feature_major(np.stack([w["c_ctx"], w["c"][0]])).transpose(1, 2, 0)

    def taps(x):
        return feature_major(x).transpose(0, 2, 3, 1).reshape(DEPTH, P, -1)

    arrays["vec"] = np.concatenate(
        [feature_major(w["mod_b"]), feature_major(w["norm1_w"]), feature_major(w["norm2_w"]),
         taps(w["hy_short_w"]), feature_major(w["hy_short_b"]), taps(w["sc_w"]), feature_major(w["sc_b"])], 2)
    fw = np.zeros((DEPTH, FH, 2 * FH + 2), np.float32)
    fw[:, 0:POS, 0:FH] = w["hy_w1"]
    fw[:, :, FH:2 * FH] = w["hy_w2"]
    fw[:, :, 2 * FH] = w["hy_b1"]
    fw[:, :, 2 * FH + 1] = w["hy_b2"]
    arrays["fw"] = fw
    arrays["decay"] = np.broadcast_to(w["hy_decay"][:, None], (DEPTH, P, 2048))
    arrays["fbias"] = w["hy_bias"].reshape(DEPTH, 1, 2, DH)
    arrays["router"] = w["router_w"].reshape(DEPTH, KC, P, NE).transpose(0, 2, 1, 3)
    qkw = np.concatenate([np.tile(w["q_norm_w"], (1, NQ)), np.tile(w["k_norm_w"], (1, NKV))], 1)
    arrays["qkw"] = np.broadcast_to(qkw[:, None], (DEPTH, P, QK))
    arrays["ctx_k"] = w["cache_k"][0].reshape(DEPTH, PAST, P).transpose(0, 2, 1)
    arrays["ctx_v"] = w["cache_v"][0].reshape(DEPTH, PAST, P)
    arrays = {k: np.ascontiguousarray(v) for k, v in arrays.items()}

    nc = bacc.Bacc("TRN2", target_bir_lowering=False, num_devices=1)
    args = {k: nc.dram_tensor(f"in_{k}", v.shape, F32, kind="ExternalInput").ap() for k, v in arrays.items()}
    args["kspec"] = nc.dram_tensor("kspec", [2, NT, 2, P, DH], F32, kind="Internal").ap()
    args["gates"] = nc.dram_tensor("gates", [24, P, T], F32, kind="Internal").ap()
    for name, shape in (("y", [P, KC, T]), ("new_k", [DEPTH, SEQ_C, P]), ("new_v", [DEPTH, SEQ_C, P])):
        args[name] = nc.dram_tensor(f"out_{name}", shape, F32, kind="ExternalOutput").ap()
    build(nc, args)
    r = run_bass_kernel_spmd(nc, [{f"in_{k}": v for k, v in arrays.items()}], core_ids=[0]).results[0]
    y = r["out_y"].transpose(1, 0, 2).reshape(D, T).T
    caches = [r[f"out_{n}"].reshape(1, DEPTH, SEQ_C, NKV, HD) for n in ("new_k", "new_v")]
    return (np.ascontiguousarray(y[None, 0:LI]), np.ascontiguousarray(y[None, LI:T]), *caches)
```

```python
from contextlib import ExitStack

import concourse.bass as bass
import numpy as np
from concourse import mybir

ACT = mybir.ActivationFunctionType
ALU = mybir.AluOpType
AX = mybir.AxisListType
F32 = mybir.dt.float32
F32R = mybir.dt.float32r

P = 128
D = 1024
KC = D // P
DEPTH = 2
LI, LS = 128, 512
T = LI + LS
NT = T // P
GROUPS = ((0, 0, LI), (1, LI, T))
HALVES = ((0, T // 2), (T // 2, T))
FRONT, BACK, BACK_R = 56 * 256, 85 * 256 + 128, 50 * 256
DH = 512
NE = 16
EPS = 1e-6
SHIFT = 0.05
HD = 64
NQ, NKV = 8, 2
QK = (NQ + NKV) * HD
QKV = QK + NKV * HD
PAST = 128
POS = 33
FH = 64
CAP = (2 * LI // NE, 2 * LS // NE)
SLOTS = CAP[0] + CAP[1]

ITEM = 2048
SLOT = 4
N_MOD, N_FILT, N_HY, N_SC, N_QKV, N_GATE, N_BR, N_WO, N_EXP = 24, 3, 6, 6, 3, 12, 6, 4, 96
P_FILT = N_MOD
P_HY = P_FILT + N_FILT
P_SC = P_HY + N_HY
P_QKV = P_SC + N_SC
P_GATE = P_QKV + N_QKV
P_BR = P_GATE + N_GATE
P_WO = P_BR + N_BR
P_EXP = P_WO + N_WO
ITEMS = P_EXP + N_EXP
LAPS = ITEMS // SLOT
assert ITEMS % SLOT == 0

V_MODB, V_N1, V_N2, V_HYW, V_HYB, V_SCW, V_SCB, NV = 0, 48, 56, 64, 100, 112, 124, 128

PHASES = 9
TWO_PI = (6.28125, 0.0019340515136718750, 2 * np.pi - 6.28125 - 0.0019340515136718750)
ROUND = 1.5 * 2.0 ** 23
PI_IN = 3.1415925
SEQ_C = LI
N_CONSTS = 16 * 12
QSCALE = HD ** -0.5


def build(nc, a):
    with ExitStack() as ctx:
        def sb(name, shape):
            return ctx.enter_context(nc.sbuf_tensor(name, shape, F32))

        def sem(name):
            return ctx.enter_context(nc.semaphore(name))

        ring = sb("ring", [P, SLOT, ITEM])
        X = sb("X", [P, KC, T])
        ident = sb("ident", [P, P])
        onesm = sb("onesm", [P, P])
        ones1 = sb("ones1", [P, P])
        utri = sb("utri", [P, P])
        sel = sb("sel", [P, 2])
        tneg = sb("tneg", [P, NT])
        rope = sb("rope", [P, 2, NT - 1, HD])
        iota = sb("iota", [P, HD])
        csi = sb("csi", [P, 2, P])
        cfi = sb("cfi", [P, 2, P])
        vec = sb("vec", [P, NV])
        fw = sb("fw", [FH, 2 * FH + 2])
        rw = sb("rw", [P, KC, NE])
        qkw = sb("qkw", [P, QK])
        cs = sb("cs", [P, KC, 32])
        cond = sb("cond", [P, KC, 2])
        mod = sb("mod", [P, 48, 2])
        ws = sb("ws", [P, 2, KC, 2])
        st5 = sb("st5", [P, NT, 10])
        rst5 = sb("rst5", [P, NT, 10])
        mx = sb("mx", [P, 2])
        nb = sb("nb", [P, 2])
        rsum = sb("rsum", [P, 2])
        rinv = sb("rinv", [P, 2])
        gt = sb("gt", [P, NE])
        m8 = sb("m8", [NE, 8])
        eps = sb("eps", [P, 1])
        with nc.sbuf_tensor("front_r", [P, FRONT], F32R) as front_r:
            pass
        front = sb("front", [P, FRONT])
        with nc.sbuf_tensor("back_r", [P, BACK_R], F32R) as back_r:
            pass
        back = sb("back", [P, BACK])
        ps = ctx.enter_context(nc.psum_tensor("ps", [P, 8, 512], F32))

        def region(kb, shape, parts=P, r=False):
            n = int(np.prod(shape))
            o = int(kb * 256)
            if o < FRONT:
                mem, size = (front_r if r else front), FRONT
            else:
                mem, size, o = (back_r if r else back), (BACK_R if r else BACK), o - FRONT
            assert o + n <= size, (kb, shape)
            v = mem[0:parts, o:o + n]
            names = "abcd"[:len(shape)]
            if len(shape) == 1:
                return v
            return v.rearrange(f"p ({' '.join(names)}) -> p {' '.join(names)}",
                               **{names[i]: shape[i] for i in range(len(shape) - 1)})

        def region_r(kb, shape):
            return region(kb, shape, r=True)

        W2 = region_r(40, [2, 2, 1024])
        zfeat = region(88, [T], POS)
        fa, fb = region(0, [NT, 2, DH]), region(20, [NT, 2, DH])
        win, dec = region(40, [2048]), region(48, [2048])
        fdir = region(56, [2, DH])
        kout = region(60, [4, DH])
        farg, frnd = region(68, [T], FH), region(70.5, [T], FH)
        fh1, fh2 = region(73, [T], FH), region(75.5, [T], FH + 1)
        fbias = region(78, [2, DH], 1)
        mrow = region(82, [4, 256])
        h_hi, h_lo, h_x = region_r(0, [KC, T]), region_r(20, [KC, T]), region(20, [KC, T])
        Y3 = region(56, [3, 4, T])
        sq = region(56, [KC, T])
        u_tm, x1_tm = region(86, [NT, DH]), region(96, [NT, DH])
        qkv = region(106, [NT, QKV])
        raw, cv = region(121, [2, T + 3]), region(126.25, [2, T + 1])
        ubuf, rstd = region(131.5, [2, T]), region(131.5, [T])
        sgb = region(136.5, [2, T])
        prep, prep2 = region(121, [2, QK]), region(126.25, [2, QK])
        qT, kT, qj = region(0, [4, T]), region(10, [P + PAST + LS]), region(13, [T])
        ctxv = region(15.5, [P])
        PT, PTi = region(16, [2, NT, LS]), region(36, [2, P])
        Pb = region(37, [2, T])
        Kb = region(0, [NT, 2, DH])
        Yb = region(20, [NT, 2, DH])
        CS = region(40, [2, 4, DH])
        ytmp = region(106, [4, DH])
        Y_hi, Y_lo = region_r(0, [3, 4, T]), region_r(56, [3, 4, T])
        merged, m_lo = region(86, [KC, T]), region_r(86, [KC, T])
        m_hi = [region_r(30, [4, T]), region_r(0, [4, T])]
        sgin, mtmp = region(106, [4, T]), region(116, [2, T])
        h, sq2, rstd2 = region(0, [KC, T]), region(56, [KC, T]), region(131.5, [T])
        h2_tm = region(20, [NT, D])
        Ps, Pi = region(40, [4, NE * HD]), region(56, [NE, 32])
        PTs, PTc = region(58, [8, LS]), region(74, [4, P])
        xs = region(76, [KC, NE, SLOTS])
        aft, work, mask = (region(116 + 2.5 * i, [T], NE) for i in range(3))
        maskT, q1, aff = (region(123.5 + 0.5 * i, [NT, NE]) for i in range(3))
        lg, r1 = region(125, [NT, NE]), region(125.5, [NT, 2])
        ys, yc = region(0, [8, D]), region(32, [4, D])
        xe = region(116, [2, KC, SLOTS])
        sg, hid = region(121, [2, DH], SLOTS), region(125, [2, DH], SLOTS)
        hidT = region(129, [2, 4, SLOTS])

        landed = [sem(f"item_landed{s}") for s in range(SLOT)]
        item_used = sem("item_used")
        phase = sem("phase")
        consts = sem("consts")
        waited = sem("waited")
        lay = sem("layer_vectors")
        s_cs, s_csz = sem("silu_cond"), sem("cs_zeroed")
        modrow_sb, modcol_ready, modcol_read = sem("modrow_sb"), sem("modcol_ready"), sem("modcol_read")
        f_mm, f_arg, f_sin, f_win, f_winread = sem("f_mm"), sem("f_arg"), sem("f_sin"), sem("f_win"), sem("f_winread")
        f_ones, f_dec = sem("f_ones"), sem("f_dec")
        f_taps, f_tapsread = sem("f_taps"), sem("f_taps_read")
        k_ready, k_evac = sem("k_ready"), sem("k_evac")
        k_stored = [sem(f"k_stored{i}") for i in range(4)]
        s_sq, s_ms, s_rt, s_rstd, s_xn, s_h = (sem(n) for n in (
            "squares", "mean_square", "root", "rstd_ready", "x_normed", "h_ready"))
        x_hi, x_lo = sem("operand_hi"), sem("operand_lo")
        OP, OP_Y, OP_M = KC + 12 + KC, KC, KC + 12
        w_hi, w_lo = sem("weights_hi"), sem("weights_lo")
        chunk_ready = sem("chunk_ready")
        act_freed, dve_freed = sem("act_freed"), sem("dve_freed")
        conv_done, tr_ready, tr_evac, pads = sem("conv_done"), sem("tr_ready"), sem("tr_evac"), sem("pads_zeroed")
        prep_done = sem("prep_done")
        qs_ready, qrt = sem("q_squares"), sem("q_root")
        sg_ready, sg_free = sem("sg_ready"), sem("sg_free")
        sg_stored = [sem(f"sg_stored{i}") for i in range(2)]
        cache_st = sem("cache_stored")
        a_tr, a_trev, a_ctx = sem("a_tr"), sem("a_tr_evac"), sem("ctx_loaded")
        a_qj, a_s, a_max, a_exp, a_norm, a_pt, a_ptev, a_pv, a_pvev = (sem(n) for n in (
            "a_qj", "a_scores", "a_max", "a_exp", "a_norm", "a_pt", "a_ptev", "a_pv", "a_pvev"))
        cs_loaded, k_loaded, k_free = sem("cs_loaded"), sem("k_loaded"), sem("k_free")
        y_fwd, y_mul, y_inv, y_out = sem("y_fwd"), sem("y_mul"), sem("y_inv"), sem("y_out")
        sg_in = [sem(f"sg_in{i}") for i in range(4)]
        br_ready, br_read = sem("br_ready"), sem("br_read")
        wo_ready, wo_read = sem("wo_ready"), sem("wo_read")
        r_lg, r_sub, r_exp, r_aff, r_affT, r_aft, r_mask, r_maskT, r_mt, r_pos, r_P = (sem(n) for n in (
            "r_lg", "r_sub", "r_exp", "r_aff", "r_affT", "r_aft", "r_mask", "r_maskT", "r_mt", "r_pos", "r_P"))
        t_ready, t_evac, g_ready, g_evac, g_zero = (sem(n) for n in (
            "t_ready", "t_evac", "g_ready", "g_evac", "yc_zeroed"))
        e_x, e_up, e_silu, e_hid, e_t, e_hidT, e_yev, e_ycev = (sem(n) for n in (
            "e_x", "e_up", "e_silu", "e_hid", "e_t", "e_hidT", "e_yev", "e_ycev"))
        c_ready, c_read = sem("c_ready"), sem("c_read")
        out_st = sem("out_stored")

        block = ctx.enter_context(nc.Block())

        def apart(eng):
            eng.sem_inc(waited, 1)

        def end_phase(eng, l, n):
            eng.drain().then_inc(phase, 1)
            eng.wait_ge(phase, l * (4 * PHASES) + 4 * (n + 1))
            apart(eng)

        def tok(b):
            return ps[:, 2 * b:2 * b + 2, :].rearrange("p a n -> p (a n)")[:, 384:1024]

        def tokh(b):
            return ps[:, 2 * b:2 * b + 2, :].rearrange("p a n -> p (a n)")[:, 192:832]

        def w2(u, kc, part):
            return W2[:, u % 2, part, :].rearrange("p (k n) -> p k n", k=kc)

        def half_item(u):
            p = P_HY + u // 2
            w = ring[:, p % SLOT, :]
            if P_QKV <= p < P_GATE:
                return p, w[:, 1024 * (u % 2):1024 * (u % 2) + 1024]
            kc = 4 if P_BR <= p < P_WO else KC
            n = 1024 // kc
            return p, w.rearrange("p (k n) -> p k n", k=kc)[:, :, n * (u % 2):n * (u % 2) + n]

        def half_dst(u, part):
            p = P_HY + u // 2
            if P_QKV <= p < P_GATE:
                return W2[:, u % 2, part, :]
            return w2(u, 4 if P_BR <= p < P_WO else KC, part)

        def wait_half_used(eng, l, u):
            if u < UNITS1:
                eng.wait_ge(chunk_ready, l * CHUNKS + half_chunk(u))
            elif u < UNITS1 + 2 * N_BR:
                eng.wait_ge(br_ready, l * 24 + 2 * (u - UNITS1) + 2)
            else:
                eng.wait_ge(wo_ready, l * 8 + u - UNITS1 - 2 * N_BR + 1)

        def freed_by(c):
            def kind(x):
                return "act" if x < 12 or (x - 12) % 6 < 2 or x >= 24 else "dve"
            me = kind(c)
            return me, sum(kind(x) == me for x in range(c + 1))

        A_FREED = 12 + 4 + 9

        def wait_chunk_freed(eng, l, c):
            who, n = freed_by(c)
            if who == "act":
                eng.wait_ge(act_freed, l * A_FREED + n)
            else:
                eng.wait_ge(dve_freed, l * 8 + n)

        UNITS1 = 2 * (N_HY + N_SC + N_QKV + N_GATE)
        UNITS = UNITS1 + 2 * (N_BR + N_WO)
        CHUNKS = 24 + 4 * N_QKV + 24

        def half_chunk(u):
            if u < 24:
                return u + 1
            if u < 24 + 2 * N_QKV:
                return 24 + 4 * ((u - 24) // 2) + (4 if u % 2 else 1)
            return u - 2 * N_QKV + 4 * N_QKV + 1

        def wait_chunk(eng, l, c):
            n = c + 1 if c < 24 else 24 + 4 * ((c - 24) // 3) + 2 + (c - 24) % 3
            eng.wait_ge(chunk_ready, l * CHUNKS + n)

        @block.sync
        def _(sp):
            for s in range(SLOT):
                sp.dma_start(ring[:, s, :], a["stream"][s]).then_inc(landed[s], 16)
            with sp.Fori(1, LAPS * DEPTH) as lap:
                for s in range(SLOT):
                    sp.wait_ge(item_used, lap * SLOT + (s + 1 - SLOT))
                    sp.dma_start(ring[:, s, :], a["stream"][lap * SLOT + s]).then_inc(landed[s], 16)

        @block.gpsimd
        def _(pool):
            pairs = [(X, "x"), (ident, "ident"), (onesm, "onesm"), (ones1, "ones1"), (utri, "utri"), (sel, "sel"),
                     (tneg, "tneg"), (rope, "rope"), (iota, "iota"), (csi, "csi"), (cfi, "cfi"),
                     (cond, "cond")]
            for dst, name in pairs:
                pool.dma_start(dst[:], a[name]).then_inc(consts, 16)
            for i in range(2):
                pool.drain().then_inc(sg_free, 1)
            with pool.Fori(0, DEPTH) as l:
                for dst, src in ((vec[:], a["vec"][l]), (fw[:], a["fw"][l]), (dec, a["decay"][l]),
                                 (rw[:], a["router"][l]), (qkw[:], a["qkw"][l]), (fbias, a["fbias"][l]), (zfeat, a["zfeat"])):
                    pool.dma_start(dst, src).then_inc(lay, 16)
                for n in range(20):
                    pool.wait_ge(k_evac, l * 20 + n + 1)
                    apart(pool)
                    pool.dma_start(a["kspec"][n // 10, (n % 10) // 2, n % 2],
                                   kout[:, n % 4, :]).then_inc(k_stored[n % 4], 16)
                for i in range(4):
                    pool.wait_ge(k_stored[i], l * 80 + 80)
                    apart(pool)
                end_phase(pool, l, 0)
                with pool.Fori(0, 12) as g:
                    for i in range(2):
                        pool.wait_ge(sg_ready, l * 24 + g * 2 + (i + 5))
                        apart(pool)
                        pool.dma_start(a["gates"][g * 2 + i], sgb[:, i, :]).then_inc(sg_stored[i], 16)
                        pool.wait_ge(sg_stored[i], l * 192 + g * 16 + 16)
                        apart(pool)
                        pool.drain().then_inc(sg_free, 1)
                pool.wait_ge(prep_done, l + 1)
                apart(pool)
                pool.dma_start(a["new_k"][l], qkv[:, 0, NQ * HD:QK]).then_inc(cache_st, 16)
                pool.dma_start(a["new_v"][l], qkv[:, 0, QK:QKV]).then_inc(cache_st, 16)
                pool.wait_ge(cache_st, l * 32 + 32)
                apart(pool)
                end_phase(pool, l, 1)
                pool.dma_start(kT[:, P:P + PAST], a["ctx_k"][l]).then_inc(a_ctx, 16)
                pool.dma_start(ctxv, a["ctx_v"][l]).then_inc(a_ctx, 16)
                end_phase(pool, l, 2)
                pool.dma_start(CS, a["cs"]).then_inc(cs_loaded, 16)
                for o in range(2):
                    if o:
                        pool.wait_ge(y_mul, l * 10 + 5)
                        apart(pool)
                    pool.dma_start(Kb, a["kspec"][o].rearrange("c r p n -> p c r n")).then_inc(k_loaded, 16)
                end_phase(pool, l, 3)
                for n in range(24):
                    half, br, m = n // 12, n % 12 // 4, n % 4
                    if n >= 4:
                        pool.wait_ge(br_read, l * 24 + n - 3)
                        apart(pool)
                    pool.dma_start(sgin[:, n % 4, :], a["gates"][8 * br + 4 * half + m]).then_inc(sg_in[n % 4], 16)
                for i in range(4, PHASES):
                    if i == 7:
                        pool.memset(yc, 0.0).then_inc(g_zero, 1)
                    end_phase(pool, l, i)
            pool.dma_start(a["y"], X[:]).then_inc(out_st, 16)
            pool.wait_ge(out_st, 16)
            apart(pool)

        @block.tensor
        def _(pe):
            def item(l, p, j=0):
                pe.wait_ge(landed[p % SLOT], l * (16 * LAPS) + j * 16 + 16 * (p // SLOT + 1))
                return ring[:, p % SLOT, :]

            def passes(n):
                for k in range(n):
                    for wp, hp in ((0, 0), (0, 1), (1, 0)):
                        yield k, wp, hp, k == 0 and wp + hp == 0, k == n - 1 and wp == 1

            def chunk(b, w, src, n, wait=None):
                for k, wp, hp, first, last in passes(n):
                    if wait and wp + hp == 0:
                        wait(k)
                    for c0, c1 in HALVES:
                        mm = pe.matmul(tokh(b)[:, c0:c1], w(wp)[:, k, :], src(hp, k)[:, c0:c1], start=first, stop=last)
                return mm

            def half_ready(l, u):
                pe.wait_ge(w_lo, l * UNITS + u + 1)
                if u % 2:
                    pe.sem_inc(item_used, 1)

            def mean_square(l, src, n):
                for k in range(KC):
                    pe.wait_ge(s_sq, l * 16 + 8 * n + k + 1)
                    for c0, c1 in HALVES:
                        mm = pe.matmul(tokh(0)[:, c0:c1], onesm[:], src[:, k, c0:c1], start=k == 0, stop=k == KC - 1)
                mm.then_inc(s_ms, 1)

            pe.wait_ge(consts, N_CONSTS)
            pe.wait_ge(s_cs, 1)
            for _ in range(2):
                pe.drain().then_inc(a_pv, 1)
            with pe.Fori(0, DEPTH) as l:
                with pe.Fori(0, N_MOD // SLOT) as it:
                    def turn(s):
                        pe.wait_ge(modrow_sb, l * N_MOD + it * SLOT + (s + 1 + SLOT))
                        pe.wait_ge(modcol_read, l * N_MOD + it * SLOT + (s + 1))
                        for c in range(2):
                            mm = pe.matmul(ps[:, 4 + s, 2 * c:2 * c + 2], mrow[:, s, P * c:P * c + P], sel[:],
                                           start=True, stop=True)
                        mm.then_inc(modcol_ready, 1)

                    for s in range(SLOT):
                        w = item(l, s, it).rearrange("p (k n) -> p k n", k=KC)
                        pe.wait_ge(modrow_sb, l * N_MOD + it * SLOT + (s + 1))
                        for k in range(KC):
                            j = k % 4
                            mm = pe.matmul(ps[32 * j:32 * j + 32, s, 0:256], cs[:, k, :], w[:, k, :],
                                           start=k < 4, stop=k >= 4)
                        mm.then_inc(item_used, 1)
                        if s:
                            turn(s - 1)
                    turn(SLOT - 1)
                pe.wait_ge(lay, l * 112 + 112)
                for n, (w, src) in enumerate(((fw[0:POS, 0:FH], zfeat), (fw[:, FH:2 * FH], fh1))):
                    if n:
                        pe.wait_ge(f_sin, l * 2 + 1)
                    else:
                        pe.wait_ge(modrow_sb, l * N_MOD + N_MOD + SLOT)
                        pe.wait_ge(modcol_read, l * N_MOD + N_MOD + SLOT)
                    apart(pe)
                    for c0, c1 in HALVES:
                        mm = pe.matmul(tokh(0)[0:FH, c0:c1], w, src[:, c0:c1], start=True, stop=True)
                    mm.then_inc(f_mm, 1)
                pe.wait_ge(f_sin, l * 2 + 2)
                pe.wait_ge(f_ones, l + 1)
                w3 = item(l, P_FILT)
                for n in range(2 * NT):
                    t, o = n // 2, n % 2
                    if n >= 2:
                        pe.wait_ge(f_tapsread, l * 10 + n - 1)
                    for d in range(2):
                        mm = pe.matmul(ps[:, 2 + 2 * (n % 2) + d, :], fh2[:, P * t:P * t + P],
                                       w3[0:FH + 1, DH * (2 * d + o):DH * (2 * d + o + 1)], start=True, stop=True)
                    mm.then_inc(item_used if n == 2 * NT - 1 else f_taps, 1)
                cf = [item(l, P_FILT + 1 + r).rearrange("p (t k) -> p t k", t=4) for r in range(2)]
                pe.wait_ge(f_tapsread, l * 10 + 10)
                for n in range(20):
                    o, kc, r = n // 10, n % 10 // 2, n % 2
                    src = (fa, fb)[r]
                    if n >= 2:
                        pe.wait_ge(k_evac, l * 20 + n - 1)
                    if kc == 0:
                        mm = pe.matmul(ps[:, n % 2, :], cfi[:, r, :], src[:, 0, o, :], start=True, stop=True)
                    for t in range(4 if kc else 0):
                        mm = pe.matmul(ps[:, n % 2, :], cf[r][:, t, P * (kc - 1):P * kc], src[:, 1 + t, o, :],
                                       start=t == 0, stop=t == 3)
                    mm.then_inc(item_used if n >= 18 else k_ready, 1)
                end_phase(pe, l, 0)

                mean_square(l, sq, 0)
                pe.wait_ge(s_rt, l * 2 + 1)

                def h_part(part, k):
                    return (h_hi, h_lo)[part][:, k, :]

                def transposes(c):
                    pe.wait_ge(conv_done, l * 12 + c + 1)
                    if c:
                        pe.wait_ge(tr_evac, l * 8 + c)
                    for t in range(NT):
                        x0 = P * t + (t > 0)
                        mm = pe.transpose(ps[:, 6 + t // 4, P * (t % 4):P * (t % 4) + P], cv[:, c % 2, x0:x0 + P],
                                          ident[:])
                    mm.then_inc(tr_ready, 1)

                for c in range(24):
                    half_ready(l, c)
                    if c >= 3:
                        wait_chunk_freed(pe, l, c - 3)
                    wait = (lambda k: pe.wait_ge(x_lo, l * OP + k + 1)) if c == 0 else None
                    chunk(c % 3, lambda part: w2(c, KC, part), h_part, KC, wait).then_inc(chunk_ready, 1)
                    if 1 <= c <= 8:
                        transposes(c - 1)
                for i in range(3):
                    for hf in range(2):
                        half_ready(l, 24 + 2 * i + hf)
                        for u in range(3):
                            n = 24 + 3 * i + u
                            if hf == 0:
                                wait_chunk_freed(pe, l, n - 3)
                            for t in range(2 * u, min(2 * u + 2, NT)):
                                for k, wp, hp, first, last in passes(4):
                                    mm = pe.matmul(ps[:, 2 * (n % 3) + t % 2, 0:256],
                                                   h_part(hp, 4 * hf + k)[:, P * t:P * t + P],
                                                   w2(hf, 4, wp)[:, k, :], start=first and hf == 0, stop=last and hf == 1)
                            if hf or u == 2:
                                mm.then_inc(chunk_ready, 1)
                wait_chunk_freed(pe, l, 32)
                pe.wait_ge(tr_evac, l * 8 + 8)
                apart(pe)
                with pe.Fori(0, 6) as it:
                    for n in range(4):
                        u = 30 + n
                        pe.wait_ge(w_lo, l * UNITS + it * 4 + (u + 1))
                        if n % 2:
                            pe.sem_inc(item_used, 1)
                        pe.wait_ge(sg_ready, l * 24 + it * 4 + (n + 1))
                        chunk(n, lambda part: w2(n, KC, part), h_part, KC).then_inc(chunk_ready, 1)
                end_phase(pe, l, 1)

                for t in range(NT):
                    if t >= 2:
                        pe.wait_ge(a_trev, l * 6 + t - 1)
                    for j in range(4):
                        mm = pe.transpose(ps[:, t % 2, P * j:P * j + P], qkv[:, t, P * j:P * j + P], ident[:])
                    mm.then_inc(a_tr, 1)
                for t in range(NT):
                    mm = pe.transpose(ps[:, 2 + (t + 3) // 4, P * ((t + 3) % 4):P * ((t + 3) % 4) + P],
                                      qkv[:, t, NQ * HD:QK], ident[:])
                mm.then_inc(a_tr, 1)
                pe.wait_ge(a_trev, l * 6 + 6)
                pe.wait_ge(a_ctx, l * 32 + 32)
                apart(pe)
                def scores(j, u):
                    g, t = u // 5, u % 5
                    if t == 0:
                        pe.wait_ge(a_qj, l * 8 + j * 2 + (g + 1))
                    pe.wait_ge(a_exp, l * 40 + j * 10 + (u + 1))
                    apart(pe)
                    q = qj[HD * g:HD * g + HD, P * t:P * t + P]
                    kk = kT[HD * g:HD * g + HD, :]
                    b = 2 * (u % 2)
                    if t == 0:
                        mm = pe.matmul(ps[:, b, 0:P], q, kk[:, 0:P], start=True, stop=True)
                    else:
                        pe.matmul(ps[:, b, 0:512], q, kk[:, P:P + 512], start=True, stop=True)
                        mm = pe.matmul(ps[:, b + 1, 0:P], q, kk[:, P + 512:P + 640], start=True, stop=True)
                    mm.then_inc(a_s, 1)

                def turn_p(j, u):
                    t = u % 5
                    pe.wait_ge(a_norm, l * 40 + j * 10 + (u + 1))
                    pe.wait_ge(a_ptev, l * 40 + j * 10 + (u + 1))
                    for kt in range(1 if t == 0 else NT):
                        mm = pe.transpose(ps[:, 4 + kt // 4, P * (kt % 4):P * (kt % 4) + P],
                                          Pb[:, u % 2, P * kt:P * kt + P], ident[:])
                    mm.then_inc(a_pt, 1)

                def values(j, g, kt):
                    vc = slice(QK + HD * g, QK + HD * g + HD)
                    o = slice(HD * g, HD * g + HD)
                    if kt == 0:
                        pe.wait_ge(a_ptev, l * 40 + j * 10 + (5 * g + 6))
                        if g == 0:
                            pe.wait_ge(a_pvev, l * 4 + j + 1)
                            apart(pe)
                        pe.matmul(ps[o, 6, 0:P], qkv[:, 0, vc], PTi[:, g, :], start=True, stop=True)
                    v = ctxv[:, HD * g:HD * g + HD] if kt == 0 else qkv[:, kt, vc]
                    mm = pe.matmul(ps[o, 7, :], v, PT[:, g, kt, :], start=kt == 0, stop=kt == NT - 1)
                    if kt == NT - 1:
                        mm.then_inc(a_pv, 1)

                def heads(j, first, last):
                    for u in range(10):
                        turn_p(j, u)
                        if u + 2 < 10:
                            scores(j, u + 2)
                        elif not last:
                            scores(j + 1, u - 8)
                        if u >= 5:
                            values(j, 0, u - 5)
                        elif not first:
                            values(j - 1, 1, u)

                scores(0, 0)
                scores(0, 1)
                heads(0, True, False)
                with pe.Fori(1, 3) as j:
                    heads(j, False, False)
                heads(3, False, True)
                for kt in range(NT):
                    values(3, 1, kt)
                end_phase(pe, l, 2)

                pe.wait_ge(cs_loaded, l * 16 + 16)
                for o in range(2):
                    if o:
                        pe.wait_ge(y_out, l * 9 + 5)
                    for kc in range(NT):
                        n = 5 * o + kc
                        if kc >= 4:
                            pe.wait_ge(y_mul, l * 10 + n - 3)
                        for r in range(2):
                            bank = 2 * (kc % 4) + r
                            if kc == 0:
                                mm = pe.matmul(ps[:, bank, :], csi[:, r, :], u_tm[:, 0, :], start=True, stop=True)
                            for t in range(4 if kc else 0):
                                mm = pe.matmul(ps[:, bank, :], CS[:, r, t, P * (kc - 1):P * kc], u_tm[:, 1 + t, :],
                                               start=t == 0, stop=t == 3)
                        mm.then_inc(y_fwd, 1)
                    pe.wait_ge(y_mul, l * 10 + 5 * o + 5)
                    for m in range(NT - o):
                        n = 5 * o + m
                        if m >= 2:
                            pe.wait_ge(y_out, l * 9 + n - 1)
                        b = 2 * (m % 2)
                        if o == 0 and m == 0:
                            for r in range(2):
                                mm = pe.matmul(ps[:, b, :], csi[:, r, :], Yb[:, 0, r, :], start=r == 0, stop=r == 1)
                        elif o == 0:
                            for kc in range(4):
                                for r in range(2):
                                    mm = pe.matmul(ps[:, b, :], CS[:, r, kc, P * (m - 1):P * m], Yb[:, 1 + kc, r, :],
                                                   start=kc + r == 0, stop=kc + r == 4)
                        else:
                            tb = tok(m % 2)
                            for r in range(2):
                                pe.matmul(tb[:, 0:LI], Yb[:, 0, r, P * m:P * m + P], csi[:, r, :], start=r == 0,
                                          stop=r == 1)
                            for kc in range(4):
                                for r in range(2):
                                    mm = pe.matmul(tb[:, LI:T], Yb[:, 1 + kc, r, P * m:P * m + P], CS[:, r, kc, :],
                                                   start=kc + r == 0, stop=kc + r == 4)
                        mm.then_inc(y_inv, 1)
                end_phase(pe, l, 3)

                for n in range(24):
                    half, br, m = n // 12, n % 12 // 4, n % 4
                    if n % 2 == 0:
                        half_ready(l, UNITS1 + n // 2)
                    if n >= 4:
                        pe.wait_ge(br_read, l * 24 + n - 3)
                    wait = (lambda k: pe.wait_ge(x_lo, l * OP + OP_Y + 4 * br + k + 1)) if n in (0, 4, 8) else None
                    chunk(n % 4, lambda part: w2(n // 2, 4, part)[:, :, P * (m % 2):P * (m % 2) + P],
                          lambda part, k: (Y_hi, Y_lo)[part][:, br, k, :], 4, wait).then_inc(br_ready, 1)
                pe.wait_ge(br_read, l * 24 + 24)
                for c in range(KC):
                    half_ready(l, UNITS1 + 2 * N_BR + c)
                    if c >= 4:
                        pe.wait_ge(wo_read, l * 8 + c - 3)
                    wait = (lambda k: pe.wait_ge(x_lo, l * OP + OP_M + k + 1)) if c == 0 else None
                    chunk(c % 4, lambda part: w2(c, KC, part),
                          lambda part, k: m_lo[:, k, :] if part else m_hi[k // 4][:, k % 4, :], KC, wait)\
                        .then_inc(wo_ready, 1)
                end_phase(pe, l, 4)

                mean_square(l, sq2, 1)
                end_phase(pe, l, 5)

                for t in range(NT):
                    for k in range(KC):
                        mm = pe.matmul(ps[:, 0, NE * t:NE * t + NE], h[:, k, P * t:P * t + P], rw[:, k, :],
                                       start=k == 0, stop=k == KC - 1)
                mm.then_inc(r_lg, 1)
                for n in range(2 * NT):
                    t, hf = n // 2, n % 2
                    if n >= 2:
                        pe.wait_ge(t_evac, l * 19 + n - 1)
                    for i in range(4):
                        mm = pe.transpose(ps[:, 4 + n % 2, P * i:P * i + P], h[:, 4 * hf + i, P * t:P * t + P],
                                          ident[:])
                    mm.then_inc(t_ready, 1)
                pe.wait_ge(r_aff, l + 1)
                for t in range(NT):
                    mm = pe.transpose(tok(1)[0:NE, P * t:P * t + P], aff[:, t, :], ident[:])
                mm.then_inc(r_affT, 1)
                pe.wait_ge(r_mask, l + 1)
                apart(pe)
                for t in range(NT):
                    mm = pe.transpose(ps[:, 0, NE * t:NE * t + NE], mask[:, P * t:P * t + P], ident[0:NE, 0:NE])
                mm.then_inc(r_maskT, 1)
                pe.wait_ge(r_mt, l + 1)
                for t in range(NT):
                    pe.matmul(ps[:, 1, NE * t:NE * t + NE], utri[:], maskT[:, t, :], start=True, stop=t <= 1)
                    for s in range(1, t):
                        mm = pe.matmul(ps[:, 1, NE * t:NE * t + NE], ones1[:], maskT[:, s, :], start=False,
                                       stop=s == t - 1)
                mm.then_inc(r_pos, 1)
                pe.wait_ge(r_P, l + 1)
                pe.wait_ge(t_evac, l * 19 + 10)
                for n in range(3 * KC):
                    k, part = n // 3, n % 3
                    if n >= 4:
                        pe.wait_ge(g_evac, l * 25 + n - 3)
                    bank = ps[:, n % 4, :]
                    if part < 2:
                        for t in range(4):
                            mm = pe.matmul(bank, h2_tm[:, 1 + t, P * k:P * k + P], Ps[:, t, 512 * part:512 * part + 512],
                                           start=t == 0, stop=t == 3)
                    else:
                        mm = pe.matmul(bank[:, 0:256], h2_tm[:, 0, P * k:P * k + P], Pi[:, :, 0:CAP[0]],
                                       start=True, stop=True)
                    mm.then_inc(g_ready, 1)
                pe.wait_ge(g_evac, l * 25 + 21)
                for e in range(NE):
                    for t in range(4):
                        pe.matmul(ps[0:CAP[1], 0, e:e + 1], Ps[:, t, HD * e:HD * e + HD], aff[:, 1 + t, e:e + 1],
                                  start=t == 0, stop=t == 3)
                    mm = pe.matmul(ps[CAP[1]:SLOTS, 0, e:e + 1], Pi[:, e, 0:CAP[0]], aff[:, 0, e:e + 1],
                                   start=True, stop=True)
                mm.then_inc(g_ready, 1)
                for n in range(8):
                    pe.wait_ge(t_evac, l * 19 + 10 + max(n - 1, 0))
                    for t in range(4):
                        mm = pe.transpose(ps[:, 4 + n % 2, P * t:P * t + P], Ps[:, t, P * n:P * n + P], ident[:])
                    mm.then_inc(t_ready, 1)
                for g in range(4):
                    mm = pe.transpose(ps[:, 6, P * g:P * g + P],
                                      Pi[:, 4 * g:4 * g + 4, :].rearrange("p e s -> p (e s)"), ident[:])
                mm.then_inc(t_ready, 1)
                end_phase(pe, l, 6)

                with pe.Fori(0, NE // 4) as b:
                    for ee in range(4):
                        p0 = P_EXP + 6 * ee

                        def w_in_item(i):
                            return item(l, p0 + i, b * 6).rearrange("p (k n) -> p k n", k=KC)

                        x = xe[:, ee % 2]
                        pe.wait_ge(e_x, l * NE + b * 4 + ee + 1)
                        def up(hf, which):
                            w = w_in_item(2 * hf + which)
                            for k in range(KC):
                                mm = pe.matmul(ps[0:SLOTS, 2 * hf + which, 0:256], x[:, k, :], w[:, k, :],
                                               start=k == 0, stop=k == KC - 1)
                            mm.then_inc(item_used, 1)

                        def turn_hidden(hf):
                            pe.wait_ge(e_hid, l * 2 * NE + b * 8 + 2 * ee + hf + 1)
                            for i in range(2):
                                mm = pe.transpose(ps[:, 4 + hf, SLOTS * i:SLOTS * i + SLOTS],
                                                  hid[:, ee % 2, P * (2 * hf + i):P * (2 * hf + i) + P],
                                                  ident[0:SLOTS, 0:SLOTS])
                            mm.then_inc(e_t, 1)

                        def down(c, hf):
                            for k in range(2 * hf, 2 * hf + 2):
                                mm = pe.matmul(ps[0:SLOTS, 6 + c, :], hidT[:, ee % 2, k, :], wd[c][:, k, :],
                                               start=k == 0, stop=k == 3)
                            return mm

                        up(0, 0)
                        up(0, 1)
                        up(1, 0)
                        turn_hidden(0)
                        up(1, 1)
                        wd = [item(l, p0 + 4 + i, b * 6).rearrange("p (k n) -> p k n", k=4) for i in range(2)]
                        pe.wait_ge(e_hidT, l * 2 * NE + b * 8 + 2 * ee + 1)
                        pe.wait_ge(e_yev, l * NE + b * 4 + ee + 1)
                        pe.wait_ge(e_ycev, l * NE + b * 4 + ee + 1)
                        down(0, 0)
                        turn_hidden(1)
                        down(1, 0)
                        pe.wait_ge(e_hidT, l * 2 * NE + b * 8 + 2 * ee + 2)
                        down(0, 1).then_inc(item_used, 1)
                        down(1, 1).then_inc(item_used, 1)
                end_phase(pe, l, 7)

                for m in range(KC):
                    if m >= 4:
                        pe.wait_ge(c_read, l * 8 + m - 3)
                    tb = tok(m % 4)
                    for g in range(4):
                        pe.matmul(tb[:, 0:LI], yc[:, g, P * m:P * m + P], PTc[:, g, :], start=g == 0, stop=g == 3)
                    for n in range(8):
                        mm = pe.matmul(tb[:, LI:T], ys[:, n, P * m:P * m + P], PTs[:, n, :], start=n == 0, stop=n == 7)
                    mm.then_inc(c_ready, 1)
                end_phase(pe, l, 8)

        @block.scalar
        def _(act):
            def copy(o, i):
                return act.activation(o, i, ACT.Copy)

            def split(l, u):
                p, src = half_item(u)
                wait_half_used(act, l, u - 2)
                act.wait_ge(landed[p % SLOT], l * (16 * LAPS) + 16 * (p // SLOT + 1))
                copy(half_dst(u, 0), src).then_inc(w_hi, 1)

            def split_first(l, u):
                p, src = half_item(u)
                act.wait_ge(landed[p % SLOT], l * (16 * LAPS) + 16 * (p // SLOT + 1))
                copy(half_dst(u, 0), src).then_inc(w_hi, 1)

            def norm(l, n, squares, root, dst):
                for k in range(KC):
                    act.activation(squares[:, k, :], X[:, k, :], ACT.Square).then_inc(s_sq, 1)
                if n == 0:
                    split_first(l, 0)
                    split_first(l, 1)
                act.wait_ge(s_ms, l * 2 + n + 1)
                act.activation(root, tokh(0), ACT.Sqrt, bias=eps[:, 0:1]).then_inc(s_rt, 1)
                for k in range(KC):
                    act.wait_ge(s_xn, l * 16 + 8 * n + k + 1)
                    for g, c0, c1 in GROUPS:
                        x = dst[:, k, c0:c1] if n else h_x[:, k, c0:c1]
                        ins = act.activation(dst[:, k, c0:c1], x, ACT.Identity, bias=mod[:, 24 * n + k, g:g + 1])
                    ins.then_inc(s_h if n else x_hi, 1)

            act.wait_ge(consts, N_CONSTS)
            act.wait_ge(s_csz, 1)
            act.activation(cs[:, :, 0:2], cond[:], ACT.Silu).then_inc(s_cs, 1)
            for _ in range(SLOT):
                act.drain().then_inc(modrow_sb, 1)
                act.drain().then_inc(sg_ready, 1)
            act.drain().then_inc(e_ycev, 1)
            for _ in range(2):
                act.drain().then_inc(a_exp, 1)
            act.drain().then_inc(a_ptev, 1)
            act.drain().then_inc(a_pvev, 1)
            with act.Fori(0, DEPTH) as l:
                with act.Fori(0, N_MOD // SLOT) as it:
                    for s in range(SLOT):
                        act.wait_ge(item_used, l * ITEMS + it * SLOT + (s + 1))
                        act.wait_ge(modcol_read, l * N_MOD + it * SLOT + (s + 1))
                        copy(mrow[:, s, :], ps[:, s, 0:256]).then_inc(modrow_sb, 1)
                for n, dst in enumerate((fh1, fh2)):
                    act.wait_ge(f_arg, l * 2 + n + 1)
                    act.activation(dst[0:FH, :], farg, ACT.Sin).then_inc(f_sin, 1)
                act.wait_ge(f_dec, l + 1)
                for t in range(NT):
                    if t:
                        act.wait_ge(f_tapsread, l * 10 + 2 * t)
                    act.activation(win, dec, ACT.Exp, scale=tneg[:, t:t + 1]).then_inc(f_win, 1)
                for n in range(20):
                    if n >= 18:
                        act.wait_ge(item_used, l * ITEMS + P_FILT + 1 + n - 17)
                    else:
                        act.wait_ge(k_ready, l * 18 + n + 1)
                    if n >= 4:
                        act.wait_ge(k_stored[n % 4], l * 80 + 16 * (n // 4))
                    copy(kout[:, n % 4, :], ps[:, n % 2, :]).then_inc(k_evac, 1)
                end_phase(act, l, 0)
                norm(l, 0, sq, rstd, h_hi)
                act.wait_ge(pads, l + 1)

                def evac_tr(c):
                    act.wait_ge(tr_ready, l * 8 + c + 1)
                    dst = (u_tm, x1_tm)[c // 4][:, :, P * (c % 4):P * (c % 4) + P]
                    src = ps[:, 6:8, :].rearrange("p a n -> p (a n)")[:, 0:T].rearrange("p (t n) -> p t n", t=NT)
                    copy(dst, src).then_inc(tr_evac, 1)

                for c in range(24):
                    if freed_by(c)[0] == "act":
                        wait_chunk(act, l, c)
                        if c < 12:
                            if c >= 2:
                                act.wait_ge(conv_done, l * 12 + c - 1)
                            copy(raw[:, c % 2, 1:1 + LI], tokh(c % 3)[:, 0:LI])
                            copy(raw[:, c % 2, 2 + LI:2 + T], tokh(c % 3)[:, LI:T]).then_inc(act_freed, 1)
                        else:
                            if c >= 18:
                                act.wait_ge(dve_freed, l * 8 + c % 2 + 1)
                            copy(ubuf[:, c % 2, :], tokh(c % 3)).then_inc(act_freed, 1)
                    split(l, c + 2)
                    if 2 <= c <= 9:
                        evac_tr(c - 2)
                for n in range(9):
                    i, u = n // 3, n % 3
                    if u == 0:
                        split(l, 26 + 2 * i)
                    wait_chunk(act, l, 24 + n)
                    t1 = min(2 * u + 2, NT)
                    b = 2 * ((24 + n) % 3)
                    copy(qkv[:, 2 * u:t1, 256 * i:256 * i + 256], ps[:, b:b + t1 - 2 * u, 0:256]).then_inc(act_freed, 1)
                    if u == 2:
                        split(l, 27 + 2 * i)
                act.wait_ge(qs_ready, l + 1)
                act.activation(st5[:], st5[:], ACT.Sqrt, bias=eps[:, 0:1], scale=1.0 / HD).then_inc(qrt, 1)
                def gates(n, it):
                    act.wait_ge(chunk_ready, l * CHUNKS + it * 8 + (24 + 4 * N_QKV + n + 1))
                    act.wait_ge(sg_free, l * 24 + it * 8 + (n + 1))
                    act.activation(sgb[:, n % 2, :], tokh(n % 4), ACT.Sigmoid).then_inc(sg_ready, 1)

                def turn(it, last):
                    for n in range(8):
                        gates(n, it)
                        if last and n >= 6:
                            continue
                        p, src = half_item(32 + n)
                        act.wait_ge(landed[p % SLOT], l * (16 * LAPS) + it * 16 + 16 * (p // SLOT + 1))
                        copy(w2(n, KC, 0), src).then_inc(w_hi, 1)

                with act.Fori(0, 2) as it:
                    turn(it, False)
                turn(2, True)
                end_phase(act, l, 1)
                for t in range(NT):
                    act.wait_ge(a_tr, l * 6 + t + 1)
                    act.activation(qT[:, :, P * t:P * t + P], ps[:, t % 2, :].rearrange("p (j n) -> p j n", j=4),
                                   ACT.Copy, scale=QSCALE).then_inc(a_trev, 1)
                act.wait_ge(a_tr, l * 6 + 6)
                copy(kT[:, 0:P], tok(1)[:, 0:LI])
                copy(kT[:, P + PAST:], tok(1)[:, LI:T]).then_inc(a_trev, 1)
                def exp(j, u):
                    t = u % 5
                    n = P if t == 0 else T
                    act.wait_ge(a_max, l * 40 + j * 10 + (u + 1))
                    src = ps[:, 2 * (u % 2):2 * (u % 2) + 2, :].rearrange("p a n -> p (a n)")[:, 0:n]
                    act.activation(Pb[:, u % 2, 0:n], src, ACT.Exp, bias=nb[:, u % 2:u % 2 + 1],
                                   accum_out=rsum[:, u % 2:u % 2 + 1]).then_inc(a_exp, 1)

                def evac_pt(j, u):
                    g, t = u // 5, u % 5
                    act.wait_ge(a_pt, l * 40 + j * 10 + (u + 1))
                    act.wait_ge(a_pv, l * 8 + j * 2 + (g + 1))
                    flat = ps[:, 4:6, :].rearrange("p a n -> p (a n)")
                    if t == 0:
                        copy(PTi[:, g, :], flat[:, 0:P]).then_inc(a_ptev, 1)
                    else:
                        copy(PT[:, g, :, P * (t - 1):P * t],
                             flat[:, 0:T].rearrange("p (k n) -> p k n", k=NT)).then_inc(a_ptev, 1)

                def evac_values(j):
                    act.wait_ge(a_pv, l * 8 + j * 2 + 4)
                    copy(Y3[:, 1, j, 0:LI], ps[:, 6, 0:LI])
                    copy(Y3[:, 1, j, LI:T], ps[:, 7, :]).then_inc(a_pvev, 1)

                def heads(j, first, last):
                    for u in range(10):
                        evac_pt(j, u)
                        if u == 5 and not first:
                            evac_values(j - 1)
                        if u + 2 < 10:
                            exp(j, u + 2)
                        elif not last:
                            exp(j + 1, u - 8)

                exp(0, 0)
                exp(0, 1)
                heads(0, True, False)
                with act.Fori(1, 3) as j:
                    heads(j, False, False)
                heads(3, False, True)
                evac_values(3)
                end_phase(act, l, 2)
                end_phase(act, l, 3)
                def merged_hi(c):
                    act.wait_ge(br_read, l * 24 + (21 + c - 4 if c >= 4 else 9 + c))
                    copy(m_hi[c // 4][:, c % 4, :], merged[:, c, :]).then_inc(x_hi, 1)

                for br in range(3):
                    if br < 2:
                        split_first(l, UNITS1 + br)
                    for k in range(4):
                        copy(Y_hi[:, br, k, :], Y3[:, br, k, :]).then_inc(x_hi, 1)
                for u in range(UNITS1 + 2, UNITS):
                    split(l, u)
                    if u == UNITS1 + 7:
                        for c in range(4):
                            merged_hi(c)
                    if u == UNITS1 + 2 * N_BR + 1:
                        for c in range(4, KC):
                            merged_hi(c)
                end_phase(act, l, 4)
                norm(l, 1, sq2, rstd2, h)
                end_phase(act, l, 5)

                def evac_t(n):
                    act.wait_ge(t_ready, l * 19 + n + 1)
                    copy(h2_tm[:, n // 2, 512 * (n % 2):512 * (n % 2) + 512], ps[:, 4 + n % 2, :]).then_inc(t_evac, 1)

                evac_t(0)
                evac_t(1)
                act.wait_ge(r_sub, l + 1)
                act.activation(lg, lg, ACT.Exp).then_inc(r_exp, 1)
                for n in range(2, 10):
                    evac_t(n)
                for n in range(8):
                    act.wait_ge(t_ready, l * 19 + 10 + n + 1)
                    copy(PTs[:, n, :], ps[:, 4 + n % 2, :]).then_inc(t_evac, 1)
                act.wait_ge(t_ready, l * 19 + 19)
                copy(PTc, ps[:, 6, :].rearrange("p (g n) -> p g n", g=4)).then_inc(t_evac, 1)
                end_phase(act, l, 6)

                act.wait_ge(g_zero, l + 1)
                with act.Fori(0, NE // 4) as b:
                    for ee in range(4):
                        p0 = P_EXP + 6 * ee
                        if ee == 0:
                            copy(xe[:, 0], xs[:, :, b * 4, :]).then_inc(e_x, 1)
                        for hf in range(2):
                            act.wait_ge(item_used, l * ITEMS + b * 24 + (p0 + 2 * hf + 1))
                            act.activation(sg[:, ee % 2, 256 * hf:256 * hf + 256], ps[0:SLOTS, 2 * hf, 0:256],
                                           ACT.Silu).then_inc(e_silu, 1)
                        for hf in range(2):
                            act.wait_ge(e_t, l * 2 * NE + b * 8 + (2 * ee + hf + 1))
                            copy(hidT[:, ee % 2, 2 * hf:2 * hf + 2, :],
                                 ps[:, 4 + hf, 0:2 * SLOTS].rearrange("p (k n) -> p k n", k=2)).then_inc(e_hidT, 1)
                            if hf == 0 and ee < 3:
                                copy(xe[:, (ee + 1) % 2], xs[:, :, b * 4 + (ee + 1), :]).then_inc(e_x, 1)
                        act.wait_ge(item_used, l * ITEMS + b * 24 + (p0 + 6))
                        act.activation(yc[32 * ee:32 * ee + CAP[0], b, :],
                                       ps[CAP[1]:SLOTS, 6:8, :].rearrange("p a n -> p (a n)"), ACT.Copy,
                                       scale=gt[CAP[1]:SLOTS, bass.ds(b * 4 + ee, 1)]).then_inc(e_ycev, 1)
                end_phase(act, l, 7)
                end_phase(act, l, 8)

        @block.vector
        def _(dve):
            settle = dve.drain

            def split(l, u):
                src = half_item(u)[1]
                dve.wait_ge(w_hi, l * UNITS + u + 1)
                dve.tensor_tensor(half_dst(u, 1), src, half_dst(u, 0).bitcast(F32), ALU.subtract).then_inc(w_lo, 1)

            def norm(l, n, root, dst):
                def lo(k):
                    dve.wait_ge(x_hi, l * OP + k + 1)
                    for g, c0, c1 in GROUPS:
                        ins = dve.scalar_tensor_tensor(out=h_lo[:, k, c0:c1], in0=h_x[:, k, c0:c1],
                                                       scalar=mod[:, k, g:g + 1],
                                                       in1=h_hi[:, k, c0:c1].bitcast(F32),
                                                       op0=ALU.add, op1=ALU.subtract)
                    ins.then_inc(x_lo, 1)

                dve.wait_ge(s_rt, l * 2 + n + 1)
                dve.reciprocal(root, root)
                settle()
                for k in range(KC):
                    for g, c0, c1 in GROUPS:
                        ins = dve.scalar_tensor_tensor(out=dst[:, k, c0:c1], in0=X[:, k, c0:c1],
                                                       scalar=ws[:, n, k, g:g + 1], in1=root[:, c0:c1],
                                                       op0=ALU.mult, op1=ALU.mult)
                    ins.then_inc(s_xn, 1)
                    if n == 0 and k:
                        lo(k - 1)
                if n == 0:
                    lo(KC - 1)

            def residual(src, k, gate):
                for g, c0, c1 in GROUPS:
                    ins = dve.scalar_tensor_tensor(out=X[:, k, c0:c1], in0=src[:, c0:c1],
                                                   scalar=mod[:, gate + k, g:g + 1], in1=X[:, k, c0:c1],
                                                   op0=ALU.mult, op1=ALU.add)
                return ins

            dve.memset(cs[:], 0.0)
            dve.memset(eps[:], EPS)
            settle().then_inc(s_csz, 1)
            for _ in range(SLOT):
                settle().then_inc(modcol_read, 1)
            settle().then_inc(e_yev, 1)
            dve.wait_ge(consts, N_CONSTS)
            with dve.Fori(0, DEPTH) as l:
                dve.wait_ge(lay, l * 112 + 112)
                dve.memset(fh2[FH:FH + 1, :], 1.0).then_inc(f_ones, 1)
                dve.tensor_scalar(win, dec, -1.0, None, ALU.mult)
                settle()
                dve.tensor_tensor(dec, dec, win, ALU.max).then_inc(f_dec, 1)
                with dve.Fori(0, N_MOD // SLOT) as it:
                    for s in range(SLOT):
                        dve.wait_ge(modcol_ready, l * N_MOD + it * SLOT + (s + 1))
                        n = it * (2 * SLOT) + 2 * s
                        dve.tensor_tensor(mod[:, bass.ds(n, 2), :],
                                          ps[:, 4 + s, 0:4].rearrange("p (c g) -> p c g", c=2),
                                          vec[:, bass.ds(n, 2)].unsqueeze(2).to_broadcast([P, 2, 2]),
                                          ALU.add).then_inc(modcol_read, 1)
                settle()
                for n in range(2):
                    dve.scalar_tensor_tensor(out=ws[:, n], in0=mod[:, 24 * n + 8:24 * n + 16, :], scalar=1.0,
                                             in1=vec[:, V_N1 + 8 * n:V_N1 + 8 * n + 8].unsqueeze(2)
                                             .to_broadcast([P, KC, 2]),
                                             op0=ALU.add, op1=ALU.mult)
                for n in range(2):
                    dve.wait_ge(f_mm, l * 2 + n + 1)
                    dve.tensor_scalar(farg, tokh(0)[0:FH, :], fw[:, 2 * FH + n:2 * FH + n + 1], None, ALU.add)
                    settle()
                    dve.tensor_scalar(frnd, farg, float(1 / (2 * np.pi)), ROUND, ALU.mult, ALU.add)
                    settle()
                    dve.tensor_scalar(frnd, frnd, -ROUND, None, ALU.add)
                    for part in TWO_PI:
                        settle()
                        dve.scalar_tensor_tensor(out=farg, in0=frnd, scalar=-part, in1=farg, op0=ALU.mult,
                                                 op1=ALU.add)
                    settle()
                    dve.tensor_scalar(farg, farg, -PI_IN, PI_IN, ALU.max, ALU.min).then_inc(f_arg, 1)
                for n in range(2 * NT):
                    t, o = n // 2, n % 2
                    settle()
                    dve.wait_ge(f_win, l * 5 + t + 1)
                    if n == 2 * NT - 1:
                        dve.wait_ge(item_used, l * ITEMS + P_FILT + 1)
                    else:
                        dve.wait_ge(f_taps, l * 9 + n + 1)
                    for d in range(2):
                        w0 = DH * (2 * d + o)
                        dve.scalar_tensor_tensor(out=fdir[:, d, :], in0=win[:, w0:w0 + DH], scalar=SHIFT,
                                                 in1=ps[:, 2 + 2 * (n % 2) + d, :], op0=ALU.add, op1=ALU.mult)
                    settle()
                    if t <= 1:
                        dve.memset(fdir[0:1, 1, :], 0.0)
                        settle()
                    dve.tensor_tensor(fa[:, t, o, :], fdir[:, 0, :], fdir[:, 1, :], ALU.add)
                    ins = dve.tensor_tensor(fb[:, t, o, :], fdir[:, 1, :], fdir[:, 0, :], ALU.subtract)
                    if t <= 1:
                        settle()
                        ins = dve.tensor_tensor(fa[0:1, t, o, :], fa[0:1, t, o, :], fbias[:, o, :], ALU.add)
                    ins.then_inc(f_tapsread, 1)
                end_phase(dve, l, 0)

                for b in range(2):
                    for c0 in (0, LI + 1, T + 2):
                        ins = dve.memset(raw[:, b, c0:c0 + 1], 0.0)
                ins.then_inc(pads, 1)
                split(l, 0)
                split(l, 1)
                norm(l, 0, rstd, h_x)

                def conv(dst, src, w, bias):
                    dve.tensor_scalar(dst, src(1), vec[:, w + 1:w + 2], vec[:, bias:bias + 1], ALU.mult, ALU.add)
                    for tap in (0, 2):
                        settle()
                        ins = dve.scalar_tensor_tensor(out=dst, in0=src(tap), scalar=vec[:, w + tap:w + tap + 1],
                                                       in1=dst, op0=ALU.mult, op1=ALU.add)
                    return ins

                for c in range(24):
                    b = c % 2
                    settle()
                    split(l, c + 2)
                    if c < 12:
                        before = (c // 2) * 2 + c % 2
                        dve.wait_ge(act_freed, l * A_FREED + before + 1)
                        if 2 <= c < 8 or c in (8, 9):
                            dve.wait_ge(tr_ready, l * 8 + c - 1)
                        ins = conv(cv[:, b, :], lambda i: raw[:, b, i:i + T + 1], V_HYW + 3 * c, V_HYB + c)
                        if c < 8:
                            ins.then_inc(conv_done, 1)
                        else:
                            settle()
                            dve.tensor_copy(Y3[:, 0, c - 8, 0:LI], cv[:, b, 0:LI])
                            dve.tensor_copy(Y3[:, 0, c - 8, LI:T], cv[:, b, LI + 1:T + 1]).then_inc(conv_done, 1)
                        continue
                    if freed_by(c)[0] == "act":
                        continue
                    j = 2 * ((c - 12) // 6) + b
                    settle()
                    wait_chunk(dve, l, c)
                    pieces = ((0, LI, 0), (LI, T, 1))
                    if (c - 12) % 6 < 4:
                        dve.wait_ge(act_freed, l * A_FREED + freed_by(12 + 6 * ((c - 12) // 6) + b)[1])
                        for c0, c1, x in pieces:
                            ins = dve.tensor_tensor(raw[:, b, 1 + c0 + x:1 + c1 + x], tokh(c % 3)[:, c0:c1],
                                                    ubuf[:, b, c0:c1], ALU.mult)
                        ins.then_inc(dve_freed, 1)
                        settle()
                        conv(cv[:, b, :], lambda i: raw[:, b, i:i + T + 1], V_SCW + 3 * j, V_SCB + j)
                    else:
                        for c0, c1, x in pieces:
                            ins = dve.tensor_tensor(Y3[:, 2, j, c0:c1], tokh(c % 3)[:, c0:c1],
                                                    cv[:, b, c0 + x:c1 + x], ALU.mult)
                        ins.then_inc(dve_freed, 1)
                for u in range(26, 32):
                    split(l, u)
                dve.wait_ge(act_freed, l * A_FREED + A_FREED)
                for t in range(NT):
                    qk = qkv[:, t, 0:QK]
                    dve.tensor_tensor(prep[:, t % 2, :], qk, qk, ALU.mult)
                    settle()
                    ins = dve.tensor_reduce(st5[:, t, :], prep[:, t % 2, :].rearrange("p (h d) -> p h d", h=10), AX.X,
                                            ALU.add)
                ins.then_inc(qs_ready, 1)

                def weigh(t):
                    qk = qkv[:, t, 0:QK]
                    heads = qk.rearrange("p (h d) -> p h d", h=10)
                    dve.tensor_tensor(heads, heads, rst5[:, t, :].unsqueeze(2).to_broadcast([P, 10, HD]), ALU.mult)
                    settle()
                    return dve.tensor_tensor(qk, qk, qkw[:], ALU.mult)

                def rotate(t):
                    v4 = "p (h a f i) -> p h a f i"
                    src = qkv[:, t, 0:QK]
                    dve.tensor_tensor(prep[:, t % 2, :].rearrange("p (h d) -> p h d", h=10),
                                      src.rearrange("p (h d) -> p h d", h=10),
                                      rope[:, 0, t - 1, :].unsqueeze(1).to_broadcast([P, 10, HD]), ALU.mult)
                    for f in range(2):
                        sin = rope[:, 1, t - 1, :].rearrange("p (a f i) -> p a f i", a=2, f=2)[:, :, f, :]
                        for axis in range(2):
                            dve.tensor_tensor(prep2[:, t % 2, :].rearrange(v4, h=10, a=2, f=2)[:, :, axis, f, :],
                                              src.rearrange(v4, h=10, a=2, f=2)[:, :, axis, 1 - f, :],
                                              sin[:, axis, :].unsqueeze(1).to_broadcast([P, 10, 16]), ALU.mult)
                    settle()
                    return dve.tensor_tensor(src, prep[:, t % 2, :], prep2[:, t % 2, :], ALU.add)

                for u in range(32, UNITS1):
                    split(l, u)
                    if u == 32:
                        dve.wait_ge(qrt, l + 1)
                        dve.reciprocal(rst5[:], st5[:])
                        settle()
                        for t in range(3):
                            weigh(t)
                    elif u == 33:
                        for t in range(3, NT):
                            weigh(t)
                        settle()
                    elif u <= 37:
                        rotate(u - 33)
                        settle()
                    if u == 38:
                        settle().then_inc(prep_done, 1)
                end_phase(dve, l, 1)

                dve.wait_ge(a_trev, l * 6 + 6)
                apart(dve)
                def queries(j, g):
                    dve.tensor_copy(qj[HD * g:HD * g + HD, :], qT[HD * g:HD * g + HD, j, :]).then_inc(a_qj, 1)

                def row_max(j, u):
                    t = u % 5
                    n = P if t == 0 else T
                    dve.wait_ge(a_s, l * 40 + j * 10 + (u + 1))
                    src = ps[:, 2 * (u % 2):2 * (u % 2) + 2, :].rearrange("p a n -> p (a n)")[:, 0:n]
                    dve.tensor_reduce(nb[:, u % 2:u % 2 + 1], src, AX.X, ALU.max, negate=True).then_inc(a_max, 1)

                def scale_rows(j, u):
                    n = P if u % 5 == 0 else T
                    i = slice(u % 2, u % 2 + 1)
                    dve.wait_ge(a_exp, l * 40 + j * 10 + (u + 3))
                    dve.reciprocal(rinv[:, i], rsum[:, i])
                    settle()
                    dve.tensor_scalar(Pb[:, u % 2, 0:n], Pb[:, u % 2, 0:n], rinv[:, i], None,
                                      ALU.mult).then_inc(a_norm, 1)

                def heads(j, last):
                    for u in range(10):
                        if u + 1 < 10:
                            scale_rows(j, u + 1)
                        elif not last:
                            scale_rows(j + 1, 0)
                        if u + 2 < 10:
                            row_max(j, u + 2)
                        elif not last:
                            row_max(j + 1, u - 8)
                        if u % 5 == 3 and not last:
                            queries(j + 1, u // 5)

                queries(0, 0)
                queries(0, 1)
                row_max(0, 0)
                row_max(0, 1)
                scale_rows(0, 0)
                with dve.Fori(0, 3) as j:
                    heads(j, False)
                heads(3, True)
                end_phase(dve, l, 2)

                for o in range(2):
                    dve.wait_ge(k_loaded, l * 32 + 16 * o + 16)
                    apart(dve)
                    for kc in range(NT):
                        settle()
                        dve.wait_ge(y_fwd, l * 10 + 5 * o + kc + 1)
                        uc, us = ps[:, 2 * (kc % 4), :], ps[:, 2 * (kc % 4) + 1, :]
                        kr, ki = Kb[:, kc, 0, :], Kb[:, kc, 1, :]
                        for i, (x, y) in enumerate(((uc, kr), (us, ki), (us, kr), (uc, ki))):
                            dve.tensor_tensor(ytmp[:, i, :], x, y, ALU.mult)
                        settle()
                        dve.tensor_tensor(Yb[:, kc, 0, :], ytmp[:, 0, :], ytmp[:, 1, :], ALU.add)
                        dve.tensor_tensor(Yb[:, kc, 1, :], ytmp[:, 2, :], ytmp[:, 3, :],
                                          ALU.subtract).then_inc(y_mul, 1)
                    for m in range(NT - o):
                        dve.wait_ge(y_inv, l * 9 + 5 * o + m + 1)
                        if o == 0:
                            ins = dve.tensor_tensor(u_tm[:, m, :], ps[:, 2 * (m % 2), :], x1_tm[:, m, :], ALU.mult)
                        else:
                            ins = dve.tensor_tensor(Y3[:, 0, m, :], tok(m % 2), Y3[:, 0, m, :], ALU.mult)
                        ins.then_inc(y_out, 1)
                end_phase(dve, l, 3)

                def branch_lo(br):
                    for k in range(4):
                        dve.wait_ge(x_hi, l * OP + OP_Y + 4 * br + k + 1)
                        dve.tensor_tensor(Y_lo[:, br, k, :], Y3[:, br, k, :], Y_hi[:, br, k, :].bitcast(F32),
                                          ALU.subtract).then_inc(x_lo, 1)

                def merged_lo(c):
                    dve.wait_ge(x_hi, l * OP + OP_M + c + 1)
                    dve.tensor_tensor(m_lo[:, c, :], merged[:, c, :], m_hi[c // 4][:, c % 4, :].bitcast(F32),
                                      ALU.subtract).then_inc(x_lo, 1)

                for u in range(2):
                    split(l, UNITS1 + u)
                    branch_lo(u)
                for n in range(24):
                    half, br, m = n // 12, n % 12 // 4, n % 4
                    c = 4 * half + m
                    dve.wait_ge(sg_in[n % 4], l * 96 + 16 * (n // 4) + 16)
                    dve.wait_ge(br_ready, l * 24 + n + 1)
                    dst = mtmp[:, n % 2, :] if br else merged[:, c, :]
                    ins = dve.tensor_tensor(dst, tokh(n % 4), sgin[:, n % 4, :], ALU.mult)
                    if br:
                        settle()
                        ins = dve.tensor_tensor(merged[:, c, :], merged[:, c, :], dst, ALU.add)
                    ins.then_inc(br_read, 1)
                    if n == 0:
                        branch_lo(2)
                    if n % 2:
                        split(l, UNITS1 + 2 + n // 2)
                    if 16 <= n < 20:
                        merged_lo(n - 16)
                    settle()
                for c in range(4, KC):
                    merged_lo(c)
                for c in range(KC):
                    settle()
                    dve.wait_ge(wo_ready, l * KC + c + 1)
                    residual(tokh(c % 4), c, 16).then_inc(wo_read, 1)
                    if c + 2 < KC:
                        split(l, UNITS1 + 2 * N_BR + 2 + c)
                end_phase(dve, l, 4)
                norm(l, 1, rstd2, h)
                end_phase(dve, l, 5)

                dve.wait_ge(r_lg, l + 1)
                logits = ps[:, 0, 0:NT * NE].rearrange("p (t e) -> p t e", t=NT)
                dve.tensor_reduce(r1[:, :, 0:1], logits, AX.X, ALU.max)
                settle()
                dve.tensor_tensor(lg, logits, r1[:, :, 0:1].to_broadcast([P, NT, NE]), ALU.subtract)\
                    .then_inc(r_sub, 1)
                dve.wait_ge(r_exp, l + 1)
                dve.tensor_reduce(r1[:, :, 0:1], lg, AX.X, ALU.add)
                settle()
                dve.reciprocal(r1[:, :, 1:2], r1[:, :, 0:1])
                settle()
                dve.tensor_tensor(aff, lg, r1[:, :, 1:2].to_broadcast([P, NT, NE]), ALU.mult).then_inc(r_aff, 1)
                dve.wait_ge(r_affT, l + 1)
                dve.tensor_copy(work, tok(1)[0:NE, :])
                for g, c0, c1 in GROUPS:
                    for _ in range(CAP[g] // 8):
                        settle()
                        dve.max(m8[:], work[:, c0:c1])
                        settle()
                        dve.match_replace(work[:, c0:c1], m8[:], work[:, c0:c1], -1.0)
                settle()
                dve.tensor_scalar(mask, work, 0.0, None, ALU.is_lt).then_inc(r_mask, 1)
                dve.wait_ge(r_maskT, l + 1)
                dve.tensor_copy(maskT, ps[:, 0, 0:NT * NE].rearrange("p (t e) -> p t e", t=NT)).then_inc(r_mt, 1)
                settle()
                dve.wait_ge(r_pos, l + 1)
                dve.scalar_tensor_tensor(out=q1, in0=ps[:, 1, 0:NT * NE].rearrange("p (t e) -> p t e", t=NT),
                                         scalar=1.0, in1=maskT, op0=ALU.add, op1=ALU.mult)
                settle()
                for t in range(NT):
                    n = HD if t else 32
                    dst = Ps[:, t - 1, :].rearrange("p (e s) -> p e s", e=NE) if t else Pi
                    ins = dve.tensor_tensor(dst, iota[:, 0:n].unsqueeze(1).to_broadcast([P, NE, n]),
                                            q1[:, t, :].unsqueeze(2).to_broadcast([P, NE, n]), ALU.is_equal)
                ins.then_inc(r_P, 1)
                for n in range(3 * KC):
                    k, part = n // 3, n % 3
                    dve.wait_ge(g_ready, l * 25 + n + 1)
                    if part < 2:
                        ins = dve.tensor_copy(xs[:, k, 8 * part:8 * part + 8, 0:CAP[1]],
                                              ps[:, n % 4, :].rearrange("p (e s) -> p e s", e=8))
                    else:
                        ins = dve.tensor_copy(xs[:, k, :, CAP[1]:SLOTS],
                                              ps[:, n % 4, 0:256].rearrange("p (e s) -> p e s", e=NE))
                    ins.then_inc(g_evac, 1)
                dve.wait_ge(g_ready, l * 25 + 25)
                dve.tensor_copy(gt[0:SLOTS, :], ps[0:SLOTS, 0, 0:NE]).then_inc(g_evac, 1)
                end_phase(dve, l, 6)

                with dve.Fori(0, NE // 4) as b:
                    for ee in range(4):
                        p0 = P_EXP + 6 * ee
                        for hf in range(2):
                            dve.wait_ge(e_silu, l * 2 * NE + b * 8 + (2 * ee + hf + 1))
                            dve.wait_ge(item_used, l * ITEMS + b * 24 + (p0 + 2 * hf + 2))
                            cols = slice(256 * hf, 256 * hf + 256)
                            dve.tensor_tensor(hid[:, ee % 2, cols], ps[0:SLOTS, 2 * hf + 1, 0:256],
                                              sg[:, ee % 2, cols], ALU.mult).then_inc(e_hid, 1)
                        dve.wait_ge(item_used, l * ITEMS + b * 24 + (p0 + 6))
                        r0 = HD * (ee % 2)
                        dve.tensor_scalar(ys[r0:r0 + HD, b * 2 + ee // 2, :],
                                          ps[0:CAP[1], 6:8, :].rearrange("p a n -> p (a n)"),
                                          gt[0:CAP[1], bass.ds(b * 4 + ee, 1)], None, ALU.mult).then_inc(e_yev, 1)
                end_phase(dve, l, 7)

                for m in range(KC):
                    dve.wait_ge(c_ready, l * 8 + m + 1)
                    residual(tok(m % 4), m, 40).then_inc(c_read, 1)
                end_phase(dve, l, 8)


CONSTS = ("ident", "onesm", "ones1", "utri", "sel", "zfeat", "tneg", "rope", "iota", "csi", "cfi", "cs")


def constants():
    f = np.float32
    out = {"ident": np.eye(P), "onesm": np.full((P, P), 1 / D), "ones1": np.ones((P, P)),
           "utri": np.triu(np.ones((P, P)), 1), "iota": np.tile(np.arange(1, HD + 1), (P, 1))}
    sel = np.zeros((P, 2))
    for g in range(2):
        sel[g::32, g] = 1
    out["sel"] = sel
    z, tn = np.zeros((POS, T)), np.zeros((P, NT))
    for (g, c0, c1), L in zip(GROUPS, (LI, LS)):
        n = np.arange(L)
        bands = np.linspace(1e-4, 15, 16)
        ang = 2 * np.pi * n[:, None] * bands[None] / L
        z[:, c0:c1] = np.concatenate([(n / (L - 1))[:, None], np.cos(ang), np.sin(ang)], 1).T
        for t in range(c0 // P, c1 // P):
            tn[:, t] = -(np.arange(P) + P * t - c0) / (L - 1)
    out["zfeat"], out["tneg"] = z, tn
    n = np.arange(LS)
    inv = 10000.0 ** (-np.arange(0, 32, 2) / 32)
    ar, ac = (n // 64)[:, None] * inv, (n % 64)[:, None] * inv
    cosv = np.concatenate([np.cos(ar), np.cos(ar), np.cos(ac), np.cos(ac)], 1)
    sinv = np.concatenate([-np.sin(ar), np.sin(ar), -np.sin(ac), np.sin(ac)], 1)
    out["rope"] = np.stack([x.reshape(4, P, HD).transpose(1, 0, 2) for x in (cosv, sinv)], 1)

    def tables(L):
        k = np.arange(L) + 0.5
        th, ph = np.pi * np.outer(k, k) / L, np.pi * np.outer(np.arange(L), k) / L
        return np.stack([np.cos(th), np.sin(th)]), np.stack([np.cos(ph), np.sin(ph)]) / L

    (ci, fi), (cl, fl) = tables(LI), tables(LS)
    out["csi"], out["cfi"] = ci.transpose(1, 0, 2), fi.transpose(1, 0, 2)
    out["cs"] = cl.reshape(2, 4, P, LS).transpose(2, 0, 1, 3)
    out["cf"] = fl.reshape(2, 4, P, LS).transpose(0, 2, 1, 3).reshape(2, P, ITEM)
    return {k: np.ascontiguousarray(v, dtype=f) for k, v in out.items()}


def weight_stream(w, cf):
    out = np.zeros((DEPTH, ITEMS, P, ITEM), np.float32)

    def columns(dst, m, width, kc):
        for i in range(m.shape[1] // width):
            dst[i] = m[:, i * width:(i + 1) * width].reshape(kc, P, width).transpose(1, 0, 2).reshape(P, -1)

    heads = np.concatenate([np.concatenate([np.arange(HD) + HD * j, np.arange(HD) + HD * (4 + j)])
                            for j in range(4)])
    for l in range(DEPTH):
        o = out[l]
        columns(o[0:], w["mod_w"][l], 256, KC)
        o[P_FILT, 0:FH] = w["hy_w3"][l]
        o[P_FILT, FH] = w["hy_b3"][l]
        o[P_FILT + 1:P_FILT + 3] = cf
        win = w["w_in"][l]
        columns(o[P_HY:], win[:, 0:1536], 256, KC)
        base = 1536 + QKV
        for jp in range(2):
            for n, part in enumerate((0, 2, 1)):
                c = base + 512 * part + 256 * jp
                columns(o[P_SC + 3 * jp + n:], win[:, c:c + 256], 256, KC)
        columns(o[P_QKV:], win[:, 1536:base][:, np.concatenate([heads, np.arange(NQ * HD, QKV)])], 256, KC)
        columns(o[P_GATE:], win[:, base + 1536:], 256, KC)
        for n, (name, rows) in enumerate((("w_br_a", slice(None)), ("w_br_b", heads), ("w_br_c", slice(None)))):
            for half in range(2):
                columns(o[P_BR + 3 * half + n:], w[name][l][rows][:, 512 * half:512 * half + 512], 512, 4)
        columns(o[P_WO:], w["w_o"][l], 256, KC)
        for e in range(NE):
            p = P_EXP + 6 * e
            for hf in range(2):
                columns(o[p + 2 * hf:], w["exp_w_gate"][l, e][:, 256 * hf:256 * hf + 256], 256, KC)
                columns(o[p + 2 * hf + 1:], w["exp_w_up"][l, e][:, 256 * hf:256 * hf + 256], 256, KC)
            columns(o[p + 4:], w["exp_w_down"][l, e], 512, 4)
    return out.reshape(DEPTH * ITEMS, P, ITEM)


def kernel(**inputs):
    import concourse.bacc as bacc
    from concourse.bass_utils import run_bass_kernel_spmd

    w = {k: np.asarray(v) for k, v in inputs.items()}
    f = constants()
    arrays = {"stream": weight_stream(w, f.pop("cf")), **f}

    def feature_major(x):
        return np.swapaxes(x.reshape(*x.shape[:-1], -1, P), -1, -2)

    tokens = np.concatenate([w["x_prompt"][0], w["x_sample"][0]], 0)
    arrays["x"] = tokens.T.reshape(KC, P, T).transpose(1, 0, 2)
    arrays["cond"] = feature_major(np.stack([w["c_ctx"], w["c"][0]])).transpose(1, 2, 0)

    def taps(x):
        return feature_major(x).transpose(0, 2, 3, 1).reshape(DEPTH, P, -1)

    arrays["vec"] = np.concatenate(
        [feature_major(w["mod_b"]), feature_major(w["norm1_w"]), feature_major(w["norm2_w"]),
         taps(w["hy_short_w"]), feature_major(w["hy_short_b"]), taps(w["sc_w"]), feature_major(w["sc_b"])], 2)
    fw = np.zeros((DEPTH, FH, 2 * FH + 2), np.float32)
    fw[:, 0:POS, 0:FH] = w["hy_w1"]
    fw[:, :, FH:2 * FH] = w["hy_w2"]
    fw[:, :, 2 * FH] = w["hy_b1"]
    fw[:, :, 2 * FH + 1] = w["hy_b2"]
    arrays["fw"] = fw
    arrays["decay"] = np.broadcast_to(w["hy_decay"][:, None], (DEPTH, P, 2048))
    arrays["fbias"] = w["hy_bias"].reshape(DEPTH, 1, 2, DH)
    arrays["router"] = w["router_w"].reshape(DEPTH, KC, P, NE).transpose(0, 2, 1, 3)
    qkw = np.concatenate([np.tile(w["q_norm_w"], (1, NQ)), np.tile(w["k_norm_w"], (1, NKV))], 1)
    arrays["qkw"] = np.broadcast_to(qkw[:, None], (DEPTH, P, QK))
    arrays["ctx_k"] = w["cache_k"][0].reshape(DEPTH, PAST, P).transpose(0, 2, 1)
    arrays["ctx_v"] = w["cache_v"][0].reshape(DEPTH, PAST, P)
    arrays = {k: np.ascontiguousarray(v) for k, v in arrays.items()}

    nc = bacc.Bacc("TRN2", target_bir_lowering=False, num_devices=1)
    args = {k: nc.dram_tensor(f"in_{k}", v.shape, F32, kind="ExternalInput").ap() for k, v in arrays.items()}
    args["kspec"] = nc.dram_tensor("kspec", [2, NT, 2, P, DH], F32, kind="Internal").ap()
    args["gates"] = nc.dram_tensor("gates", [24, P, T], F32, kind="Internal").ap()
    for name, shape in (("y", [P, KC, T]), ("new_k", [DEPTH, SEQ_C, P]), ("new_v", [DEPTH, SEQ_C, P])):
        args[name] = nc.dram_tensor(f"out_{name}", shape, F32, kind="ExternalOutput").ap()
    build(nc, args)
    r = run_bass_kernel_spmd(nc, [{f"in_{k}": v for k, v in arrays.items()}], core_ids=[0]).results[0]
    y = r["out_y"].transpose(1, 0, 2).reshape(D, T).T
    caches = [r[f"out_{n}"].reshape(1, DEPTH, SEQ_C, NKV, HD) for n in ("new_k", "new_v")]
    return (np.ascontiguousarray(y[None, 0:LI]), np.ascontiguousarray(y[None, LI:T]), *caches)
```

```python
from contextlib import ExitStack

import concourse.bass as bass
import numpy as np
from concourse import mybir

ACT = mybir.ActivationFunctionType
ALU = mybir.AluOpType
AX = mybir.AxisListType
F32 = mybir.dt.float32
F32R = mybir.dt.float32r

P = 128
D = 1024
KC = D // P
DEPTH = 2
LI, LS = 128, 512
T = LI + LS
NT = T // P
GROUPS = ((0, 0, LI), (1, LI, T))
HALVES = ((0, T // 2), (T // 2, T))
FRONT, BACK, BACK_R = 56 * 256, 85 * 256 + 128, 50 * 256
DH = 512
NE = 16
EPS = 1e-6
SHIFT = 0.05
HD = 64
NQ, NKV = 8, 2
QK = (NQ + NKV) * HD
QKV = QK + NKV * HD
PAST = 128
POS = 33
FH = 64
CAP = (2 * LI // NE, 2 * LS // NE)
SLOTS = CAP[0] + CAP[1]

ITEM = 2048
SLOT = 4
N_MOD, N_FILT, N_HY, N_SC, N_QKV, N_GATE, N_BR, N_WO, N_EXP = 24, 3, 6, 6, 3, 12, 6, 4, 96
P_MOD = 1
P_DFT = P_MOD + N_MOD
P_HY = N_MOD + N_FILT
P_SC = P_HY + N_HY
P_QKV = P_SC + N_SC
P_GATE = P_QKV + N_QKV
P_BR = P_GATE + N_GATE
P_WO = P_BR + N_BR
P_EXP = P_WO + N_WO
ITEMS = P_EXP + N_EXP
LAPS = ITEMS // SLOT
assert ITEMS % SLOT == 0

V_MODB, V_N1, V_N2, V_HYW, V_HYB, V_SCW, V_SCB, NV = 0, 48, 56, 64, 100, 112, 124, 128

PHASES = 9
TWO_PI = (6.28125, 0.0019340515136718750, 2 * np.pi - 6.28125 - 0.0019340515136718750)
ROUND = 1.5 * 2.0 ** 23
PI_IN = 3.1415925
SEQ_C = LI
N_CONSTS = 16 * 10
QSCALE = HD ** -0.5


def build(nc, a):
    with ExitStack() as ctx:
        def sb(name, shape):
            return ctx.enter_context(nc.sbuf_tensor(name, shape, F32))

        def sem(name):
            return ctx.enter_context(nc.semaphore(name))

        ring = sb("ring", [P, SLOT, ITEM])
        X = sb("X", [P, KC, T])
        ident = sb("ident", [P, P])
        onesm = sb("onesm", [P, P])
        ones1 = sb("ones1", [P, P])
        utri = sb("utri", [P, P])
        sel = sb("sel", [P, 2])
        tneg = sb("tneg", [P, NT])
        rope = sb("rope", [P, 2, NT - 1, HD])
        iota = sb("iota", [P, HD])
        csi = sb("csi", [P, 2, P])
        cfi = sb("cfi", [P, 2, P])
        vec = sb("vec", [P, NV])
        fw = sb("fw", [FH, 2 * FH + 2])
        rw = sb("rw", [P, KC, NE])
        qkw = sb("qkw", [P, QK])
        cs = sb("cs", [P, KC, 32])
        cond = sb("cond", [P, KC, 2])
        mod = sb("mod", [P, 48, 2])
        ws = sb("ws", [P, 2, KC, 2])
        st5 = sb("st5", [P, NT, 10])
        rst5 = sb("rst5", [P, NT, 10])
        mx = sb("mx", [P, 2])
        nb = sb("nb", [P, 2])
        rsum = sb("rsum", [P, 2])
        rinv = sb("rinv", [P, 2])
        gt = sb("gt", [P, NE])
        m8 = sb("m8", [NE, 8])
        eps = sb("eps", [P, 1])
        with nc.sbuf_tensor("front_r", [P, FRONT], F32R) as front_r:
            pass
        front = sb("front", [P, FRONT])
        with nc.sbuf_tensor("back_r", [P, BACK_R], F32R) as back_r:
            pass
        back = sb("back", [P, BACK])
        ps = ctx.enter_context(nc.psum_tensor("ps", [P, 8, 512], F32))

        def region(kb, shape, parts=P, r=False):
            n = int(np.prod(shape))
            o = int(kb * 256)
            if o < FRONT:
                mem, size = (front_r if r else front), FRONT
            else:
                mem, size, o = (back_r if r else back), (BACK_R if r else BACK), o - FRONT
            assert o + n <= size, (kb, shape)
            v = mem[0:parts, o:o + n]
            names = "abcd"[:len(shape)]
            if len(shape) == 1:
                return v
            return v.rearrange(f"p ({' '.join(names)}) -> p {' '.join(names)}",
                               **{names[i]: shape[i] for i in range(len(shape) - 1)})

        def region_r(kb, shape):
            return region(kb, shape, r=True)

        W2 = region_r(40, [2, 2, 1024])
        zfeat = region(88, [T], POS)
        w3 = region(91, [2048], FH + 1)
        fa, fb = region(0, [NT, 2, DH]), region(20, [NT, 2, DH])
        win, dec = region(40, [2048]), region(48, [2048])
        fdir = region(56, [2, DH])
        kout = region(60, [4, DH])
        farg, frnd = region(68, [T], FH), region(70.5, [T], FH)
        fh1, fh2 = region(73, [T], FH), region(75.5, [T], FH + 1)
        fbias = region(78, [2, DH], 1)
        mrow = region(82, [4, 256])
        h_hi, h_lo, h_x = region_r(0, [KC, T]), region_r(20, [KC, T]), region(20, [KC, T])
        Y3 = region(56, [3, 4, T])
        sq = region(56, [KC, T])
        u_tm, x1_tm = region(86, [NT, DH]), region(96, [NT, DH])
        qkv = region(106, [NT, QKV])
        raw, cv = region(121, [2, T + 3]), region(126.25, [2, T + 1])
        ubuf, rstd = region(131.5, [2, T]), region(131.5, [T])
        sgb = region(136.5, [2, T])
        prep, prep2 = region(121, [2, QK]), region(126.25, [2, QK])
        qT, kT, qj = region(0, [4, T]), region(10, [P + PAST + LS]), region(13, [T])
        ctxv = region(15.5, [P])
        PT, PTi = region(16, [2, NT, LS]), region(36, [2, P])
        Pb = region(37, [2, T])
        Kb = region(0, [NT, 2, DH])
        Yb = region(20, [NT, 2, DH])
        CS = region(40, [2, 4, DH])
        ytmp = region(106, [4, DH])
        Y_hi, Y_lo = region_r(0, [3, 4, T]), region_r(56, [3, 4, T])
        merged, m_lo = region(86, [KC, T]), region_r(86, [KC, T])
        m_hi = [region_r(30, [4, T]), region_r(0, [4, T])]
        sgin, mtmp = region(106, [4, T]), region(116, [2, T])
        h, sq2, rstd2 = region(0, [KC, T]), region(56, [KC, T]), region(131.5, [T])
        h2_hi, h2_lo = region_r(20, [NT, D]), region_r(56, [NT, D])
        Ps, Pi = region_r(40, [4, NE * HD]), region_r(76, [NE, 32])
        PTs, PTc = region_r(78, [8, LS]), region_r(94, [4, P])
        xs = region(96, [KC, NE, SLOTS])
        work, mask = (region(96 + 2.5 * i, [T], NE) for i in range(2))
        maskT, q1, aff, lg = (region(136 + 0.5 * i, [NT, NE]) for i in range(4))
        r1 = region(138, [NT, 2])
        xe = region(72, [2, KC, SLOTS])
        W4 = region_r(56, [4, 2, 512])
        hidT = (region_r(48, [2, 4, SLOTS]), region_r(51, [2, 4, SLOTS]))
        sg, hid = region(136, [DH], SLOTS), region(138, [DH], SLOTS)
        ysc, ysc_lo = region(0, [12, D]), region_r(0, [12, D])
        ys, yc = ysc[:, 0:8, :], ysc[:, 8:12, :]
        ysc_hi = region_r(56, [2, 12, P])

        landed = [sem(f"item_landed{s}") for s in range(SLOT)]
        item_used = sem("item_used")
        phase = sem("phase")
        cond_in, consts = sem("cond_in"), sem("consts")
        waited = sem("waited")
        lay_net, lay = sem("network_loaded"), sem("layer_vectors")
        s_cs, s_csz = sem("silu_cond"), sem("cs_zeroed")
        modrow_sb, modcol_ready, modcol_read = sem("modrow_sb"), sem("modcol_ready"), sem("modcol_read")
        f_mm, f_arg, f_sin, f_win, f_winread = sem("f_mm"), sem("f_arg"), sem("f_sin"), sem("f_win"), sem("f_winread")
        f_ones, f_dec = sem("f_ones"), sem("f_dec")
        f_taps, f_tapsread = sem("f_taps"), sem("f_taps_read")
        k_ready, k_evac = sem("k_ready"), sem("k_evac")
        k_stored = [sem(f"k_stored{i}") for i in range(4)]
        s_sq, s_ms, s_rt, s_rstd, s_xn, s_h = (sem(n) for n in (
            "squares", "mean_square", "root", "rstd_ready", "x_normed", "h_ready"))
        x_hi, x_lo = sem("operand_hi"), sem("operand_lo")
        OP_Y, OP_M, OP_T = KC, KC + 12, KC + 12 + KC
        OP, OP_HI = OP_T, OP_T + 2 * NT
        o_hi, o_lo = sem("outputs_hi"), sem("outputs_lo")
        w_hi, w_lo = sem("weights_hi"), sem("weights_lo")
        chunk_ready = sem("chunk_ready")
        act_freed, dve_freed = sem("act_freed"), sem("dve_freed")
        conv_done, tr_ready, tr_evac, pads = sem("conv_done"), sem("tr_ready"), sem("tr_evac"), sem("pads_zeroed")
        prep_done = sem("prep_done")
        qs_ready, qrt = sem("q_squares"), sem("q_root")
        sg_ready, sg_free = sem("sg_ready"), sem("sg_free")
        sg_stored = [sem(f"sg_stored{i}") for i in range(2)]
        cache_st = sem("cache_stored")
        a_tr, a_trev, a_ctx = sem("a_tr"), sem("a_tr_evac"), sem("ctx_loaded")
        a_qj, a_s, a_max, a_exp, a_norm, a_pt, a_ptev, a_pv, a_pvev = (sem(n) for n in (
            "a_qj", "a_scores", "a_max", "a_exp", "a_norm", "a_pt", "a_ptev", "a_pv", "a_pvev"))
        cs_loaded, k_loaded, k_free = sem("cs_loaded"), sem("k_loaded"), sem("k_free")
        y_fwd, y_mul, y_inv, y_out = sem("y_fwd"), sem("y_mul"), sem("y_inv"), sem("y_out")
        sg_in = [sem(f"sg_in{i}") for i in range(4)]
        mg_ready, mg_read, MG = sem("merge_ready"), sem("merge_read"), 24 + KC
        r_lg, r_sub, r_exp, r_aff, r_affT, r_aft, r_mask, r_maskT, r_mt, r_pos, r_P = (sem(n) for n in (
            "r_lg", "r_sub", "r_exp", "r_aff", "r_affT", "r_aft", "r_mask", "r_maskT", "r_mt", "r_pos", "r_P"))
        t_ready, t_evac, g_ready, g_evac, g_zero = (sem(n) for n in (
            "t_ready", "t_evac", "g_ready", "g_evac", "yc_zeroed"))
        e_x, e_up, e_silu, e_hid, e_t, e_hidT, e_yev, e_ycev = (sem(n) for n in (
            "e_x", "e_up", "e_silu", "e_hid", "e_t", "e_hidT", "e_yev", "e_ycev"))
        e_hlo, e_whi, e_wlo, e_used = sem("e_hidT_lo"), sem("e_weights_hi"), sem("e_weights_lo"), sem("e_quarter_used")
        c_ready, c_read = sem("c_ready"), sem("c_read")
        out_st = sem("out_stored")

        block = ctx.enter_context(nc.Block())

        def apart(eng):
            eng.sem_inc(waited, 1)

        def end_phase(eng, l, n):
            eng.drain().then_inc(phase, 1)
            eng.wait_ge(phase, l * (4 * PHASES) + 4 * (n + 1))
            apart(eng)

        def tok(b):
            return ps[:, 2 * b:2 * b + 2, :].rearrange("p a n -> p (a n)")[:, 384:1024]

        def tokh(b):
            return ps[:, 2 * b:2 * b + 2, :].rearrange("p a n -> p (a n)")[:, 192:832]

        def w2(u, kc, part):
            return W2[:, u % 2, part, :].rearrange("p (k n) -> p k n", k=kc)

        def half_item(u):
            p = P_HY + u // 2
            w = ring[:, p % SLOT, :]
            if P_QKV <= p < P_GATE:
                return p, w[:, 1024 * (u % 2):1024 * (u % 2) + 1024]
            kc = 4 if P_BR <= p < P_WO else KC
            n = 1024 // kc
            return p, w.rearrange("p (k n) -> p k n", k=kc)[:, :, n * (u % 2):n * (u % 2) + n]

        def half_dst(u, part):
            p = P_HY + u // 2
            if P_QKV <= p < P_GATE:
                return W2[:, u % 2, part, :]
            return w2(u, 4 if P_BR <= p < P_WO else KC, part)

        def wait_half_used(eng, l, u):
            if u < UNITS1:
                eng.wait_ge(chunk_ready, l * CHUNKS + half_chunk(u))
            elif u < UNITS1 + 2 * N_BR:
                eng.wait_ge(mg_ready, l * MG + 2 * (u - UNITS1) + 2)
            else:
                eng.wait_ge(mg_ready, l * MG + 24 + u - UNITS1 - 2 * N_BR + 1)

        QUARTERS = ((0, 0), (0, 1), (1, 0), (1, 1), (0, 2), (0, 3), (1, 2), (1, 3))

        def quarter(l, b, ee, v):
            return l * (8 * NE) + b * 32 + (8 * ee + v)

        def quarter_item(ee, v):
            c, k = QUARTERS[v]
            p = P_EXP + 6 * ee + 4 + c
            return p, ring[:, p % SLOT, 512 * k:512 * k + 512]

        def freed_by(c):
            def kind(x):
                return "act" if x < 12 or (x - 12) % 6 < 2 or x >= 24 else "dve"
            me = kind(c)
            return me, sum(kind(x) == me for x in range(c + 1))

        A_FREED = 12 + 4 + 9

        def wait_chunk_freed(eng, l, c):
            who, n = freed_by(c)
            if who == "act":
                eng.wait_ge(act_freed, l * A_FREED + n)
            else:
                eng.wait_ge(dve_freed, l * 8 + n)

        UNITS1 = 2 * (N_HY + N_SC + N_QKV + N_GATE)
        UNITS = UNITS1 + 2 * (N_BR + N_WO)
        CHUNKS = 24 + 4 * N_QKV + 24

        def half_chunk(u):
            if u < 24:
                return u + 1
            if u < 24 + 2 * N_QKV:
                return 24 + 4 * ((u - 24) // 2) + (4 if u % 2 else 1)
            return u - 2 * N_QKV + 4 * N_QKV + 1

        def wait_chunk(eng, l, c):
            n = c + 1 if c < 24 else 24 + 4 * ((c - 24) // 3) + 2 + (c - 24) % 3
            eng.wait_ge(chunk_ready, l * CHUNKS + n)

        @block.sync
        def _(sp):
            for s in range(SLOT):
                sp.dma_start(ring[:, s, :], a["stream"][s]).then_inc(landed[s], 16)
            with sp.Fori(1, LAPS * DEPTH) as lap:
                for s in range(SLOT):
                    sp.wait_ge(item_used, lap * SLOT + (s + 1 - SLOT))
                    sp.dma_start(ring[:, s, :], a["stream"][lap * SLOT + s]).then_inc(landed[s], 16)

        @block.gpsimd
        def _(pool):
            pairs = [(tneg, "tneg"), (cfi, "cfi"), (X, "x"), (onesm, "onesm"), (ident, "ident"), (rope, "rope"),
                     (csi, "csi"), (ones1, "ones1"), (utri, "utri"), (iota, "iota")]
            for dst, name in pairs:
                pool.dma_start(dst[:], a[name]).then_inc(consts, 16)
            for i in range(2):
                pool.drain().then_inc(sg_free, 1)
            with pool.Fori(0, DEPTH) as l:
                for n in range(20):
                    pool.wait_ge(k_evac, l * 20 + n + 1)
                    apart(pool)
                    pool.dma_start(a["kspec"][n // 10, (n % 10) // 2, n % 2],
                                   kout[:, n % 4, :]).then_inc(k_stored[n % 4], 16)
                for i in range(4):
                    pool.wait_ge(k_stored[i], l * 80 + 80)
                    apart(pool)
                end_phase(pool, l, 0)
                with pool.Fori(0, 12) as g:
                    for i in range(2):
                        pool.wait_ge(sg_ready, l * 24 + g * 2 + (i + 5))
                        apart(pool)
                        pool.dma_start(a["gates"][g * 2 + i], sgb[:, i, :]).then_inc(sg_stored[i], 16)
                        pool.wait_ge(sg_stored[i], l * 192 + g * 16 + 16)
                        apart(pool)
                        pool.drain().then_inc(sg_free, 1)
                pool.wait_ge(prep_done, l + 1)
                apart(pool)
                pool.dma_start(a["new_k"][l], qkv[:, 0, NQ * HD:QK]).then_inc(cache_st, 16)
                pool.dma_start(a["new_v"][l], qkv[:, 0, QK:QKV]).then_inc(cache_st, 16)
                pool.wait_ge(cache_st, l * 32 + 32)
                apart(pool)
                end_phase(pool, l, 1)
                pool.dma_start(kT[:, P:P + PAST], a["ctx_k"][l]).then_inc(a_ctx, 16)
                pool.dma_start(ctxv, a["ctx_v"][l]).then_inc(a_ctx, 16)
                end_phase(pool, l, 2)
                pool.dma_start(CS, a["cs"]).then_inc(cs_loaded, 16)
                for o in range(2):
                    if o:
                        pool.wait_ge(y_mul, l * 10 + 5)
                        apart(pool)
                    pool.dma_start(Kb, a["kspec"][o].rearrange("c r p n -> p c r n")).then_inc(k_loaded, 16)
                end_phase(pool, l, 3)
                for n in range(24):
                    half, br, m = n // 12, n % 12 // 4, n % 4
                    if n >= 4:
                        pool.wait_ge(mg_read, l * MG + n - 3)
                        apart(pool)
                    pool.dma_start(sgin[:, n % 4, :], a["gates"][8 * br + 4 * half + m]).then_inc(sg_in[n % 4], 16)
                for i in range(4, PHASES):
                    if i == 7:
                        pool.memset(yc, 0.0).then_inc(g_zero, 1)
                        with pool.Fori(0, NE // 4) as b:
                            for ee in range(4):
                                pool.wait_ge(item_used, l * ITEMS + b * 24 + (P_EXP + 6 * ee - 8))
                                apart(pool)
                                pool.tensor_copy(xe[:, ee % 2], xs[:, :, b * 4 + ee, :]).then_inc(e_x, 1)
                    end_phase(pool, l, i)
            pool.dma_start(a["y"], X[:]).then_inc(out_st, 16)
            pool.wait_ge(out_st, 16)
            apart(pool)

        @block.tensor
        def _(pe):
            def item(l, p, j=0):
                pe.wait_ge(landed[p % SLOT], l * (16 * LAPS) + j * 16 + 16 * (p // SLOT + 1))
                return ring[:, p % SLOT, :]

            def passes(n):
                for k in range(n):
                    for wp, hp in ((0, 0), (0, 1), (1, 0)):
                        yield k, wp, hp, k == 0 and wp + hp == 0, k == n - 1 and wp == 1

            def chunk(b, w, src, n, wait=None):
                for k, wp, hp, first, last in passes(n):
                    if wait and wp + hp == 0:
                        wait(k)
                    for c0, c1 in HALVES:
                        mm = pe.matmul(tokh(b)[:, c0:c1], w(wp)[:, k, :], src(hp, k)[:, c0:c1], start=first, stop=last)
                return mm

            def half_ready(l, u):
                pe.wait_ge(w_lo, l * UNITS + u + 1)
                if u % 2:
                    pe.sem_inc(item_used, 1)

            def mean_square(l, src, n):
                for k in range(KC):
                    pe.wait_ge(s_sq, l * 16 + 8 * n + k + 1)
                    for c0, c1 in HALVES:
                        mm = pe.matmul(tokh(0)[:, c0:c1], onesm[:], src[:, k, c0:c1], start=k == 0, stop=k == KC - 1)
                mm.then_inc(s_ms, 1)

            for _ in range(4):
                pe.drain().then_inc(e_used, 1)
            pe.wait_ge(cond_in, 32)
            pe.wait_ge(s_cs, 1)
            for _ in range(2):
                pe.drain().then_inc(a_pv, 1)
            with pe.Fori(0, DEPTH) as l:
                def modulation(it):
                    def turn(s):
                        pe.wait_ge(modrow_sb, l * N_MOD + 4 * it + s + 5)
                        pe.wait_ge(modcol_read, l * N_MOD + 4 * it + s + 3)
                        for c in range(2):
                            mm = pe.matmul(ps[:, 2 + s % 2, 2 * c:2 * c + 2], mrow[:, s, P * c:P * c + P], sel[:],
                                           start=True, stop=True)
                        mm.then_inc(modcol_ready, 1)

                    for s in range(4):
                        w = item(l, P_MOD + 4 * it + s).rearrange("p (k n) -> p k n", k=KC)
                        pe.wait_ge(modrow_sb, l * N_MOD + 4 * it + s + 3)
                        for k in range(KC):
                            j = k % 4
                            mm = pe.matmul(ps[32 * j:32 * j + 32, s % 2, 0:256], cs[:, k, :], w[:, k, :],
                                           start=k < 4, stop=k >= 4)
                        mm.then_inc(item_used, 1)
                        if s:
                            turn(s - 1)
                    turn(3)

                def network(n):
                    apart(pe)
                    w, src = ((fw[0:POS, 0:FH], zfeat), (fw[:, FH:2 * FH], fh1))[n]
                    for c0, c1 in HALVES:
                        mm = pe.matmul(tokh(2)[0:FH, c0:c1], w, src[:, c0:c1], start=True, stop=True)
                    mm.then_inc(f_mm, 1)

                def taps(n):
                    t, o = n // 2, n % 2
                    if n >= 2:
                        pe.wait_ge(f_tapsread, l * 10 + n - 1)
                    for d in range(2):
                        mm = pe.matmul(ps[:, 4 + 2 * (n % 2) + d, :], fh2[:, P * t:P * t + P],
                                       w3[:, DH * (2 * d + o):DH * (2 * d + o + 1)], start=True, stop=True)
                    mm.then_inc(f_taps, 1)

                pe.wait_ge(item_used, l * ITEMS + 1)
                pe.wait_ge(lay_net, l * 32 + 32)
                network(0)
                modulation(0)
                pe.wait_ge(f_sin, l * 2 + 1)
                network(1)
                modulation(1)
                pe.wait_ge(f_sin, l * 2 + 2)
                pe.wait_ge(f_ones, l + 1)
                for t in range(NT):
                    taps(2 * t)
                    taps(2 * t + 1)
                    if t < 4:
                        modulation(2 + t)
                pe.wait_ge(modrow_sb, l * N_MOD + N_MOD + 4)
                pe.wait_ge(consts, N_CONSTS)
                cf = [item(l, P_DFT + r).rearrange("p (t k) -> p t k", t=4) for r in range(2)]
                pe.wait_ge(f_tapsread, l * 10 + 10)
                for n in range(20):
                    o, kc, r = n // 10, n % 10 // 2, n % 2
                    src = (fa, fb)[r]
                    if n >= 2:
                        pe.wait_ge(k_evac, l * 20 + n - 1)
                    if kc == 0:
                        mm = pe.matmul(ps[:, n % 2, :], cfi[:, r, :], src[:, 0, o, :], start=True, stop=True)
                    for t in range(4 if kc else 0):
                        mm = pe.matmul(ps[:, n % 2, :], cf[r][:, t, P * (kc - 1):P * kc], src[:, 1 + t, o, :],
                                       start=t == 0, stop=t == 3)
                    mm.then_inc(item_used if n >= 18 else k_ready, 1)
                end_phase(pe, l, 0)

                mean_square(l, sq, 0)
                pe.wait_ge(s_rt, l * 2 + 1)

                def h_part(part, k):
                    return (h_hi, h_lo)[part][:, k, :]

                def transposes(c):
                    pe.wait_ge(conv_done, l * 12 + c + 1)
                    if c:
                        pe.wait_ge(tr_evac, l * 8 + c)
                    for t in range(NT):
                        x0 = P * t + (t > 0)
                        mm = pe.transpose(ps[:, 6 + t // 4, P * (t % 4):P * (t % 4) + P], cv[:, c % 2, x0:x0 + P],
                                          ident[:])
                    mm.then_inc(tr_ready, 1)

                for c in range(24):
                    half_ready(l, c)
                    if c >= 3:
                        wait_chunk_freed(pe, l, c - 3)
                    wait = (lambda k: pe.wait_ge(x_lo, l * OP + k + 1)) if c == 0 else None
                    chunk(c % 3, lambda part: w2(c, KC, part), h_part, KC, wait).then_inc(chunk_ready, 1)
                    if 1 <= c <= 8:
                        transposes(c - 1)
                for i in range(3):
                    for hf in range(2):
                        half_ready(l, 24 + 2 * i + hf)
                        for u in range(3):
                            n = 24 + 3 * i + u
                            if hf == 0:
                                wait_chunk_freed(pe, l, n - 3)
                            for t in range(2 * u, min(2 * u + 2, NT)):
                                for k, wp, hp, first, last in passes(4):
                                    mm = pe.matmul(ps[:, 2 * (n % 3) + t % 2, 0:256],
                                                   h_part(hp, 4 * hf + k)[:, P * t:P * t + P],
                                                   w2(hf, 4, wp)[:, k, :], start=first and hf == 0, stop=last and hf == 1)
                            if hf or u == 2:
                                mm.then_inc(chunk_ready, 1)
                wait_chunk_freed(pe, l, 32)
                pe.wait_ge(tr_evac, l * 8 + 8)
                apart(pe)
                with pe.Fori(0, 6) as it:
                    for n in range(4):
                        u = 30 + n
                        pe.wait_ge(w_lo, l * UNITS + it * 4 + (u + 1))
                        if n % 2:
                            pe.sem_inc(item_used, 1)
                        pe.wait_ge(sg_ready, l * 24 + it * 4 + (n + 1))
                        chunk(n, lambda part: w2(n, KC, part), h_part, KC).then_inc(chunk_ready, 1)
                end_phase(pe, l, 1)

                for t in range(NT):
                    if t >= 2:
                        pe.wait_ge(a_trev, l * 6 + t - 1)
                    for j in range(4):
                        mm = pe.transpose(ps[:, t % 2, P * j:P * j + P], qkv[:, t, P * j:P * j + P], ident[:])
                    mm.then_inc(a_tr, 1)
                for t in range(NT):
                    mm = pe.transpose(ps[:, 2 + (t + 3) // 4, P * ((t + 3) % 4):P * ((t + 3) % 4) + P],
                                      qkv[:, t, NQ * HD:QK], ident[:])
                mm.then_inc(a_tr, 1)
                pe.wait_ge(a_trev, l * 6 + 6)
                pe.wait_ge(a_ctx, l * 32 + 32)
                apart(pe)
                def scores(j, u):
                    g, t = u // 5, u % 5
                    if t == 0:
                        pe.wait_ge(a_qj, l * 8 + j * 2 + (g + 1))
                    pe.wait_ge(a_exp, l * 40 + j * 10 + (u + 1))
                    apart(pe)
                    q = qj[HD * g:HD * g + HD, P * t:P * t + P]
                    kk = kT[HD * g:HD * g + HD, :]
                    b = 2 * (u % 2)
                    if t == 0:
                        mm = pe.matmul(ps[:, b, 0:P], q, kk[:, 0:P], start=True, stop=True)
                    else:
                        pe.matmul(ps[:, b, 0:512], q, kk[:, P:P + 512], start=True, stop=True)
                        mm = pe.matmul(ps[:, b + 1, 0:P], q, kk[:, P + 512:P + 640], start=True, stop=True)
                    mm.then_inc(a_s, 1)

                def turn_p(j, u):
                    t = u % 5
                    pe.wait_ge(a_norm, l * 40 + j * 10 + (u + 1))
                    pe.wait_ge(a_ptev, l * 40 + j * 10 + (u + 1))
                    for kt in range(1 if t == 0 else NT):
                        mm = pe.transpose(ps[:, 4 + kt // 4, P * (kt % 4):P * (kt % 4) + P],
                                          Pb[:, u % 2, P * kt:P * kt + P], ident[:])
                    mm.then_inc(a_pt, 1)

                def values(j, g, kt):
                    vc = slice(QK + HD * g, QK + HD * g + HD)
                    o = slice(HD * g, HD * g + HD)
                    if kt == 0:
                        pe.wait_ge(a_ptev, l * 40 + j * 10 + (5 * g + 6))
                        if g == 0:
                            pe.wait_ge(a_pvev, l * 4 + j + 1)
                            apart(pe)
                        pe.matmul(ps[o, 6, 0:P], qkv[:, 0, vc], PTi[:, g, :], start=True, stop=True)
                    v = ctxv[:, HD * g:HD * g + HD] if kt == 0 else qkv[:, kt, vc]
                    mm = pe.matmul(ps[o, 7, :], v, PT[:, g, kt, :], start=kt == 0, stop=kt == NT - 1)
                    if kt == NT - 1:
                        mm.then_inc(a_pv, 1)

                def heads(j, first, last):
                    for u in range(10):
                        turn_p(j, u)
                        if u + 2 < 10:
                            scores(j, u + 2)
                        elif not last:
                            scores(j + 1, u - 8)
                        if u >= 5:
                            values(j, 0, u - 5)
                        elif not first:
                            values(j - 1, 1, u)

                scores(0, 0)
                scores(0, 1)
                heads(0, True, False)
                with pe.Fori(1, 3) as j:
                    heads(j, False, False)
                heads(3, False, True)
                for kt in range(NT):
                    values(3, 1, kt)
                end_phase(pe, l, 2)

                pe.wait_ge(cs_loaded, l * 16 + 16)
                for o in range(2):
                    if o:
                        pe.wait_ge(y_out, l * 9 + 5)
                    for kc in range(NT):
                        n = 5 * o + kc
                        if kc >= 4:
                            pe.wait_ge(y_mul, l * 10 + n - 3)
                        for r in range(2):
                            bank = 2 * (kc % 4) + r
                            if kc == 0:
                                mm = pe.matmul(ps[:, bank, :], csi[:, r, :], u_tm[:, 0, :], start=True, stop=True)
                            for t in range(4 if kc else 0):
                                mm = pe.matmul(ps[:, bank, :], CS[:, r, t, P * (kc - 1):P * kc], u_tm[:, 1 + t, :],
                                               start=t == 0, stop=t == 3)
                        mm.then_inc(y_fwd, 1)
                    pe.wait_ge(y_mul, l * 10 + 5 * o + 5)
                    for m in range(NT - o):
                        n = 5 * o + m
                        if m >= 2:
                            pe.wait_ge(y_out, l * 9 + n - 1)
                        b = 2 * (m % 2)
                        if o == 0 and m == 0:
                            for r in range(2):
                                mm = pe.matmul(ps[:, b, :], csi[:, r, :], Yb[:, 0, r, :], start=r == 0, stop=r == 1)
                        elif o == 0:
                            for kc in range(4):
                                for r in range(2):
                                    mm = pe.matmul(ps[:, b, :], CS[:, r, kc, P * (m - 1):P * m], Yb[:, 1 + kc, r, :],
                                                   start=kc + r == 0, stop=kc + r == 4)
                        else:
                            tb = tok(m % 2)
                            for r in range(2):
                                pe.matmul(tb[:, 0:LI], Yb[:, 0, r, P * m:P * m + P], csi[:, r, :], start=r == 0,
                                          stop=r == 1)
                            for kc in range(4):
                                for r in range(2):
                                    mm = pe.matmul(tb[:, LI:T], Yb[:, 1 + kc, r, P * m:P * m + P], CS[:, r, kc, :],
                                                   start=kc + r == 0, stop=kc + r == 4)
                        mm.then_inc(y_inv, 1)
                end_phase(pe, l, 3)

                for n in range(24):
                    half, br, m = n // 12, n % 12 // 4, n % 4
                    if n % 2 == 0:
                        half_ready(l, UNITS1 + n // 2)
                    if n >= 4:
                        pe.wait_ge(mg_read, l * MG + n - 3)
                    wait = (lambda k: pe.wait_ge(x_lo, l * OP + OP_Y + 4 * br + k + 1)) if n in (0, 4, 8) else None
                    chunk(n % 4, lambda part: w2(n // 2, 4, part)[:, :, P * (m % 2):P * (m % 2) + P],
                          lambda part, k: (Y_hi, Y_lo)[part][:, br, k, :], 4, wait).then_inc(mg_ready, 1)
                pe.wait_ge(mg_read, l * MG + 24)
                for c in range(KC):
                    half_ready(l, UNITS1 + 2 * N_BR + c)
                    if c >= 4:
                        pe.wait_ge(mg_read, l * MG + 24 + c - 3)
                    wait = (lambda k: pe.wait_ge(x_lo, l * OP + OP_M + k + 1)) if c == 0 else None
                    chunk(c % 4, lambda part: w2(c, KC, part),
                          lambda part, k: m_lo[:, k, :] if part else m_hi[k // 4][:, k % 4, :], KC, wait)\
                        .then_inc(mg_ready, 1)
                end_phase(pe, l, 4)

                mean_square(l, sq2, 1)
                end_phase(pe, l, 5)

                for t in range(NT):
                    for k in range(KC):
                        mm = pe.matmul(ps[:, 0, NE * t:NE * t + NE], h[:, k, P * t:P * t + P], rw[:, k, :],
                                       start=k == 0, stop=k == KC - 1)
                mm.then_inc(r_lg, 1)
                for n in range(2 * NT):
                    t, hf = n // 2, n % 2
                    if n == 2:
                        pe.wait_ge(r_aff, l + 1)
                        for i in range(NT):
                            mm = pe.transpose(tok(1)[0:NE, P * i:P * i + P], aff[:, i, :], ident[:])
                        mm.then_inc(r_affT, 1)
                    if n >= 2:
                        pe.wait_ge(t_evac, l * 19 + n - 1)
                    for i in range(4):
                        mm = pe.transpose(ps[:, 4 + n % 2, P * i:P * i + P], h[:, 4 * hf + i, P * t:P * t + P],
                                          ident[:])
                    mm.then_inc(t_ready, 1)
                pe.wait_ge(r_mask, l + 1)
                apart(pe)
                for t in range(NT):
                    mm = pe.transpose(ps[:, 0, NE * t:NE * t + NE], mask[:, P * t:P * t + P], ident[0:NE, 0:NE])
                mm.then_inc(r_maskT, 1)
                pe.wait_ge(r_mt, l + 1)
                for t in range(NT):
                    pe.matmul(ps[:, 1, NE * t:NE * t + NE], utri[:], maskT[:, t, :], start=True, stop=t <= 1)
                    for s in range(1, t):
                        mm = pe.matmul(ps[:, 1, NE * t:NE * t + NE], ones1[:], maskT[:, s, :], start=False,
                                       stop=s == t - 1)
                mm.then_inc(r_pos, 1)
                pe.wait_ge(r_P, l + 1)
                pe.wait_ge(t_evac, l * 19 + 10)
                for n in range(3 * KC):
                    k, part = n // 3, n % 3
                    if n >= 4:
                        pe.wait_ge(g_evac, l * 25 + n - 3)
                    bank = ps[:, n % 4, :]
                    if part < 2:
                        for t in range(4):
                            for i, h2 in enumerate((h2_hi, h2_lo)):
                                mm = pe.matmul(bank, h2[:, 1 + t, P * k:P * k + P],
                                               Ps[:, t, 512 * part:512 * part + 512],
                                               start=t + i == 0, stop=t + i == 4)
                    else:
                        for i, h2 in enumerate((h2_hi, h2_lo)):
                            mm = pe.matmul(bank[:, 0:256], h2[:, 0, P * k:P * k + P], Pi[:, :, 0:CAP[0]],
                                           start=i == 0, stop=i == 1)
                    mm.then_inc(g_ready, 1)
                pe.wait_ge(g_evac, l * 25 + 21)
                for e in range(NE):
                    for t in range(4):
                        pe.matmul(ps[0:CAP[1], 0, e:e + 1], Ps[:, t, HD * e:HD * e + HD].bitcast(F32), aff[:, 1 + t, e:e + 1],
                                  start=t == 0, stop=t == 3)
                    mm = pe.matmul(ps[CAP[1]:SLOTS, 0, e:e + 1], Pi[:, e, 0:CAP[0]].bitcast(F32), aff[:, 0, e:e + 1],
                                   start=True, stop=True)
                mm.then_inc(g_ready, 1)
                for n in range(8):
                    pe.wait_ge(t_evac, l * 19 + 10 + max(n - 1, 0))
                    for t in range(4):
                        mm = pe.transpose(ps[:, 4 + n % 2, P * t:P * t + P], Ps[:, t, P * n:P * n + P].bitcast(F32),
                                          ident[:])
                    mm.then_inc(t_ready, 1)
                for g in range(4):
                    mm = pe.transpose(ps[:, 6, P * g:P * g + P],
                                      Pi[:, 4 * g:4 * g + 4, :].rearrange("p e s -> p (e s)").bitcast(F32), ident[:])
                mm.then_inc(t_ready, 1)
                end_phase(pe, l, 6)

                with pe.Fori(0, NE // 4) as b:
                    for ee in range(4):
                        p0 = P_EXP + 6 * ee

                        def w_in_item(i):
                            return item(l, p0 + i, b * 6).rearrange("p (k n) -> p k n", k=KC)

                        x = xe[:, ee % 2]
                        pe.wait_ge(e_x, l * NE + b * 4 + ee + 1)
                        def up(hf, which):
                            w = w_in_item(2 * hf + which)
                            for k in range(KC):
                                mm = pe.matmul(ps[0:SLOTS, 2 * hf + which, 0:256], x[:, k, :], w[:, k, :],
                                               start=k == 0, stop=k == KC - 1)
                            mm.then_inc(item_used, 1)

                        def turn_hidden(hf):
                            pe.wait_ge(e_hid, l * 2 * NE + b * 8 + 2 * ee + hf + 1)
                            for i in range(2):
                                mm = pe.transpose(ps[:, 4 + hf, SLOTS * i:SLOTS * i + SLOTS],
                                                  hid[:, P * (2 * hf + i):P * (2 * hf + i) + P],
                                                  ident[0:SLOTS, 0:SLOTS])
                            mm.then_inc(e_t, 1)

                        def down(v):
                            c, k = QUARTERS[v]
                            pe.wait_ge(e_whi, quarter(l, b, ee, v + 1))
                            if k == 3:
                                pe.wait_ge(e_wlo, quarter(l, b, ee, v + 1))
                            for n, (wp, hp) in enumerate(((0, 0), (0, 1), (1, 0))):
                                if n == 2 and k < 3:
                                    pe.wait_ge(e_wlo, quarter(l, b, ee, v + 1))
                                mm = pe.matmul(ps[0:SLOTS, 6 + c, :], hidT[hp][:, ee % 2, k, :], W4[:, v % 4, wp, :],
                                               start=k + n == 0, stop=k == 3 and n == 2)
                                if n == 0 and k == 3:
                                    mm.then_inc(item_used, 1)
                            mm.then_inc(e_used, 1)

                        up(0, 0)
                        up(0, 1)
                        up(1, 0)
                        turn_hidden(0)
                        up(1, 1)
                        pe.wait_ge(e_hlo, l * 2 * NE + b * 8 + 2 * ee + 1)
                        pe.wait_ge(e_yev, l * NE + b * 4 + ee + 1)
                        pe.wait_ge(e_ycev, l * NE + b * 4 + ee + 1)
                        down(0)
                        down(1)
                        turn_hidden(1)
                        down(2)
                        down(3)
                        pe.wait_ge(e_hlo, l * 2 * NE + b * 8 + 2 * ee + 2)
                        for v in range(4, 8):
                            down(v)
                end_phase(pe, l, 7)

                for m in range(KC):
                    if m >= 4:
                        pe.wait_ge(c_read, l * 8 + m - 3)
                    pe.wait_ge(o_lo, l * 8 + m + 1)
                    tb = tok(m % 4)
                    parts = (ysc_hi[:, m % 2], ysc_lo[:, :, P * m:P * m + P])
                    for g in range(4):
                        for i in range(2):
                            pe.matmul(tb[:, 0:LI], parts[i][:, 8 + g, :], PTc[:, g, :], start=g + i == 0,
                                      stop=g + i == 4)
                    for n in range(8):
                        for i in range(2):
                            mm = pe.matmul(tb[:, LI:T], parts[i][:, n, :], PTs[:, n, :], start=n + i == 0,
                                           stop=n + i == 8)
                    mm.then_inc(c_ready, 1)
                end_phase(pe, l, 8)

        @block.scalar
        def _(act):
            def copy(o, i):
                return act.activation(o, i, ACT.Copy)

            def split(l, u):
                p, src = half_item(u)
                wait_half_used(act, l, u - 2)
                act.wait_ge(landed[p % SLOT], l * (16 * LAPS) + 16 * (p // SLOT + 1))
                copy(half_dst(u, 0), src).then_inc(w_hi, 1)

            def split_first(l, u):
                p, src = half_item(u)
                act.wait_ge(landed[p % SLOT], l * (16 * LAPS) + 16 * (p // SLOT + 1))
                copy(half_dst(u, 0), src).then_inc(w_hi, 1)

            def norm(l, n, squares, root, dst):
                for k in range(KC):
                    act.activation(squares[:, k, :], X[:, k, :], ACT.Square).then_inc(s_sq, 1)
                if n == 0:
                    split_first(l, 0)
                    split_first(l, 1)
                act.wait_ge(s_ms, l * 2 + n + 1)
                act.activation(root, tokh(0), ACT.Sqrt, bias=eps[:, 0:1]).then_inc(s_rt, 1)
                for k in range(KC):
                    act.wait_ge(s_xn, l * 16 + 8 * n + k + 1)
                    for g, c0, c1 in GROUPS:
                        x = dst[:, k, c0:c1] if n else h_x[:, k, c0:c1]
                        ins = act.activation(dst[:, k, c0:c1], x, ACT.Identity, bias=mod[:, 24 * n + k, g:g + 1])
                    ins.then_inc(s_h if n else x_hi, 1)

            act.dma_start(cond[:], a["cond"]).then_inc(cond_in, 16)
            act.dma_start(sel[:], a["sel"]).then_inc(cond_in, 16)
            act.wait_ge(cond_in, 32)
            act.wait_ge(s_csz, 1)
            act.activation(cs[:, :, 0:2], cond[:], ACT.Silu).then_inc(s_cs, 1)
            for _ in range(SLOT):
                act.drain().then_inc(modrow_sb, 1)
                act.drain().then_inc(sg_ready, 1)
            act.drain().then_inc(e_ycev, 1)
            for _ in range(2):
                act.drain().then_inc(a_exp, 1)
            act.drain().then_inc(a_ptev, 1)
            act.drain().then_inc(a_pvev, 1)
            with act.Fori(0, DEPTH) as l:
                for dst, src in ((fw[:], a["fw"][l]), (zfeat, a["zfeat"])):
                    act.dma_start(dst, src).then_inc(lay_net, 16)
                for dst, src in ((vec[:], a["vec"][l]), (dec, a["decay"][l]), (fbias, a["fbias"][l]),
                                 (rw[:], a["router"][l]), (qkw[:], a["qkw"][l])):
                    act.dma_start(dst, src).then_inc(lay, 16)
                act.wait_ge(landed[0], l * (16 * LAPS) + 16)
                copy(w3, ring[0:FH + 1, 0, :]).then_inc(item_used, 1)

                def modulation(it):
                    for s in range(4):
                        act.wait_ge(item_used, l * ITEMS + P_MOD + 4 * it + s + 1)
                        act.wait_ge(modcol_read, l * N_MOD + 4 * it + s + 1)
                        copy(mrow[:, s, :], ps[:, s % 2, 0:256]).then_inc(modrow_sb, 1)

                def sine(n, dst):
                    act.wait_ge(f_arg, l * 2 + n + 1)
                    act.activation(dst[0:FH, :], farg, ACT.Sin).then_inc(f_sin, 1)

                sine(0, fh1)
                modulation(0)
                sine(1, fh2)
                modulation(1)
                act.wait_ge(consts, N_CONSTS)
                act.wait_ge(f_dec, l + 1)
                for t in range(NT):
                    if t:
                        act.wait_ge(f_tapsread, l * 10 + 2 * t)
                    act.activation(win, dec, ACT.Exp, scale=tneg[:, t:t + 1]).then_inc(f_win, 1)
                    if t < 4:
                        modulation(2 + t)
                for n in range(20):
                    if n >= 18:
                        act.wait_ge(item_used, l * ITEMS + P_DFT + n - 17)
                    else:
                        act.wait_ge(k_ready, l * 18 + n + 1)
                    if n >= 4:
                        act.wait_ge(k_stored[n % 4], l * 80 + 16 * (n // 4))
                    copy(kout[:, n % 4, :], ps[:, n % 2, :]).then_inc(k_evac, 1)
                end_phase(act, l, 0)
                norm(l, 0, sq, rstd, h_hi)
                act.wait_ge(pads, l + 1)

                def evac_tr(c):
                    act.wait_ge(tr_ready, l * 8 + c + 1)
                    dst = (u_tm, x1_tm)[c // 4][:, :, P * (c % 4):P * (c % 4) + P]
                    src = ps[:, 6:8, :].rearrange("p a n -> p (a n)")[:, 0:T].rearrange("p (t n) -> p t n", t=NT)
                    copy(dst, src).then_inc(tr_evac, 1)

                for c in range(24):
                    if freed_by(c)[0] == "act":
                        wait_chunk(act, l, c)
                        if c < 12:
                            if c >= 2:
                                act.wait_ge(conv_done, l * 12 + c - 1)
                            copy(raw[:, c % 2, 1:1 + LI], tokh(c % 3)[:, 0:LI])
                            copy(raw[:, c % 2, 2 + LI:2 + T], tokh(c % 3)[:, LI:T]).then_inc(act_freed, 1)
                        else:
                            if c >= 18:
                                act.wait_ge(dve_freed, l * 8 + c % 2 + 1)
                            copy(ubuf[:, c % 2, :], tokh(c % 3)).then_inc(act_freed, 1)
                    split(l, c + 2)
                    if 2 <= c <= 9:
                        evac_tr(c - 2)
                for n in range(9):
                    i, u = n // 3, n % 3
                    if u == 0:
                        split(l, 26 + 2 * i)
                    wait_chunk(act, l, 24 + n)
                    t1 = min(2 * u + 2, NT)
                    b = 2 * ((24 + n) % 3)
                    copy(qkv[:, 2 * u:t1, 256 * i:256 * i + 256], ps[:, b:b + t1 - 2 * u, 0:256]).then_inc(act_freed, 1)
                    if u == 2:
                        split(l, 27 + 2 * i)
                act.wait_ge(qs_ready, l + 1)
                act.activation(st5[:], st5[:], ACT.Sqrt, bias=eps[:, 0:1], scale=1.0 / HD).then_inc(qrt, 1)
                def gates(n, it):
                    act.wait_ge(chunk_ready, l * CHUNKS + it * 8 + (24 + 4 * N_QKV + n + 1))
                    act.wait_ge(sg_free, l * 24 + it * 8 + (n + 1))
                    act.activation(sgb[:, n % 2, :], tokh(n % 4), ACT.Sigmoid).then_inc(sg_ready, 1)

                def turn(it, last):
                    for n in range(8):
                        gates(n, it)
                        if last and n >= 6:
                            continue
                        p, src = half_item(32 + n)
                        act.wait_ge(landed[p % SLOT], l * (16 * LAPS) + it * 16 + 16 * (p // SLOT + 1))
                        copy(w2(n, KC, 0), src).then_inc(w_hi, 1)

                with act.Fori(0, 2) as it:
                    turn(it, False)
                turn(2, True)
                end_phase(act, l, 1)
                for t in range(NT):
                    act.wait_ge(a_tr, l * 6 + t + 1)
                    act.activation(qT[:, :, P * t:P * t + P], ps[:, t % 2, :].rearrange("p (j n) -> p j n", j=4),
                                   ACT.Copy, scale=QSCALE).then_inc(a_trev, 1)
                act.wait_ge(a_tr, l * 6 + 6)
                copy(kT[:, 0:P], tok(1)[:, 0:LI])
                copy(kT[:, P + PAST:], tok(1)[:, LI:T]).then_inc(a_trev, 1)
                def exp(j, u):
                    t = u % 5
                    n = P if t == 0 else T
                    act.wait_ge(a_max, l * 40 + j * 10 + (u + 1))
                    src = ps[:, 2 * (u % 2):2 * (u % 2) + 2, :].rearrange("p a n -> p (a n)")[:, 0:n]
                    act.activation(Pb[:, u % 2, 0:n], src, ACT.Exp, bias=nb[:, u % 2:u % 2 + 1],
                                   accum_out=rsum[:, u % 2:u % 2 + 1]).then_inc(a_exp, 1)

                def evac_pt(j, u):
                    g, t = u // 5, u % 5
                    act.wait_ge(a_pt, l * 40 + j * 10 + (u + 1))
                    act.wait_ge(a_pv, l * 8 + j * 2 + (g + 1))
                    flat = ps[:, 4:6, :].rearrange("p a n -> p (a n)")
                    if t == 0:
                        copy(PTi[:, g, :], flat[:, 0:P]).then_inc(a_ptev, 1)
                    else:
                        copy(PT[:, g, :, P * (t - 1):P * t],
                             flat[:, 0:T].rearrange("p (k n) -> p k n", k=NT)).then_inc(a_ptev, 1)

                def evac_values(j):
                    act.wait_ge(a_pv, l * 8 + j * 2 + 4)
                    copy(Y3[:, 1, j, 0:LI], ps[:, 6, 0:LI])
                    copy(Y3[:, 1, j, LI:T], ps[:, 7, :]).then_inc(a_pvev, 1)

                def heads(j, first, last):
                    for u in range(10):
                        evac_pt(j, u)
                        if u == 5 and not first:
                            evac_values(j - 1)
                        if u + 2 < 10:
                            exp(j, u + 2)
                        elif not last:
                            exp(j + 1, u - 8)

                exp(0, 0)
                exp(0, 1)
                heads(0, True, False)
                with act.Fori(1, 3) as j:
                    heads(j, False, False)
                heads(3, False, True)
                evac_values(3)
                end_phase(act, l, 2)
                end_phase(act, l, 3)
                def merged_hi(c):
                    act.wait_ge(mg_read, l * MG + (21 + c - 4 if c >= 4 else 9 + c))
                    copy(m_hi[c // 4][:, c % 4, :], merged[:, c, :]).then_inc(x_hi, 1)

                for br in range(3):
                    if br < 2:
                        split_first(l, UNITS1 + br)
                    for k in range(4):
                        copy(Y_hi[:, br, k, :], Y3[:, br, k, :]).then_inc(x_hi, 1)
                for u in range(UNITS1 + 2, UNITS):
                    split(l, u)
                    if u == UNITS1 + 7:
                        for c in range(4):
                            merged_hi(c)
                    if u == UNITS1 + 2 * N_BR + 1:
                        for c in range(4, KC):
                            merged_hi(c)
                end_phase(act, l, 4)
                norm(l, 1, sq2, rstd2, h)
                end_phase(act, l, 5)

                def evac_t(n):
                    act.wait_ge(t_ready, l * 19 + n + 1)
                    copy(h2_hi[:, n // 2, 512 * (n % 2):512 * (n % 2) + 512], ps[:, 4 + n % 2, :]).then_inc(x_hi, 1)

                evac_t(0)
                evac_t(1)
                act.wait_ge(r_sub, l + 1)
                act.activation(lg, lg, ACT.Exp).then_inc(r_exp, 1)
                for n in range(2, 10):
                    evac_t(n)
                for n in range(8):
                    act.wait_ge(t_ready, l * 19 + 10 + n + 1)
                    copy(PTs[:, n, :], ps[:, 4 + n % 2, :]).then_inc(t_evac, 1)
                act.wait_ge(t_ready, l * 19 + 19)
                copy(PTc, ps[:, 6, :].rearrange("p (g n) -> p g n", g=4)).then_inc(t_evac, 1)
                end_phase(act, l, 6)

                act.wait_ge(g_zero, l + 1)
                with act.Fori(0, NE // 4) as b:
                    for ee in range(4):
                        p0 = P_EXP + 6 * ee
                        for hf in range(2):
                            act.wait_ge(item_used, l * ITEMS + b * 24 + (p0 + 2 * hf + 1))
                            act.activation(sg[:, 256 * hf:256 * hf + 256], ps[0:SLOTS, 2 * hf, 0:256],
                                           ACT.Silu).then_inc(e_silu, 1)

                        def hidden_hi(hf):
                            act.wait_ge(e_t, l * 2 * NE + b * 8 + (2 * ee + hf + 1))
                            copy(hidT[0][:, ee % 2, 2 * hf:2 * hf + 2, :],
                                 ps[:, 4 + hf, 0:2 * SLOTS].rearrange("p (k n) -> p k n", k=2)).then_inc(e_hidT, 1)

                        def quarter_hi(v):
                            p, src = quarter_item(ee, v)
                            act.wait_ge(e_used, quarter(l, b, ee, v + 1))
                            if v in (0, 2):
                                act.wait_ge(landed[p % SLOT], l * (16 * LAPS) + b * 96 + 16 * (p // SLOT + 1))
                            copy(W4[:, v % 4, 0, :], src).then_inc(e_whi, 1)

                        hidden_hi(0)
                        for v in range(4):
                            quarter_hi(v)
                        quarter_hi(4)
                        hidden_hi(1)
                        quarter_hi(5)
                        quarter_hi(6)
                        quarter_hi(7)
                        act.wait_ge(e_used, quarter(l, b, ee, 12))
                        act.activation(yc[32 * ee:32 * ee + CAP[0], b, :],
                                       ps[CAP[1]:SLOTS, 6:8, :].rearrange("p a n -> p (a n)"), ACT.Copy,
                                       scale=gt[CAP[1]:SLOTS, bass.ds(b * 4 + ee, 1)]).then_inc(e_ycev, 1)
                end_phase(act, l, 7)
                for m in range(KC):
                    if m >= 2:
                        act.wait_ge(c_ready, l * 8 + m - 1)
                    copy(ysc_hi[:, m % 2], ysc[:, :, P * m:P * m + P]).then_inc(o_hi, 1)
                end_phase(act, l, 8)

        @block.vector
        def _(dve):
            settle = dve.drain

            def split(l, u):
                src = half_item(u)[1]
                dve.wait_ge(w_hi, l * UNITS + u + 1)
                dve.tensor_tensor(half_dst(u, 1), src, half_dst(u, 0).bitcast(F32), ALU.subtract).then_inc(w_lo, 1)

            def norm(l, n, root, dst):
                def lo(k):
                    dve.wait_ge(x_hi, l * OP_HI + k + 1)
                    for g, c0, c1 in GROUPS:
                        ins = dve.scalar_tensor_tensor(out=h_lo[:, k, c0:c1], in0=h_x[:, k, c0:c1],
                                                       scalar=mod[:, k, g:g + 1],
                                                       in1=h_hi[:, k, c0:c1].bitcast(F32),
                                                       op0=ALU.add, op1=ALU.subtract)
                    ins.then_inc(x_lo, 1)

                dve.wait_ge(s_rt, l * 2 + n + 1)
                dve.reciprocal(root, root)
                settle()
                for k in range(KC):
                    for g, c0, c1 in GROUPS:
                        ins = dve.scalar_tensor_tensor(out=dst[:, k, c0:c1], in0=X[:, k, c0:c1],
                                                       scalar=ws[:, n, k, g:g + 1], in1=root[:, c0:c1],
                                                       op0=ALU.mult, op1=ALU.mult)
                    ins.then_inc(s_xn, 1)
                    if n == 0 and k:
                        lo(k - 1)
                if n == 0:
                    lo(KC - 1)

            def residual(src, k, gate):
                for g, c0, c1 in GROUPS:
                    ins = dve.scalar_tensor_tensor(out=X[:, k, c0:c1], in0=src[:, c0:c1],
                                                   scalar=mod[:, gate + k, g:g + 1], in1=X[:, k, c0:c1],
                                                   op0=ALU.mult, op1=ALU.add)
                return ins

            dve.memset(cs[:], 0.0)
            dve.memset(eps[:], EPS)
            settle().then_inc(s_csz, 1)
            for _ in range(SLOT):
                settle().then_inc(modcol_read, 1)
            settle().then_inc(e_yev, 1)
            with dve.Fori(0, DEPTH) as l:
                dve.wait_ge(lay_net, l * 32 + 32)
                dve.wait_ge(lay, l * 80 + 80)
                dve.memset(fh2[FH:FH + 1, :], 1.0).then_inc(f_ones, 1)
                dve.tensor_scalar(win, dec, -1.0, None, ALU.mult)
                settle()
                dve.tensor_tensor(dec, dec, win, ALU.max).then_inc(f_dec, 1)
                def modulation(it):
                    for s in range(4):
                        dve.wait_ge(modcol_ready, l * N_MOD + 4 * it + s + 1)
                        n = 8 * it + 2 * s
                        dve.tensor_tensor(mod[:, n:n + 2, :],
                                          ps[:, 2 + s % 2, 0:4].rearrange("p (c g) -> p c g", c=2),
                                          vec[:, n:n + 2].unsqueeze(2).to_broadcast([P, 2, 2]),
                                          ALU.add).then_inc(modcol_read, 1)

                def argument(n):
                    dve.wait_ge(f_mm, l * 2 + n + 1)
                    dve.tensor_scalar(farg, tokh(2)[0:FH, :], fw[:, 2 * FH + n:2 * FH + n + 1], None, ALU.add)
                    settle()
                    dve.tensor_scalar(frnd, farg, float(1 / (2 * np.pi)), ROUND, ALU.mult, ALU.add)
                    settle()
                    dve.tensor_scalar(frnd, frnd, -ROUND, None, ALU.add)
                    for part in TWO_PI:
                        settle()
                        dve.scalar_tensor_tensor(out=farg, in0=frnd, scalar=-part, in1=farg, op0=ALU.mult,
                                                 op1=ALU.add)
                    settle()
                    dve.tensor_scalar(farg, farg, -PI_IN, PI_IN, ALU.max, ALU.min).then_inc(f_arg, 1)

                def taps(n):
                    t, o = n // 2, n % 2
                    settle()
                    dve.wait_ge(f_win, l * 5 + t + 1)
                    dve.wait_ge(f_taps, l * 10 + n + 1)
                    for d in range(2):
                        w0 = DH * (2 * d + o)
                        dve.scalar_tensor_tensor(out=fdir[:, d, :], in0=win[:, w0:w0 + DH], scalar=SHIFT,
                                                 in1=ps[:, 4 + 2 * (n % 2) + d, :], op0=ALU.add, op1=ALU.mult)
                    settle()
                    if t <= 1:
                        dve.memset(fdir[0:1, 1, :], 0.0)
                        settle()
                    dve.tensor_tensor(fa[:, t, o, :], fdir[:, 0, :], fdir[:, 1, :], ALU.add)
                    ins = dve.tensor_tensor(fb[:, t, o, :], fdir[:, 1, :], fdir[:, 0, :], ALU.subtract)
                    if t <= 1:
                        settle()
                        ins = dve.tensor_tensor(fa[0:1, t, o, :], fa[0:1, t, o, :], fbias[:, o, :], ALU.add)
                    ins.then_inc(f_tapsread, 1)

                argument(0)
                modulation(0)
                settle()
                argument(1)
                modulation(1)
                for t in range(NT):
                    taps(2 * t)
                    taps(2 * t + 1)
                    if t < 4:
                        modulation(2 + t)
                settle()
                for n in range(2):
                    dve.scalar_tensor_tensor(out=ws[:, n], in0=mod[:, 24 * n + 8:24 * n + 16, :], scalar=1.0,
                                             in1=vec[:, V_N1 + 8 * n:V_N1 + 8 * n + 8].unsqueeze(2)
                                             .to_broadcast([P, KC, 2]),
                                             op0=ALU.add, op1=ALU.mult)
                end_phase(dve, l, 0)

                dve.wait_ge(consts, N_CONSTS)
                for b in range(2):
                    for c0 in (0, LI + 1, T + 2):
                        ins = dve.memset(raw[:, b, c0:c0 + 1], 0.0)
                ins.then_inc(pads, 1)
                split(l, 0)
                split(l, 1)
                norm(l, 0, rstd, h_x)

                def conv(dst, src, w, bias):
                    dve.tensor_scalar(dst, src(1), vec[:, w + 1:w + 2], vec[:, bias:bias + 1], ALU.mult, ALU.add)
                    for tap in (0, 2):
                        settle()
                        ins = dve.scalar_tensor_tensor(out=dst, in0=src(tap), scalar=vec[:, w + tap:w + tap + 1],
                                                       in1=dst, op0=ALU.mult, op1=ALU.add)
                    return ins

                for c in range(24):
                    b = c % 2
                    settle()
                    split(l, c + 2)
                    if c < 12:
                        before = (c // 2) * 2 + c % 2
                        dve.wait_ge(act_freed, l * A_FREED + before + 1)
                        if 2 <= c < 8 or c in (8, 9):
                            dve.wait_ge(tr_ready, l * 8 + c - 1)
                        ins = conv(cv[:, b, :], lambda i: raw[:, b, i:i + T + 1], V_HYW + 3 * c, V_HYB + c)
                        if c < 8:
                            ins.then_inc(conv_done, 1)
                        else:
                            settle()
                            dve.tensor_copy(Y3[:, 0, c - 8, 0:LI], cv[:, b, 0:LI])
                            dve.tensor_copy(Y3[:, 0, c - 8, LI:T], cv[:, b, LI + 1:T + 1]).then_inc(conv_done, 1)
                        continue
                    if freed_by(c)[0] == "act":
                        continue
                    j = 2 * ((c - 12) // 6) + b
                    settle()
                    wait_chunk(dve, l, c)
                    pieces = ((0, LI, 0), (LI, T, 1))
                    if (c - 12) % 6 < 4:
                        dve.wait_ge(act_freed, l * A_FREED + freed_by(12 + 6 * ((c - 12) // 6) + b)[1])
                        for c0, c1, x in pieces:
                            ins = dve.tensor_tensor(raw[:, b, 1 + c0 + x:1 + c1 + x], tokh(c % 3)[:, c0:c1],
                                                    ubuf[:, b, c0:c1], ALU.mult)
                        ins.then_inc(dve_freed, 1)
                        settle()
                        conv(cv[:, b, :], lambda i: raw[:, b, i:i + T + 1], V_SCW + 3 * j, V_SCB + j)
                    else:
                        for c0, c1, x in pieces:
                            ins = dve.tensor_tensor(Y3[:, 2, j, c0:c1], tokh(c % 3)[:, c0:c1],
                                                    cv[:, b, c0 + x:c1 + x], ALU.mult)
                        ins.then_inc(dve_freed, 1)
                for u in range(26, 32):
                    split(l, u)
                dve.wait_ge(act_freed, l * A_FREED + A_FREED)
                for t in range(NT):
                    qk = qkv[:, t, 0:QK]
                    dve.tensor_tensor(prep[:, t % 2, :], qk, qk, ALU.mult)
                    settle()
                    ins = dve.tensor_reduce(st5[:, t, :], prep[:, t % 2, :].rearrange("p (h d) -> p h d", h=10), AX.X,
                                            ALU.add)
                ins.then_inc(qs_ready, 1)

                def weigh(t):
                    qk = qkv[:, t, 0:QK]
                    heads = qk.rearrange("p (h d) -> p h d", h=10)
                    dve.tensor_tensor(heads, heads, rst5[:, t, :].unsqueeze(2).to_broadcast([P, 10, HD]), ALU.mult)
                    settle()
                    return dve.tensor_tensor(qk, qk, qkw[:], ALU.mult)

                def rotate(t):
                    v4 = "p (h a f i) -> p h a f i"
                    src = qkv[:, t, 0:QK]
                    dve.tensor_tensor(prep[:, t % 2, :].rearrange("p (h d) -> p h d", h=10),
                                      src.rearrange("p (h d) -> p h d", h=10),
                                      rope[:, 0, t - 1, :].unsqueeze(1).to_broadcast([P, 10, HD]), ALU.mult)
                    for f in range(2):
                        sin = rope[:, 1, t - 1, :].rearrange("p (a f i) -> p a f i", a=2, f=2)[:, :, f, :]
                        for axis in range(2):
                            dve.tensor_tensor(prep2[:, t % 2, :].rearrange(v4, h=10, a=2, f=2)[:, :, axis, f, :],
                                              src.rearrange(v4, h=10, a=2, f=2)[:, :, axis, 1 - f, :],
                                              sin[:, axis, :].unsqueeze(1).to_broadcast([P, 10, 16]), ALU.mult)
                    settle()
                    return dve.tensor_tensor(src, prep[:, t % 2, :], prep2[:, t % 2, :], ALU.add)

                for u in range(32, UNITS1):
                    split(l, u)
                    if u == 32:
                        dve.wait_ge(qrt, l + 1)
                        dve.reciprocal(rst5[:], st5[:])
                        settle()
                        for t in range(3):
                            weigh(t)
                    elif u == 33:
                        for t in range(3, NT):
                            weigh(t)
                        settle()
                    elif u <= 37:
                        rotate(u - 33)
                        settle()
                    if u == 38:
                        settle().then_inc(prep_done, 1)
                end_phase(dve, l, 1)

                dve.wait_ge(a_trev, l * 6 + 6)
                apart(dve)
                def queries(j, g):
                    dve.tensor_copy(qj[HD * g:HD * g + HD, :], qT[HD * g:HD * g + HD, j, :]).then_inc(a_qj, 1)

                def row_max(j, u):
                    t = u % 5
                    n = P if t == 0 else T
                    dve.wait_ge(a_s, l * 40 + j * 10 + (u + 1))
                    src = ps[:, 2 * (u % 2):2 * (u % 2) + 2, :].rearrange("p a n -> p (a n)")[:, 0:n]
                    dve.tensor_reduce(nb[:, u % 2:u % 2 + 1], src, AX.X, ALU.max, negate=True).then_inc(a_max, 1)

                def scale_rows(j, u):
                    n = P if u % 5 == 0 else T
                    i = slice(u % 2, u % 2 + 1)
                    dve.wait_ge(a_exp, l * 40 + j * 10 + (u + 3))
                    dve.reciprocal(rinv[:, i], rsum[:, i])
                    settle()
                    dve.tensor_scalar(Pb[:, u % 2, 0:n], Pb[:, u % 2, 0:n], rinv[:, i], None,
                                      ALU.mult).then_inc(a_norm, 1)

                def heads(j, last):
                    for u in range(10):
                        if u + 1 < 10:
                            scale_rows(j, u + 1)
                        elif not last:
                            scale_rows(j + 1, 0)
                        if u + 2 < 10:
                            row_max(j, u + 2)
                        elif not last:
                            row_max(j + 1, u - 8)
                        if u % 5 == 3 and not last:
                            queries(j + 1, u // 5)

                queries(0, 0)
                queries(0, 1)
                row_max(0, 0)
                row_max(0, 1)
                scale_rows(0, 0)
                with dve.Fori(0, 3) as j:
                    heads(j, False)
                heads(3, True)
                end_phase(dve, l, 2)

                for o in range(2):
                    dve.wait_ge(k_loaded, l * 32 + 16 * o + 16)
                    apart(dve)
                    for kc in range(NT):
                        settle()
                        dve.wait_ge(y_fwd, l * 10 + 5 * o + kc + 1)
                        uc, us = ps[:, 2 * (kc % 4), :], ps[:, 2 * (kc % 4) + 1, :]
                        kr, ki = Kb[:, kc, 0, :], Kb[:, kc, 1, :]
                        for i, (x, y) in enumerate(((uc, kr), (us, ki), (us, kr), (uc, ki))):
                            dve.tensor_tensor(ytmp[:, i, :], x, y, ALU.mult)
                        settle()
                        dve.tensor_tensor(Yb[:, kc, 0, :], ytmp[:, 0, :], ytmp[:, 1, :], ALU.add)
                        dve.tensor_tensor(Yb[:, kc, 1, :], ytmp[:, 2, :], ytmp[:, 3, :],
                                          ALU.subtract).then_inc(y_mul, 1)
                    for m in range(NT - o):
                        dve.wait_ge(y_inv, l * 9 + 5 * o + m + 1)
                        if o == 0:
                            ins = dve.tensor_tensor(u_tm[:, m, :], ps[:, 2 * (m % 2), :], x1_tm[:, m, :], ALU.mult)
                        else:
                            ins = dve.tensor_tensor(Y3[:, 0, m, :], tok(m % 2), Y3[:, 0, m, :], ALU.mult)
                        ins.then_inc(y_out, 1)
                end_phase(dve, l, 3)

                def branch_lo(br):
                    for k in range(4):
                        dve.wait_ge(x_hi, l * OP_HI + OP_Y + 4 * br + k + 1)
                        dve.tensor_tensor(Y_lo[:, br, k, :], Y3[:, br, k, :], Y_hi[:, br, k, :].bitcast(F32),
                                          ALU.subtract).then_inc(x_lo, 1)

                def merged_lo(c):
                    dve.wait_ge(x_hi, l * OP_HI + OP_M + c + 1)
                    dve.tensor_tensor(m_lo[:, c, :], merged[:, c, :], m_hi[c // 4][:, c % 4, :].bitcast(F32),
                                      ALU.subtract).then_inc(x_lo, 1)

                for u in range(2):
                    split(l, UNITS1 + u)
                    branch_lo(u)
                for n in range(24):
                    half, br, m = n // 12, n % 12 // 4, n % 4
                    c = 4 * half + m
                    dve.wait_ge(sg_in[n % 4], l * 96 + 16 * (n // 4) + 16)
                    dve.wait_ge(mg_ready, l * MG + n + 1)
                    dst = mtmp[:, n % 2, :] if br else merged[:, c, :]
                    ins = dve.tensor_tensor(dst, tokh(n % 4), sgin[:, n % 4, :], ALU.mult)
                    if br:
                        settle()
                        ins = dve.tensor_tensor(merged[:, c, :], merged[:, c, :], dst, ALU.add)
                    ins.then_inc(mg_read, 1)
                    if n == 0:
                        branch_lo(2)
                    if n % 2:
                        split(l, UNITS1 + 2 + n // 2)
                    if 16 <= n < 20:
                        merged_lo(n - 16)
                    settle()
                for c in range(4, KC):
                    merged_lo(c)
                for c in range(KC):
                    settle()
                    dve.wait_ge(mg_ready, l * MG + 24 + c + 1)
                    residual(tokh(c % 4), c, 16).then_inc(mg_read, 1)
                    if c + 2 < KC:
                        split(l, UNITS1 + 2 * N_BR + 2 + c)
                end_phase(dve, l, 4)
                norm(l, 1, rstd2, h)
                end_phase(dve, l, 5)

                dve.wait_ge(r_lg, l + 1)
                logits = ps[:, 0, 0:NT * NE].rearrange("p (t e) -> p t e", t=NT)
                dve.tensor_reduce(r1[:, :, 0:1], logits, AX.X, ALU.max)
                settle()
                dve.tensor_tensor(lg, logits, r1[:, :, 0:1].to_broadcast([P, NT, NE]), ALU.subtract)\
                    .then_inc(r_sub, 1)

                def token_lo(n):
                    dve.wait_ge(x_hi, l * OP_HI + OP_T + n + 1)
                    cols = slice(512 * (n % 2), 512 * (n % 2) + 512)
                    dve.tensor_tensor(h2_lo[:, n // 2, cols], ps[:, 4 + n % 2, :], h2_hi[:, n // 2, cols].bitcast(F32),
                                      ALU.subtract).then_inc(t_evac, 1)

                token_lo(0)
                token_lo(1)
                dve.wait_ge(r_exp, l + 1)
                dve.tensor_reduce(r1[:, :, 0:1], lg, AX.X, ALU.add)
                settle()
                dve.reciprocal(r1[:, :, 1:2], r1[:, :, 0:1])
                settle()
                dve.tensor_tensor(aff, lg, r1[:, :, 1:2].to_broadcast([P, NT, NE]), ALU.mult).then_inc(r_aff, 1)
                dve.wait_ge(r_affT, l + 1)
                dve.tensor_copy(work, tok(1)[0:NE, :])
                for g, c0, c1 in GROUPS:
                    for i in range(CAP[g] // 8):
                        if g:
                            token_lo(2 + i)
                        settle()
                        dve.max(m8[:], work[:, c0:c1])
                        settle()
                        dve.match_replace(work[:, c0:c1], m8[:], work[:, c0:c1], -1.0)
                settle()
                dve.tensor_scalar(mask, work, 0.0, None, ALU.is_lt).then_inc(r_mask, 1)
                dve.wait_ge(r_maskT, l + 1)
                dve.tensor_copy(maskT, ps[:, 0, 0:NT * NE].rearrange("p (t e) -> p t e", t=NT)).then_inc(r_mt, 1)
                settle()
                dve.wait_ge(r_pos, l + 1)
                dve.scalar_tensor_tensor(out=q1, in0=ps[:, 1, 0:NT * NE].rearrange("p (t e) -> p t e", t=NT),
                                         scalar=1.0, in1=maskT, op0=ALU.add, op1=ALU.mult)
                settle()
                for t in range(NT):
                    n = HD if t else 32
                    dst = Ps[:, t - 1, :].rearrange("p (e s) -> p e s", e=NE) if t else Pi
                    ins = dve.tensor_tensor(dst, iota[:, 0:n].unsqueeze(1).to_broadcast([P, NE, n]),
                                            q1[:, t, :].unsqueeze(2).to_broadcast([P, NE, n]), ALU.is_equal)
                ins.then_inc(r_P, 1)
                for n in range(3 * KC):
                    k, part = n // 3, n % 3
                    dve.wait_ge(g_ready, l * 25 + n + 1)
                    if part < 2:
                        ins = dve.tensor_copy(xs[:, k, 8 * part:8 * part + 8, 0:CAP[1]],
                                              ps[:, n % 4, :].rearrange("p (e s) -> p e s", e=8))
                    else:
                        ins = dve.tensor_copy(xs[:, k, :, CAP[1]:SLOTS],
                                              ps[:, n % 4, 0:256].rearrange("p (e s) -> p e s", e=NE))
                    ins.then_inc(g_evac, 1)
                dve.wait_ge(g_ready, l * 25 + 25)
                dve.tensor_copy(gt[0:SLOTS, :], ps[0:SLOTS, 0, 0:NE]).then_inc(g_evac, 1)
                end_phase(dve, l, 6)

                with dve.Fori(0, NE // 4) as b:
                    for ee in range(4):
                        p0 = P_EXP + 6 * ee
                        def hidden(hf):
                            dve.wait_ge(e_silu, l * 2 * NE + b * 8 + (2 * ee + hf + 1))
                            dve.wait_ge(item_used, l * ITEMS + b * 24 + (p0 + 2 * hf + 2))
                            cols = slice(256 * hf, 256 * hf + 256)
                            dve.tensor_tensor(hid[:, cols], ps[0:SLOTS, 2 * hf + 1, 0:256], sg[:, cols],
                                              ALU.mult).then_inc(e_hid, 1)

                        def hidden_lo(hf):
                            dve.wait_ge(e_hidT, l * 2 * NE + b * 8 + (2 * ee + hf + 1))
                            rows = slice(2 * hf, 2 * hf + 2)
                            dve.tensor_tensor(hidT[1][:, ee % 2, rows, :],
                                              ps[:, 4 + hf, 0:2 * SLOTS].rearrange("p (k n) -> p k n", k=2),
                                              hidT[0][:, ee % 2, rows, :].bitcast(F32), ALU.subtract).then_inc(e_hlo, 1)

                        def quarter_lo(v):
                            dve.wait_ge(e_whi, quarter(l, b, ee, v + 1))
                            dve.tensor_tensor(W4[:, v % 4, 1, :], quarter_item(ee, v)[1],
                                              W4[:, v % 4, 0, :].bitcast(F32), ALU.subtract).then_inc(e_wlo, 1)

                        hidden(0)
                        hidden_lo(0)
                        for v in range(4):
                            quarter_lo(v)
                        hidden(1)
                        quarter_lo(4)
                        hidden_lo(1)
                        quarter_lo(5)
                        quarter_lo(6)
                        quarter_lo(7)
                        dve.wait_ge(e_used, quarter(l, b, ee, 12))
                        r0 = HD * (ee % 2)
                        dve.tensor_scalar(ys[r0:r0 + HD, b * 2 + ee // 2, :],
                                          ps[0:CAP[1], 6:8, :].rearrange("p a n -> p (a n)"),
                                          gt[0:CAP[1], bass.ds(b * 4 + ee, 1)], None, ALU.mult).then_inc(e_yev, 1)
                end_phase(dve, l, 7)

                def outputs_lo(m):
                    cols = slice(P * m, P * m + P)
                    dve.wait_ge(o_hi, l * 8 + m + 1)
                    dve.tensor_tensor(ysc_lo[:, :, cols], ysc[:, :, cols], ysc_hi[:, m % 2].bitcast(F32),
                                      ALU.subtract).then_inc(o_lo, 1)

                outputs_lo(0)
                outputs_lo(1)
                for m in range(KC):
                    dve.wait_ge(c_ready, l * 8 + m + 1)
                    if m + 2 < KC:
                        outputs_lo(m + 2)
                    residual(tok(m % 4), m, 40).then_inc(c_read, 1)
                end_phase(dve, l, 8)


CONSTS = ("ident", "onesm", "ones1", "utri", "sel", "zfeat", "tneg", "rope", "iota", "csi", "cfi", "cs")


def constants():
    f = np.float32
    out = {"ident": np.eye(P), "onesm": np.full((P, P), 1 / D), "ones1": np.ones((P, P)),
           "utri": np.triu(np.ones((P, P)), 1), "iota": np.tile(np.arange(1, HD + 1), (P, 1))}
    sel = np.zeros((P, 2))
    for g in range(2):
        sel[g::32, g] = 1
    out["sel"] = sel
    z, tn = np.zeros((POS, T)), np.zeros((P, NT))
    for (g, c0, c1), L in zip(GROUPS, (LI, LS)):
        n = np.arange(L)
        bands = np.linspace(1e-4, 15, 16)
        ang = 2 * np.pi * n[:, None] * bands[None] / L
        z[:, c0:c1] = np.concatenate([(n / (L - 1))[:, None], np.cos(ang), np.sin(ang)], 1).T
        for t in range(c0 // P, c1 // P):
            tn[:, t] = -(np.arange(P) + P * t - c0) / (L - 1)
    out["zfeat"], out["tneg"] = z, tn
    n = np.arange(LS)
    inv = 10000.0 ** (-np.arange(0, 32, 2) / 32)
    ar, ac = (n // 64)[:, None] * inv, (n % 64)[:, None] * inv
    cosv = np.concatenate([np.cos(ar), np.cos(ar), np.cos(ac), np.cos(ac)], 1)
    sinv = np.concatenate([-np.sin(ar), np.sin(ar), -np.sin(ac), np.sin(ac)], 1)
    out["rope"] = np.stack([x.reshape(4, P, HD).transpose(1, 0, 2) for x in (cosv, sinv)], 1)

    def tables(L):
        k = np.arange(L) + 0.5
        th, ph = np.pi * np.outer(k, k) / L, np.pi * np.outer(np.arange(L), k) / L
        return np.stack([np.cos(th), np.sin(th)]), np.stack([np.cos(ph), np.sin(ph)]) / L

    (ci, fi), (cl, fl) = tables(LI), tables(LS)
    out["csi"], out["cfi"] = ci.transpose(1, 0, 2), fi.transpose(1, 0, 2)
    out["cs"] = cl.reshape(2, 4, P, LS).transpose(2, 0, 1, 3)
    out["cf"] = fl.reshape(2, 4, P, LS).transpose(0, 2, 1, 3).reshape(2, P, ITEM)
    return {k: np.ascontiguousarray(v, dtype=f) for k, v in out.items()}


def weight_stream(w, cf):
    out = np.zeros((DEPTH, ITEMS, P, ITEM), np.float32)

    def columns(dst, m, width, kc):
        for i in range(m.shape[1] // width):
            dst[i] = m[:, i * width:(i + 1) * width].reshape(kc, P, width).transpose(1, 0, 2).reshape(P, -1)

    heads = np.concatenate([np.concatenate([np.arange(HD) + HD * j, np.arange(HD) + HD * (4 + j)])
                            for j in range(4)])
    for l in range(DEPTH):
        o = out[l]
        o[0, 0:FH] = w["hy_w3"][l]
        o[0, FH] = w["hy_b3"][l]
        columns(o[P_MOD:], w["mod_w"][l], 256, KC)
        o[P_DFT:P_DFT + 2] = cf
        win = w["w_in"][l]
        columns(o[P_HY:], win[:, 0:1536], 256, KC)
        base = 1536 + QKV
        for jp in range(2):
            for n, part in enumerate((0, 2, 1)):
                c = base + 512 * part + 256 * jp
                columns(o[P_SC + 3 * jp + n:], win[:, c:c + 256], 256, KC)
        columns(o[P_QKV:], win[:, 1536:base][:, np.concatenate([heads, np.arange(NQ * HD, QKV)])], 256, KC)
        columns(o[P_GATE:], win[:, base + 1536:], 256, KC)
        for n, (name, rows) in enumerate((("w_br_a", slice(None)), ("w_br_b", heads), ("w_br_c", slice(None)))):
            for half in range(2):
                columns(o[P_BR + 3 * half + n:], w[name][l][rows][:, 512 * half:512 * half + 512], 512, 4)
        columns(o[P_WO:], w["w_o"][l], 256, KC)
        for e in range(NE):
            p = P_EXP + 6 * e
            for hf in range(2):
                columns(o[p + 2 * hf:], w["exp_w_gate"][l, e][:, 256 * hf:256 * hf + 256], 256, KC)
                columns(o[p + 2 * hf + 1:], w["exp_w_up"][l, e][:, 256 * hf:256 * hf + 256], 256, KC)
            columns(o[p + 4:], w["exp_w_down"][l, e], 512, 4)
    return out.reshape(DEPTH * ITEMS, P, ITEM)


def kernel(**inputs):
    import concourse.bacc as bacc
    from concourse.bass_utils import run_bass_kernel_spmd

    w = {k: np.asarray(v) for k, v in inputs.items()}
    f = constants()
    arrays = {"stream": weight_stream(w, f.pop("cf")), **f}

    def feature_major(x):
        return np.swapaxes(x.reshape(*x.shape[:-1], -1, P), -1, -2)

    tokens = np.concatenate([w["x_prompt"][0], w["x_sample"][0]], 0)
    arrays["x"] = tokens.T.reshape(KC, P, T).transpose(1, 0, 2)
    arrays["cond"] = feature_major(np.stack([w["c_ctx"], w["c"][0]])).transpose(1, 2, 0)

    def taps(x):
        return feature_major(x).transpose(0, 2, 3, 1).reshape(DEPTH, P, -1)

    arrays["vec"] = np.concatenate(
        [feature_major(w["mod_b"]), feature_major(w["norm1_w"]), feature_major(w["norm2_w"]),
         taps(w["hy_short_w"]), feature_major(w["hy_short_b"]), taps(w["sc_w"]), feature_major(w["sc_b"])], 2)
    fw = np.zeros((DEPTH, FH, 2 * FH + 2), np.float32)
    fw[:, 0:POS, 0:FH] = w["hy_w1"]
    fw[:, :, FH:2 * FH] = w["hy_w2"]
    fw[:, :, 2 * FH] = w["hy_b1"]
    fw[:, :, 2 * FH + 1] = w["hy_b2"]
    arrays["fw"] = fw
    arrays["decay"] = np.broadcast_to(w["hy_decay"][:, None], (DEPTH, P, 2048))
    arrays["fbias"] = w["hy_bias"].reshape(DEPTH, 1, 2, DH)
    arrays["router"] = w["router_w"].reshape(DEPTH, KC, P, NE).transpose(0, 2, 1, 3)
    qkw = np.concatenate([np.tile(w["q_norm_w"], (1, NQ)), np.tile(w["k_norm_w"], (1, NKV))], 1)
    arrays["qkw"] = np.broadcast_to(qkw[:, None], (DEPTH, P, QK))
    arrays["ctx_k"] = w["cache_k"][0].reshape(DEPTH, PAST, P).transpose(0, 2, 1)
    arrays["ctx_v"] = w["cache_v"][0].reshape(DEPTH, PAST, P)
    arrays = {k: np.ascontiguousarray(v) for k, v in arrays.items()}

    nc = bacc.Bacc("TRN2", target_bir_lowering=False, num_devices=1)
    args = {k: nc.dram_tensor(f"in_{k}", v.shape, F32, kind="ExternalInput").ap() for k, v in arrays.items()}
    args["kspec"] = nc.dram_tensor("kspec", [2, NT, 2, P, DH], F32, kind="Internal").ap()
    args["gates"] = nc.dram_tensor("gates", [24, P, T], F32, kind="Internal").ap()
    for name, shape in (("y", [P, KC, T]), ("new_k", [DEPTH, SEQ_C, P]), ("new_v", [DEPTH, SEQ_C, P])):
        args[name] = nc.dram_tensor(f"out_{name}", shape, F32, kind="ExternalOutput").ap()
    build(nc, args)
    r = run_bass_kernel_spmd(nc, [{f"in_{k}": v for k, v in arrays.items()}], core_ids=[0]).results[0]
    y = r["out_y"].transpose(1, 0, 2).reshape(D, T).T
    caches = [r[f"out_{n}"].reshape(1, DEPTH, SEQ_C, NKV, HD) for n in ("new_k", "new_v")]
    return (np.ascontiguousarray(y[None, 0:LI]), np.ascontiguousarray(y[None, LI:T]), *caches)
```
